# Optimizing a Trainium2 kernel written in Bass

```python
import jax, jax.numpy as jnp
from jax import lax
import numpy as np

D_MODEL = 2048
BATCH = 1
SEQ = 256
DEPTH = 1
DEC_BATCH = 8
DEC_SEQ = 1
PAST_LEN = 2048
PAGE_SIZE = 128

N_META = 16
GLA_HEADS = 4
GLA_DK = 128
GLA_DV = 256
GLA_RANK = 16
GLA_TAU = 16.0
GLA_CHUNK = 64
SWA_HEADS = 16
SWA_KV_HEADS = 4
SWA_GROUP = SWA_HEADS // SWA_KV_HEADS
SWA_HD = 64
WINDOW = 128
D_FF = 5632
EPS = 1e-6

GLA_QK = GLA_HEADS * GLA_DK
GLA_V = GLA_HEADS * GLA_DV
SWA_Q = SWA_HEADS * SWA_HD
SWA_KV = SWA_KV_HEADS * SWA_HD
SPLITS = (GLA_QK, GLA_QK, GLA_V, GLA_V, GLA_RANK, SWA_Q, SWA_KV, SWA_KV, D_MODEL, D_MODEL)
IN_PROJ = 2 * GLA_QK + 2 * GLA_V + GLA_RANK + SWA_Q + 2 * SWA_KV + 2 * D_MODEL

kernel_name = "hybrid_gla_swa_macaron_meta_step"

F32 = jnp.float32

def rmsnorm(x, g):
    xf = x.astype(F32)
    y = xf * lax.rsqrt(jnp.mean(xf * xf, axis=-1, keepdims=True) + EPS)
    return (y * g.astype(F32)).astype(x.dtype)

def half_ffn(h, g, w_in, w_out):
    u = rmsnorm(h, g) @ w_in
    a, b = jnp.split(u, 2, axis=-1)
    return h + 0.5 * ((jax.nn.silu(a) * b) @ w_out)

def in_projection(h, g, w_in):
    u = rmsnorm(h, g) @ w_in
    parts = []
    off = 0
    for n in SPLITS:
        parts.append(u[..., off:off + n])
        off += n
    return parts

def alibi_slopes():
    h = jnp.arange(1, SWA_HEADS + 1, dtype=F32)
    return jnp.exp2(-8.0 * h / SWA_HEADS).reshape(SWA_KV_HEADS, SWA_GROUP)

def sink_softmax(s, sinks):
    sk = sinks.astype(F32).reshape(SWA_KV_HEADS, SWA_GROUP, 1)
    m = jnp.maximum(jnp.max(s, axis=-1), sk)
    p = jnp.exp(s - m[..., None])
    return p / (jnp.sum(p, axis=-1, keepdims=True) + jnp.exp(sk - m)[..., None])

def gla_inputs(gq, gk, gv, gad, a_up, a_bias):
    lead = gq.shape[:-1]
    q = gq.astype(F32).reshape(*lead, GLA_HEADS, GLA_DK) * (GLA_DK ** -0.5)
    k = gk.astype(F32).reshape(*lead, GLA_HEADS, GLA_DK)
    v = gv.astype(F32).reshape(*lead, GLA_HEADS, GLA_DV)
    logg = jax.nn.log_sigmoid((gad @ a_up + a_bias).astype(F32)) / GLA_TAU
    return q, k, v, logg.reshape(*lead, GLA_HEADS, GLA_DK)

def gla_scan(q, k, v, logg, s0, chunk):
    B, L, H, _ = q.shape
    n = L // chunk

    def to_chunks(t):
        return jnp.moveaxis(t.reshape(B, n, chunk, H, t.shape[-1]), 1, 0)

    causal = jnp.tril(jnp.ones((chunk, chunk), dtype=bool))[None, :, :, None, None]

    def step(S, xs):
        qc, kc, vc, gc = xs
        b = jnp.cumsum(gc, axis=1)
        diff = b[:, :, None] - b[:, None, :]
        decay = jnp.exp(jnp.where(causal, diff, -jnp.inf))
        att = jnp.einsum('bthd,bshd,btshd->bhts', qc, kc, decay)
        o = (jnp.einsum('bhts,bshv->bthv', att, vc)
             + jnp.einsum('bthd,bhdv->bthv', qc * jnp.exp(b), S))
        b_last = b[:, -1]
        S = (S * jnp.exp(b_last)[..., None]
             + jnp.einsum('bshd,bshv->bhdv', kc * jnp.exp(b_last[:, None] - b), vc))
        return S, o

    S, o = lax.scan(step, s0, (to_chunks(q), to_chunks(k), to_chunks(v), to_chunks(logg)))
    o = jnp.moveaxis(o, 0, 1).reshape(B, L, H, GLA_DV)
    return o, S

def gla_branch_out(o, r, onorm, w_o):
    of = o * lax.rsqrt(jnp.mean(o * o, axis=-1, keepdims=True) + EPS)
    of = of * onorm.astype(F32).reshape(GLA_HEADS, GLA_DV)
    of = of.reshape(*o.shape[:-2], GLA_V) * jax.nn.silu(r.astype(F32))
    return of.astype(r.dtype) @ w_o

def swa_prompt(q, k, v, sinks):
    B, LT, _ = q.shape
    S = LT - N_META
    nb = S // WINDOW
    q = q.astype(F32).reshape(B, LT, SWA_KV_HEADS, SWA_GROUP, SWA_HD) * (SWA_HD ** -0.5)
    k = k.astype(F32).reshape(B, LT, SWA_KV_HEADS, SWA_HD)
    v = v.astype(F32).reshape(B, LT, SWA_KV_HEADS, SWA_HD)
    qm, qr = q[:, :N_META], q[:, N_META:]
    km, kr = k[:, :N_META], k[:, N_META:]
    vm, vr = v[:, :N_META], v[:, N_META:]
    causal_m = jnp.tril(jnp.ones((N_META, N_META), dtype=bool))
    s_mm = jnp.where(causal_m, jnp.einsum('bqkgd,bskd->bkgqs', qm, km), -jnp.inf)
    o_m = jnp.einsum('bkgqs,bskd->bqkgd', sink_softmax(s_mm, sinks), vm)
    qb = qr.reshape(B, nb, WINDOW, SWA_KV_HEADS, SWA_GROUP, SWA_HD)
    kb = kr.reshape(B, nb, WINDOW, SWA_KV_HEADS, SWA_HD)
    vb = vr.reshape(B, nb, WINDOW, SWA_KV_HEADS, SWA_HD)
    pad = ((0, 0), (1, 0), (0, 0), (0, 0), (0, 0))
    kw = jnp.concatenate([jnp.pad(kb, pad)[:, :-1], kb], axis=2)
    vw = jnp.concatenate([jnp.pad(vb, pad)[:, :-1], vb], axis=2)
    i = jnp.arange(WINDOW)[:, None]
    j = jnp.arange(2 * WINDOW)[None, :]
    dist = i + WINDOW - j
    blk = jnp.arange(nb)[:, None, None]
    valid = (dist >= 0) & (dist < WINDOW) & (blk * WINDOW + j[None] - WINDOW >= 0)
    slopes = alibi_slopes()[:, :, None, None]
    s_win = jnp.einsum('bnqkgd,bnskd->bnkgqs', qb, kw) - slopes * dist.astype(F32)
    s_win = jnp.where(valid[None, :, None, None], s_win, -jnp.inf)
    s_meta = jnp.einsum('bnqkgd,bskd->bnkgqs', qb, km)
    p = sink_softmax(jnp.concatenate([s_meta, s_win], axis=-1), sinks)
    o_r = (jnp.einsum('bnkgqs,bskd->bnqkgd', p[..., :N_META], vm)
           + jnp.einsum('bnkgqs,bnskd->bnqkgd', p[..., N_META:], vw))
    return jnp.concatenate([o_m.reshape(B, N_META, SWA_Q), o_r.reshape(B, S, SWA_Q)], axis=1)

def swa_sample(q, k, v, meta_k, meta_v, win_k, win_v, sinks):
    DB, T, _ = q.shape
    WB = win_k.shape[1]
    q = q.astype(F32).reshape(DB, T, SWA_KV_HEADS, SWA_GROUP, SWA_HD) * (SWA_HD ** -0.5)
    kw = jnp.concatenate([win_k.astype(F32), k.astype(F32).reshape(DB, T, SWA_KV_HEADS, SWA_HD)], axis=1)
    vw = jnp.concatenate([win_v.astype(F32), v.astype(F32).reshape(DB, T, SWA_KV_HEADS, SWA_HD)], axis=1)
    i = jnp.arange(T)[:, None]
    c = jnp.arange(WB + T)[None, :]
    dist = i + WB - c
    valid = (dist >= 0) & (dist < WINDOW) & (PAST_LEN - WB + c >= N_META)
    slopes = alibi_slopes()[:, :, None, None]
    s_win = jnp.einsum('bqkgd,bskd->bkgqs', q, kw) - slopes * dist.astype(F32)
    s_win = jnp.where(valid, s_win, -jnp.inf)
    mk = meta_k.astype(F32)
    mv = meta_v.astype(F32)
    s_meta = jnp.einsum('bqkgd,bskd->bkgqs', q, mk)
    p = sink_softmax(jnp.concatenate([s_meta, s_win], axis=-1), sinks)
    o = (jnp.einsum('bkgqs,bskd->bqkgd', p[..., :N_META], mv)
         + jnp.einsum('bkgqs,bskd->bqkgd', p[..., N_META:], vw))
    new_k = kw[:, -WB:].astype(win_k.dtype)
    new_v = vw[:, -WB:].astype(win_v.dtype)
    return o.reshape(DB, T, SWA_Q), new_k, new_v

def merge(gla_b, swa_b, ga, gb, gate_bias, w_out):
    m = (jax.nn.sigmoid(ga + gate_bias[:D_MODEL]) * gla_b
         + jax.nn.sigmoid(gb + gate_bias[D_MODEL:]) * swa_b)
    return m @ w_out

def setup_inputs(seed: int = 0) -> dict:
    key = jax.random.key(seed)
    ks = jax.random.split(key, 32)
    WB = min(WINDOW, PAST_LEN)

    def nrm(k, shape, scale):
        return jax.random.normal(k, shape, F32) * scale

    def gain(k, shape):
        return 1.0 + 0.02 * jax.random.normal(k, shape, F32)

    return {
        "x_prompt": nrm(ks[0], (BATCH, SEQ, D_MODEL), 1.0),
        "x_sample": nrm(ks[1], (DEC_BATCH, DEC_SEQ, D_MODEL), 1.0),
        "cache_meta_k": nrm(ks[2], (DEPTH, DEC_BATCH, N_META, SWA_KV_HEADS, SWA_HD), 1.0),
        "cache_meta_v": nrm(ks[3], (DEPTH, DEC_BATCH, N_META, SWA_KV_HEADS, SWA_HD), 1.0),
        "cache_win_k": nrm(ks[4], (DEPTH, DEC_BATCH, WB, SWA_KV_HEADS, SWA_HD), 1.0),
        "cache_win_v": nrm(ks[5], (DEPTH, DEC_BATCH, WB, SWA_KV_HEADS, SWA_HD), 1.0),
        "state_gla": nrm(ks[6], (DEPTH, DEC_BATCH, GLA_HEADS, GLA_DK, GLA_DV), 1.0),
        "meta_tokens": nrm(ks[7], (N_META, D_MODEL), 1.0),
        "ffn1_norm": gain(ks[8], (DEPTH, D_MODEL)),
        "ffn1_w_in": nrm(ks[9], (DEPTH, D_MODEL, 2 * D_FF), D_MODEL ** -0.5),
        "ffn1_w_out": nrm(ks[10], (DEPTH, D_FF, D_MODEL), D_FF ** -0.5),
        "mix_norm": gain(ks[11], (DEPTH, D_MODEL)),
        "w_in": nrm(ks[12], (DEPTH, D_MODEL, IN_PROJ), D_MODEL ** -0.5),
        "gla_a_up": nrm(ks[13], (DEPTH, GLA_RANK, GLA_QK), GLA_RANK ** -0.5),
        "gla_a_bias": nrm(ks[14], (DEPTH, GLA_QK), 0.1),
        "gla_out_norm": gain(ks[15], (DEPTH, GLA_V)),
        "w_gla_o": nrm(ks[16], (DEPTH, GLA_V, D_MODEL), GLA_V ** -0.5),
        "swa_sinks": nrm(ks[17], (DEPTH, SWA_HEADS), 0.5),
        "w_swa_o": nrm(ks[18], (DEPTH, SWA_Q, D_MODEL), SWA_Q ** -0.5),
        "gate_bias": nrm(ks[19], (DEPTH, 2 * D_MODEL), 0.1),
        "w_out": nrm(ks[20], (DEPTH, D_MODEL, D_MODEL), D_MODEL ** -0.5),
        "ffn2_norm": gain(ks[21], (DEPTH, D_MODEL)),
        "ffn2_w_in": nrm(ks[22], (DEPTH, D_MODEL, 2 * D_FF), D_MODEL ** -0.5),
        "ffn2_w_out": nrm(ks[23], (DEPTH, D_FF, D_MODEL), D_FF ** -0.5),
        "final_norm": gain(ks[24], (D_MODEL,)),
    }

def reference(x_prompt, x_sample, cache_meta_k, cache_meta_v, cache_win_k, cache_win_v, state_gla,
              meta_tokens, ffn1_norm, ffn1_w_in, ffn1_w_out, mix_norm, w_in, gla_a_up, gla_a_bias,
              gla_out_norm, w_gla_o, swa_sinks, w_swa_o, gate_bias, w_out, ffn2_norm, ffn2_w_in,
              ffn2_w_out, final_norm):
    B = x_prompt.shape[0]
    DB = x_sample.shape[0]
    meta = jnp.broadcast_to(meta_tokens.astype(x_prompt.dtype)[None], (B, N_META, D_MODEL))
    hp = jnp.concatenate([meta, x_prompt], axis=1)
    hs = x_sample
    p_meta_k, p_meta_v, p_win_k, p_win_v, p_gla = [], [], [], [], []
    s_win_k, s_win_v, s_gla = [], [], []
    for l in range(DEPTH):
        hp = half_ffn(hp, ffn1_norm[l], ffn1_w_in[l], ffn1_w_out[l])
        hs = half_ffn(hs, ffn1_norm[l], ffn1_w_in[l], ffn1_w_out[l])

        gq, gk, gv, gr, gad, sq, sk, sv, ga, gb = in_projection(hp, mix_norm[l], w_in[l])
        q, k, v, logg = gla_inputs(gq, gk, gv, gad, gla_a_up[l], gla_a_bias[l])
        s0 = jnp.zeros((B, GLA_HEADS, GLA_DK, GLA_DV), F32)
        o_meta, st_meta = gla_scan(q[:, :N_META], k[:, :N_META], v[:, :N_META], logg[:, :N_META], s0, N_META)
        o_real, st_fin = gla_scan(q[:, N_META:], k[:, N_META:], v[:, N_META:], logg[:, N_META:], st_meta, GLA_CHUNK)
        gla_b = gla_branch_out(jnp.concatenate([o_meta, o_real], axis=1), gr, gla_out_norm[l], w_gla_o[l])
        swa_b = swa_prompt(sq, sk, sv, swa_sinks[l]).astype(hp.dtype) @ w_swa_o[l]
        hp = hp + merge(gla_b, swa_b, ga, gb, gate_bias[l], w_out[l])
        p_meta_k.append(sk[:, :N_META].reshape(B, N_META, SWA_KV_HEADS, SWA_HD))
        p_meta_v.append(sv[:, :N_META].reshape(B, N_META, SWA_KV_HEADS, SWA_HD))
        p_win_k.append(sk[:, -WINDOW:].reshape(B, WINDOW, SWA_KV_HEADS, SWA_HD))
        p_win_v.append(sv[:, -WINDOW:].reshape(B, WINDOW, SWA_KV_HEADS, SWA_HD))
        p_gla.append(st_fin.astype(hp.dtype))

        gq, gk, gv, gr, gad, sq, sk, sv, ga, gb = in_projection(hs, mix_norm[l], w_in[l])
        q, k, v, logg = gla_inputs(gq, gk, gv, gad, gla_a_up[l], gla_a_bias[l])
        o_s, st_s = gla_scan(q, k, v, logg, state_gla[l].astype(F32), q.shape[1])
        gla_b = gla_branch_out(o_s, gr, gla_out_norm[l], w_gla_o[l])
        o_w, nwk, nwv = swa_sample(sq, sk, sv, cache_meta_k[l], cache_meta_v[l],
                                   cache_win_k[l], cache_win_v[l], swa_sinks[l])
        swa_b = o_w.astype(hs.dtype) @ w_swa_o[l]
        hs = hs + merge(gla_b, swa_b, ga, gb, gate_bias[l], w_out[l])
        s_win_k.append(nwk)
        s_win_v.append(nwv)
        s_gla.append(st_s.astype(state_gla.dtype))

        hp = half_ffn(hp, ffn2_norm[l], ffn2_w_in[l], ffn2_w_out[l])
        hs = half_ffn(hs, ffn2_norm[l], ffn2_w_in[l], ffn2_w_out[l])

    y_prompt = rmsnorm(hp[:, N_META:], final_norm)
    y_sample = rmsnorm(hs, final_norm)
    return (y_prompt, y_sample,
            jnp.stack(p_meta_k), jnp.stack(p_meta_v), jnp.stack(p_win_k), jnp.stack(p_win_v), jnp.stack(p_gla),
            jnp.stack(s_win_k), jnp.stack(s_win_v), jnp.stack(s_gla))


_drawn_inputs = setup_inputs


def setup_inputs(seed=0):
    import zlib

    import numpy as np

    out = dict(_drawn_inputs(seed))
    spreads = {}
    factors = {'ffn1_norm': 4.987,
     'gla_out_norm': 59.653,
     'swa_sinks': 64.0,
     'gate_bias': 4.288,
     'ffn2_norm': 21.479,
     'final_norm': 22.479,
     'cache_meta_k': 5.456,
     'cache_meta_v': 4.177,
     'w_swa_o': 3.311}
    for name, (base, spread) in spreads.items():
        noise = np.random.default_rng([zlib.crc32(name.encode()), seed]).standard_normal(out[name].shape)
        drawn = base * np.exp(spread * noise) if base else spread * noise
        out[name] = __import__('jax').numpy.asarray(drawn.astype(out[name].dtype))
    for name, factor in factors.items():
        out[name] = (out[name] * factor).astype(out[name].dtype)
    return out
```

```python
from contextlib import ExitStack

import numpy as np

import concourse.bass as bass
from concourse import mybir

ALU = mybir.AluOpType
ACT = mybir.ActivationFunctionType
AX = mybir.AxisListType
F32 = mybir.dt.float32
F32R = mybir.dt.float32r

P = 128
D = 2048
DFF = 5632
KD = D // P
FT = DFF // P
CH = 4
FC = FT // CH
NP_, NS, NM = 256, 8, 16
TR = NP_ + NS
TA = TR + NM
M0 = TR
GH, DK, DV, RANK = 4, 128, 256, 16
TAU = 16.0
CK = 16
NCK = NP_ // CK
NH, HD, WIN = 16, 64, 128
EPS = 1e-6
GA_COLS = (KD - 1) * RANK + P
ROW = 2048

FFN_PAIRS = CH * (FC + KD // 2)
SWA_IN = FFN_PAIRS
GLA_IN = SWA_IN + 6
GATE_A = GLA_IN + 8
GLA_R = GATE_A + 8
MERGE = GLA_R + 4
W_OUT = MERGE + KD
FFN2 = W_OUT + KD // 2
N_PAIRS = FFN2 + FFN_PAIRS

GQ, GK, GV, SQ, SK, SV, KDUP = 0, 4, 8, 16, 24, 26, 28


def build_layer(nc, t):
    ctx = ExitStack()
    with ctx:
        def sb(name, shape, dt=F32):
            return ctx.enter_context(nc.sbuf_tensor(name, shape, dt))

        def sem(name):
            return ctx.enter_context(nc.semaphore(name))

        x_hi = sb("x_hi", [P, KD, TA], F32R)
        x_lo = sb("x_lo", [P, KD, TA], F32R)
        y_hi = sb("y_hi", [P, KD * TR], F32R)
        y_lo = sb("y_lo", [P, KD * TR], F32R)
        w_hi = sb("w_hi", [P, 2, ROW], F32R)
        w_lo = sb("w_lo", [P, 2, ROW], F32R)
        ga_hi = sb("ga_hi", [P, GA_COLS], F32R)
        ga_lo = sb("ga_lo", [P, GA_COLS], F32R)
        raw = sb("raw", [P, 2, ROW])
        hT = sb("hT", [P, KD, TA])
        proj = sb("proj", [P, 32, TA])
        rstd = sb("rstd", [P, TA])
        gadT = sb("gadT", [RANK, TA])
        y3_hi = y_hi[:].rearrange("p (k t) -> p k t", k=KD)
        y3_lo = y_lo[:].rearrange("p (k t) -> p k t", k=KD)
        s1_hi = y_hi[:, 0:FC * TA].rearrange("p (k t) -> p k t", k=FC)
        s1_lo = y_lo[:, 0:FC * TA].rearrange("p (k t) -> p k t", k=FC)

        ones = sb("ones", [P, P])
        ident = sb("ident", [P, P])
        onehot = sb("onehot", [P, CK, CK])
        gains = sb("gains", [P, 4, KD])
        gbias = sb("gbias", [P, 2, KD])
        onorm = sb("onorm", [P, 8])
        nslope = sb("nslope", [P, NH])
        sinks = sb("sinks", [P, NH])
        sink_bh = sb("sink_bh", [P, 1])
        causal = sb("causal", [CK, GH, CK])
        a_up = sb("a_up", [RANK, GH * DK])
        a_bias = sb("a_bias", [P, GH])
        eps = sb("eps", [P, 1])

        R = sb("scratch", [P, 7360])

        def at(o, *shape, parts=P):
            n = int(np.prod(shape))
            v = R[0:parts, o:o + n]
            if len(shape) == 2:
                v = v.rearrange("p (a b) -> p a b", a=shape[0])
            if len(shape) == 3:
                v = v.rearrange("p (a b c) -> p a b c", a=shape[0], b=shape[1])
            return v

        a_n, sig, act_a, b_n, s32 = (at(TA * i, TA) for i in range(5))
        acc, sq, std = (at(TA * i, TA) for i in range(5, 8))
        ga_raw = at(2240, GA_COLS)
        stat = at(256, 64)
        v_new = at(0, 256, parts=NS)
        pT_meta = at(512, 512, parts=NM)
        v_meta = at(2240, 256, parts=NM)
        dist0, dist1 = at(2500, 144), at(2644, 272)
        bias_s = at(2916, 144)
        sc = at(3060, 2, 4, 272)
        pT = at(5236, 3, 512)
        v_tok = at(6772, 2, 256)
        kT_win = at(3060, NS, 2, WIN + 1)
        kT_meta = at(1024, 2, NS, NM)
        q_pad = at(1280, NS, NH)
        ssc = at(1408, 144)
        sT, sT_meta = at(1552, P), at(1680, P, parts=NM)
        k_new = at(320, 2, NS)
        pTs, pTs_meta = at(1808, P), at(1936, P, parts=NM)
        v_win = at(5236, NS, 256)
        v_meta_s = at(3060, NS, 256, parts=NM)
        oT = at(0, 8, TR)
        spl, mnz = at(0, GH, TA), at(3232, GH, TA)
        bc = at(2112, GH, TA)
        scan_keep = at(1120, TA)
        S = at(3232, GH, DV)
        Pd = at(4256, CK, GH, CK)
        kd, edl, eb, qd, dl = (at(o, GH, CK) for o in (5280, 5344, 5408, 5472, 7296))
        attT = at(5536, GH, CK, parts=CK)
        k_tok = at(5600, 512, parts=CK)
        vbuf = at(6112, 8, CK)
        gv_tok = at(6240, 1024, parts=CK)
        a_smp = at(7264, GH, NS)
        gv_new = at(2112, 1024, parts=NS)
        vmask = at(3232, 1024, parts=NS)
        S0 = at(4256, 2, GH, DV)
        sg_r = at(6304, TR)
        osq, ostd, ors, ow = at(2112, 2, TR), at(2700, TR), at(3000, TR), at(3300, 2, TR)
        gb_n, sigb, m1, m2 = (at(o, TR) for o in (6304, 6568, 6832, 7096))
        siga = proj[:, 16:32, 0:TR]
        merged = proj[:, 0:16, 0:TR]

        bank = [ctx.enter_context(nc.psum_tensor(f"bank{i}", [P, 512], F32)) for i in range(8)]

        raw_loaded = [sem("raw_loaded0"), sem("raw_loaded1")]
        hi_split, lo_split = sem("hi_split"), sem("lo_split")
        slab_done, bank_free = sem("slab_done"), sem("bank_free")
        x_loaded = [sem(f"x_loaded{i}") for i in range(4)]
        consts_loaded, tables_loaded = sem("consts_loaded"), sem("tables_loaded")
        eps_set, acc_zero, sq_done, acc_done = sem("eps_set"), sem("acc_zero"), sem("sq_done"), sem("acc_done")
        xhi_done, xlo_done = sem("xhi_done"), sem("xlo_done")
        sumsq_done, std_done, rstd_done = sem("sumsq_done"), sem("std_done"), sem("rstd_done")
        sig_done, acta_done, s_done, shi_done, slo_done = (
            sem(n) for n in ("sig_done", "acta_done", "s_done", "shi_done", "slo_done"))
        gahi_done, galo_done, gad_done, gadT_done = (
            sem(n) for n in ("gahi_done", "galo_done", "gad_done", "gadT_done"))
        kv_out, kdup_done, vtr_done, vtok_done = (sem(n) for n in ("kv_out", "kdup_done", "vtr_done", "vtok_done"))
        scores_done, sc_done, soft_step, exp_done = (
            sem(n) for n in ("scores_done", "sc_done", "soft_step", "exp_done"))
        p_ready, ptr_done, pT_done, so_done, sohi_done, solo_done = (
            sem(n) for n in ("p_ready", "ptr_done", "pT_done", "so_done", "sohi_done", "solo_done"))
        kwin_loaded, vwin_loaded, vmeta_loaded, knew_done, qpad_done = (
            sem(n) for n in ("kwin_loaded", "vwin_loaded", "vmeta_loaded", "knew_done", "qpad_done"))
        swa_pe, swa_act, swa_dve, win_out = (sem(n) for n in ("swa_pe", "swa_act", "swa_dve", "win_out"))
        scan_loaded = sem("scan_loaded")
        z_done, prep_act, prep_dve = sem("z_done"), sem("prep_act"), sem("prep_dve")
        (g_eb, g_dl, g_edl, g_kd, g_diff, g_exp, g_pk, g_P, g_att, g_attT, g_kt, g_vt, g_ktok, g_vtok,
         g_vbuf, g_qd, g_o, g_oT, g_kv, g_S) = (sem(n) for n in (
            "g_eb", "g_dl", "g_edl", "g_kd", "g_diff", "g_exp", "g_pk", "g_P", "g_att", "g_attT", "g_kt",
            "g_vt", "g_ktok", "g_vtok", "g_vbuf", "g_qd", "g_o", "g_oT", "g_kv", "g_S"))
        state_out, nv_tr, nv_done = sem("state_out"), sem("nv_tr"), sem("nv_done")
        s0_loaded = [sem("s0_loaded0"), sem("s0_loaded1")]
        s0_stored = [sem("s0_stored0"), sem("s0_stored1")]
        n_vmask, n_vbc, n_decay, n_state, n_o, n_oT = (
            sem(n) for n in ("n_vmask", "n_vbc", "n_decay", "n_state", "n_o", "n_oT"))
        r_sig, siga_done = sem("r_sig"), sem("siga_done")
        r_done = sem("r_done")
        on_sq, on_sum, on_std, on_rs, on_w, on_g, ohi_done, olo_done = (
            sem(n) for n in ("on_sq", "on_sum", "on_std", "on_rs", "on_w", "on_g", "ohi_done", "olo_done"))
        sigb_done, m_step, merged_done, mhi_done, mlo_done = (
            sem(n) for n in ("sigb_done", "m_step", "merged_done", "mhi_done", "mlo_done"))
        y_done, y_out = sem("y_done"), sem("y_out")

        def decode_out(gp, jp, dst):
            d = dst[64 * jp:64 * jp + 64, 8:16, NP_:TR].rearrange("p (g a j) b -> p a b g j", g=2, a=2)[:, gp]
            s = bank[2][64 * gp:64 * gp + 64, 0:P].rearrange("p (b g a j e) -> p a e b g j", b=NS, g=2, a=2, j=2)[:, gp, jp]
            return d, s

        def chunk_cols(c):
            return slice(M0, TA) if c is None else (
                slice(c * CK, (c + 1) * CK) if isinstance(c, int) else bass.ds(c * CK, CK))

        def gla_exp(act, c, u):
            col = chunk_cols(c)
            if c is not None:
                act.wait_ge(g_S, 4 * u)
                act.wait_ge(g_qd, u - 1) if not isinstance(u, int) or u > 1 else None
            act.activation(eb, bc[:, :, col], ACT.Exp, scale=1.0 / TAU).then_inc(g_eb, 1)
            act.wait_ge(g_dl, u + 1)
            act.activation(edl, dl, ACT.Exp, scale=1.0 / TAU).then_inc(g_edl, 1)
            if c is not None:
                act.wait_ge(g_diff, 2 * u)
                act.activation(Pd, Pd, ACT.Exp, scale=1.0 / TAU).then_inc(g_exp, 1)

        def gla_moves(act, c, u):
            act.wait_ge(g_kt, u + 1)
            if c is not None:
                act.wait_ge(g_kv, u)
            act.activation(k_tok, bank[3][0:CK, :], ACT.Copy).then_inc(g_ktok, 1)
            act.wait_ge(g_vt, u + 1)
            act.activation(gv_tok[:, 0:512], bank[4][0:CK, :], ACT.Copy).then_inc(g_vtok, 1)
            act.activation(gv_tok[:, 512:], bank[5][0:CK, :], ACT.Copy).then_inc(g_vtok, 1)
            if c is not None:
                act.wait_ge(g_o, u)
                act.activation(oT[:, :, chunk_cols(c)], bank[3][:, 0:P].rearrange("p (a b) -> p a b", a=8),
                               ACT.Copy).then_inc(g_oT, 1)

        def gla_decays(dve, c, u):
            if c is None:
                cols, end = slice(M0, TA), slice(TA - 1, TA)
            elif isinstance(c, int):
                cols, end = slice(c * CK, (c + 1) * CK), slice(c * CK + CK - 1, c * CK + CK)
            else:
                cols, end = bass.ds(c * CK, CK), bass.ds(c * CK + CK - 1, 1)
            k, q, b = proj[:, GK:GK + 4, cols], proj[:, GQ:GQ + 4, cols], bc[:, :, cols]
            if c is not None:
                dve.wait_ge(g_kd, u)
            dve.tensor_tensor(dl, bc[:, :, end].broadcast_to([P, GH, CK]), b, ALU.subtract).then_inc(g_dl, 1)
            if c is not None:
                by_s = lambda a: a.rearrange("p h s -> p s h").unsqueeze(3).broadcast_to([P, CK, GH, CK])
                by_t = lambda a: a.unsqueeze(1).broadcast_to([P, CK, GH, CK])
                if not isinstance(u, int) or u > 1:
                    dve.wait_ge(g_att, u - 1)
                dve.tensor_tensor(Pd, by_t(b), by_s(b), ALU.subtract).then_inc(g_diff, 1)
                dve.wait_ge(g_diff, 2 * u - 1)
                dve.tensor_scalar(Pd, Pd, 0.0, None, ALU.min).then_inc(g_diff, 1)
                dve.wait_ge(g_kt, u)
            dve.wait_ge(g_edl, u + 1)
            dve.tensor_tensor(kd, k, edl, ALU.mult).then_inc(g_kd, 1)
            if c is not None:
                dve.wait_ge(g_exp, u)
                dve.tensor_tensor(Pd, Pd, by_s(k), ALU.mult).then_inc(g_pk, 1)
                dve.wait_ge(g_pk, u)
                dve.tensor_tensor(Pd, Pd, by_t(q), ALU.mult).then_inc(g_P, 1)

        def gla_state(dve, c, u):
            if c is not None:
                dve.wait_ge(g_att, u)
                dve.tensor_tensor(attT, bank[2][0:CK, 0:GH * CK].rearrange("p (h t) -> p h t", h=GH), causal[:],
                                  ALU.mult).then_inc(g_attT, 1)
                dve.wait_ge(g_o, u)
                dve.wait_ge(g_S, 4 * u)
            dve.wait_ge(g_eb, u + 1)
            dve.wait_ge(g_kv, u + 1)
            for h in range(GH):
                kv = bank[6 + h // 2][:, (h % 2) * DV:(h % 2 + 1) * DV]
                if c is None:
                    dve.tensor_copy(S[:, h], kv).then_inc(g_S, 1)
                else:
                    dve.scalar_tensor_tensor(S[:, h], S[:, h], eb[:, h, CK - 1:CK], kv, ALU.mult, ALU.add).then_inc(g_S, 1)

        def gla_turn(pe, c, u):
            pe.wait_ge(g_kd, u + 1)
            if c is not None:
                pe.wait_ge(g_ktok, u)
                if not isinstance(u, int) or u > 1:
                    pe.wait_ge(g_oT, u - 1)
            for h in range(GH):
                last = pe.transpose(bank[3][0:CK, h * DK:(h + 1) * DK], kd[:, h], ident[:])
            last.then_inc(g_kt, 1)
            pe.wait_ge(g_vbuf, u + 1)
            if c is not None:
                pe.wait_ge(g_vtok, 2 * u)
            for j in range(8):
                last = pe.transpose(bank[4 + j // 4][0:CK, (j % 4) * P:(j % 4 + 1) * P], vbuf[:, j], ident[:])
            last.then_inc(g_vt, 1)

        def gla_products(pe, c, u):
            if c is not None:
                pe.wait_ge(g_P, u)
                if not isinstance(u, int) or u > 1:
                    pe.wait_ge(g_attT, u - 1)
                for s in range(CK):
                    last = pe.matmul(bank[2][0:CK, 0:GH * CK], onehot[:, s], Pd[:, s].rearrange("p h t -> p (h t)"),
                                     start=(s == 0), stop=(s == CK - 1))
                last.then_inc(g_att, 1)
                pe.wait_ge(g_S, 4 * u)
            pe.wait_ge(g_ktok, u + 1)
            pe.wait_ge(g_vtok, 2 * u + 2)
            for h in range(GH):
                last = pe.matmul(bank[6 + h // 2][:, (h % 2) * DV:(h % 2 + 1) * DV], k_tok[:, h * DK:(h + 1) * DK],
                                 gv_tok[:, h * DV:(h + 1) * DV], start=True, stop=True)
            last.then_inc(g_kv, 1)
            if c is not None:
                pe.wait_ge(g_qd, u)
                pe.wait_ge(g_attT, u)
                for h in range(GH):
                    for q in range(2):
                        out = bank[3][:, (2 * h + q) * CK:(2 * h + q + 1) * CK]
                        pe.matmul(out, S[:, h, q * P:(q + 1) * P], qd[:, h], start=True, stop=False)
                        last = pe.matmul(out, gv_tok[:, h * DV + q * P:h * DV + (q + 1) * P], attT[:, h],
                                         start=False, stop=True)
                last.then_inc(g_o, 1)

        block = ctx.enter_context(nc.Block())

        N_CONST = 12
        N_TABLE = 3

        @block.sync
        def _(sp):
            def load_slab(src, half, b, kt, first=False):
                if not first:
                    sp.wait_ge(lo_split, 2 * half + b - 1)
                sp.dma_start(raw[:, b, 0:kt * P], src).then_inc(raw_loaded[b], 16)

            def load_pairs(w, half0, pairs, kt, i0=0):
                with sp.Fori(i0, pairs) as i:
                    for b in range(2):
                        load_slab(w[bass.ds(i, 1), b], half0 + i, b, kt)

            for b in range(2):
                load_slab(t["w1_in"][0:1, b], 0, b, KD, first=True)
            for q in range(4):
                sp.dma_start(hT[:, 4 * q:4 * q + 4, :], t["xT"][:, 4 * q:4 * q + 4, :]).then_inc(x_loaded[q], 16)
                if q == 0:
                    sp.dma_start(gains[:], t["gains"]).then_inc(consts_loaded, 16)
            for dst, name in ((ones, "c_ones"), (ident, "c_ident"), (onehot, "c_onehot"), (gbias, "gbias"),
                              (onorm, "onorm"), (nslope, "c_nslope"),
                              (causal, "c_causal"), (a_up, "a_up"), (a_bias, "a_bias"), (sink_bh, "sink_bh")):
                sp.dma_start(dst[:], t[name]).then_inc(consts_loaded, 16)
            sp.dma_start(sinks[:], t["sinks"].partition_broadcast(P)).then_inc(consts_loaded, 16)
            sp.dma_start(ga_raw, t["w_ga"]).then_inc(tables_loaded, 16)

            def ffn(w_in, w_out, half0, first=False):
                for c in range(CH):
                    h = half0 + c * (FC + KD // 2)
                    load_pairs(w_in[c * FC:(c + 1) * FC], h, FC, KD, i0=1 if first and c == 0 else 0)
                    load_pairs(w_out[c], h + FC, KD // 2, FC)

            ffn(t["w1_in"], t["w1_out"], 0, first=True)
            sp.dma_start(dist0, t["c_dist0"]).then_inc(tables_loaded, 16)
            sp.dma_start(dist1, t["c_dist1"]).then_inc(tables_loaded, 16)
            sp.dma_start(bias_s, t["c_bias_s"]).then_inc(tables_loaded, 16)
            load_pairs(t["w_proj"][0:6], SWA_IN, 6, KD)
            load_pairs(t["w_proj"][6:14], GLA_IN, 8, KD)
            load_pairs(t["w_proj"][14:22], GATE_A, 8, KD)
            load_pairs(t["w_proj"][22:26], GLA_R, 4, KD)
            load_pairs(t["w_merge"], MERGE, KD, KD)
            load_pairs(t["w_o"], W_OUT, KD // 2, KD)
            ffn(t["w2_in"], t["w2_out"], FFN2)
            for q in range(4):
                sp.wait_ge(y_done, 4 * q + 4)
                sp.dma_start(t["yT"][:, 4 * q:4 * q + 4, :], hT[:, 4 * q:4 * q + 4, 0:TR]).then_inc(y_out, 16)
            sp.wait_ge(y_out, 64)
            sp.wait_ge(kv_out, 32)
            sp.wait_ge(win_out, 32)
            sp.wait_ge(state_out, 16)
            for b in range(2):
                sp.wait_ge(s0_stored[b], 16 * (NS // 2))

        @block.gpsimd
        def _(pool):
            pool.memset(eps[:], EPS).then_inc(eps_set, 1)

            def zero_acc(r):
                if r:
                    pool.wait_ge(sumsq_done, r)
                pool.memset(acc, 0.0).then_inc(acc_zero, 1)
                pool.wait_ge(acc_zero, r + 1)

            def add_square(h, r, m, T):
                pool.tensor_tensor(sq[:, 0:T], h, h, ALU.mult).then_inc(sq_done, 1)
                pool.wait_ge(sq_done, KD * r + m + 1)
                pool.tensor_tensor(acc[:, 0:T], acc[:, 0:T], sq[:, 0:T], ALU.add).then_inc(acc_done, 1)

            zero_acc(0)
            for m in range(KD):
                pool.wait_ge(x_loaded[m // 4], 16)
                if m:
                    pool.wait_ge(acc_done, m)
                add_square(hT[:, m, :], 0, m, TA)

            def residual_squares(r, half0, T):
                pool.wait_ge(bank_free, 2 * half0)
                zero_acc(r)
                with pool.Fori(0, KD) as m:
                    pool.wait_ge(bank_free, 2 * half0 + m + 1)
                    pool.wait_ge(acc_done, KD * r + m)
                    add_square(hT[:, bass.ds(m, 1), 0:T], r, m, T)

            residual_squares(1, SWA_IN - KD // 2, TA)

            pool.wait_ge(bank_free, 2 * GLA_IN)
            pool.dma_start(t["kvT"][:, :, 0:WIN], proj[:, SK:SK + 4, NP_ - WIN:NP_]).then_inc(kv_out, 16)
            pool.dma_start(t["kvT"][:, :, WIN:], proj[:, SK:SK + 4, M0:TA]).then_inc(kv_out, 16)
            pool.memset(q_pad, 0.0).then_inc(qpad_done, 1)

            pool.wait_ge(ptr_done, 8)
            pool.dma_start(kT_win[:, :, :, 0:WIN], t["kT_cache"]).then_inc(kwin_loaded, 16)
            pool.dma_start(kT_meta, t["kT_meta"]).then_inc(kwin_loaded, 16)
            pool.wait_ge(so_done, 8)
            pool.dma_start(v_win[0:WIN - 1], t["v_cache"]).then_inc(vwin_loaded, 16)
            for b in range(NS):
                pool.dma_start(v_win[WIN - 1:WIN, b, :], v_new[b:b + 1, :]).then_inc(vwin_loaded, 16)
            pool.wait_ge(knew_done, 2)
            pool.dma_start(t["winkT"], kT_win[:, :, :, 1:WIN + 1]).then_inc(win_out, 16)
            pool.wait_ge(vwin_loaded, 16 * (1 + NS))
            pool.dma_start(t["winv"], v_win).then_inc(win_out, 16)
            pool.wait_ge(win_out, 32)
            pool.wait_ge(swa_pe, 1)
            pool.dma_start(v_meta_s, t["v_meta"]).then_inc(vmeta_loaded, 16)

            pool.wait_ge(swa_pe, 4)
            pool.dma_start(scan_keep, t["c_scan"]).then_inc(scan_loaded, 16)

            pool.wait_ge(prep_dve, 9)
            pool.tensor_copy(vbuf, proj[:, GV:GV + 8, M0:TA]).then_inc(g_vbuf, 1)

            def operands(c):
                cols = chunk_cols(c)
                pool.wait_ge(g_vt, c + 1)
                pool.tensor_copy(vbuf, proj[:, GV:GV + 8, cols]).then_inc(g_vbuf, 1)
                pool.wait_ge(g_eb, c + 2)
                if not isinstance(c, int) or c:
                    pool.wait_ge(g_o, c)
                pool.tensor_tensor(qd, proj[:, GQ:GQ + 4, cols], eb, ALU.mult).then_inc(g_qd, 1)

            for c in range(4):
                operands(c)
            with pool.Fori(4, NCK) as c:
                operands(c)
            pool.wait_ge(g_S, 4 * (NCK + 1))
            pool.dma_start(t["state_p"], S).then_inc(state_out, 16)

            for u in range(NS):
                b = u % 2
                if u >= 2:
                    pool.wait_ge(n_state, 4 * (u - 1))
                    pool.dma_start(t["state_s"][u - 2], S0[:, b]).then_inc(s0_stored[b], 16)
                    pool.wait_ge(s0_stored[b], 16 * (u // 2))
                    pool.wait_ge(n_o, u - 1)
                pool.dma_start(S0[:, b], t["state_in"][u]).then_inc(s0_loaded[b], 16)
            for b in range(2):
                u = NS - 2 + b
                pool.wait_ge(n_state, 4 * (u + 1))
                pool.dma_start(t["state_s"][u], S0[:, b]).then_inc(s0_stored[b], 16)

            residual_squares(2, W_OUT, TR)
            residual_squares(3, N_PAIRS - KD // 2, TR)

        @block.scalar
        def _(act):
            def split_hi(half, b, kt, first=False):
                act.wait_ge(raw_loaded[b], 16 * (half + 1))
                if not first:
                    act.wait_ge(slab_done, 2 * half + b - 1)
                act.activation(w_hi[:, b, 0:kt * P], raw[:, b, 0:kt * P], ACT.Copy).then_inc(hi_split, 1)

            def tile_hi(r, m, x, T):
                act.activation(x[:, m, 0:T], hT[:, m, 0:T], ACT.Copy,
                               scale=gains[:, r, m]).then_inc(xhi_done, 1)

            def root(r, T):
                act.wait_ge(sumsq_done, r + 1)
                act.activation(std[:, 0:T], bank[7][:, 0:T], ACT.Sqrt, bias=eps[:, 0:1],
                               scale=1.0 / D).then_inc(std_done, 1)

            def ffn(half0, f0, s_hi, T, r_next=None, x_next=None, kt_after=KD):
                for c in range(CH):
                    h0 = half0 + c * (FC + KD // 2)

                    def inner(i, kt_next):
                        half, f = h0 + i, f0 + c * FC + i
                        split_hi(half + 1, 0, kt_next)
                        act.wait_ge(bank_free, 2 * half + 1)
                        act.activation(sig[:, 0:T], a_n[:, 0:T], ACT.Sigmoid).then_inc(sig_done, 1)
                        split_hi(half + 1, 1, kt_next)
                        act.wait_ge(s_done, f + 1)
                        act.activation(s_hi[:, bass.ds(i, 1), 0:T], s32[:, 0:T], ACT.Copy).then_inc(shi_done, 1)

                    with act.Fori(0, FC - 1) as i:
                        inner(i, KD)
                    inner(FC - 1, FC)
                    h1 = h0 + FC
                    last = c == CH - 1

                    def outer(i, kt_next, split=True):
                        for b in range(2):
                            if split:
                                split_hi(h1 + i + 1, b, kt_next)
                            if last and x_next is not None:
                                act.wait_ge(bank_free, 2 * (h1 + i) + b + 1)
                                tile_hi(r_next, bass.ds(2 * i + b, 1), x_next, T)

                    with act.Fori(0, KD // 2 - 1) as i:
                        outer(i, FC)
                    outer(KD // 2 - 1, kt_after, split=h1 + KD // 2 < N_PAIRS)

            split_hi(0, 0, KD, first=True)
            act.wait_ge(consts_loaded, 16 * N_CONST)
            for m in range(KD):
                act.wait_ge(x_loaded[m // 4], 16)
                tile_hi(0, slice(m, m + 1), x_hi, TA)
                if m == 3:
                    split_hi(0, 1, KD, first=True)
            act.wait_ge(tables_loaded, 16)
            act.activation(ga_hi[:], ga_raw, ACT.Copy).then_inc(gahi_done, 1)
            act.wait_ge(eps_set, 1)
            root(0, TA)
            ffn(0, 0, s1_hi, TA, 1, x_hi)

            root(1, TA)
            for i in range(6):
                for b in range(2):
                    split_hi(SWA_IN + i + 1, b, KD)
            act.wait_ge(bank_free, 2 * GLA_IN)
            for a in range(2):
                for b in range(2):
                    act.activation(proj[64 * b:64 * b + 64, KDUP + a:KDUP + 4:2, :],
                                   proj[64 * a:64 * a + 64, SK:SK + 2, :], ACT.Copy).then_inc(kdup_done, 1)

            def soft_exp(u):
                nk = 144 if u % 2 == 0 else 272
                act.wait_ge(soft_step, 4 * u + 4)
                for j in range(4):
                    act.activation(sc[:, u % 2, j, 0:nk], sc[:, u % 2, j, 0:nk], ACT.Exp,
                                   bias=stat[:, 8 + j:9 + j], accum_out=stat[:, 16 + j:17 + j]).then_inc(exp_done, 1)
                act.activation(stat[:, 20:24], stat[:, 12:16], ACT.Exp).then_inc(exp_done, 1)

            def move_pT(u):
                act.wait_ge(ptr_done, u + 1)
                if u:
                    act.wait_ge(so_done, u)
                act.activation(pT_meta, bank[5][0:NM, :], ACT.Copy).then_inc(pT_done, 1)
                act.activation(pT[:, 0], bank[6][:], ACT.Copy).then_inc(pT_done, 1)
                src = bank[7] if u % 2 else bank[6]
                act.activation(pT[:, 1 if u % 2 else 2], src[:], ACT.Copy).then_inc(pT_done, 1)

            def out_hi(u):
                g, q0 = u // 2, (u % 2) * WIN
                act.wait_ge(so_done, u + 1)
                for jp in range(2):
                    src = bank[6][0:HD, :].rearrange("p (j e q) -> p e j q", j=2, e=2)[:, jp]
                    act.activation(y3_hi[64 * jp:64 * jp + 64, 8 + 2 * g:10 + 2 * g, q0:q0 + WIN], src,
                                   ACT.Copy).then_inc(sohi_done, 1)

            for u in range(8):
                half = GLA_IN + u
                split_hi(half + 1, 0, KD)
                if u == 0:
                    act.wait_ge(vtr_done, 1)
                    act.activation(v_tok, bank[2][:].rearrange("p (a b) -> p a b", a=2), ACT.Copy).then_inc(vtok_done, 1)
                    act.activation(v_meta, bank[3][0:NM, 0:256], ACT.Copy).then_inc(vtok_done, 1)
                    act.activation(v_new, bank[4][0:NS, 0:256], ACT.Copy).then_inc(vtok_done, 1)
                if u:
                    move_pT(u - 1)
                soft_exp(u)
                split_hi(half + 1, 1, KD)
                if u:
                    out_hi(u - 1)

            act.activation(k_new, proj[:, SK:SK + 2, NP_:TR], ACT.Copy).then_inc(knew_done, 1)
            act.wait_ge(qpad_done, 1)
            for gp in range(2):
                for jp in range(2):
                    src = proj[64 * jp:64 * jp + 64, SQ:SQ + 8, NP_:TR].rearrange(
                        "p (g a j) b -> p a b g j", g=2, a=2)[:, gp]
                    dst = q_pad[64 * gp:64 * gp + 64].rearrange(
                        "p b (g a j e) -> p a e b g j", g=2, a=2, j=2)[:, gp, jp]
                    act.activation(dst, src, ACT.Copy).then_inc(qpad_done, 1)

            def gate_a(half, m):
                act.activation(siga[:, m], siga[:, m], ACT.Sigmoid, bias=gbias[:, 0, m]).then_inc(siga_done, 1)

            for e in range(8):
                half, b = GATE_A + e // 2, e % 2
                split_hi(half + 1, b, KD)
                if e == 0:
                    move_pT(7)
                if e == 1:
                    out_hi(7)
                    act.wait_ge(kwin_loaded, 32)
                    act.wait_ge(knew_done, 1)
                    act.activation(kT_win[:, :, :, WIN].rearrange("p b g -> p g b"), k_new, ACT.Copy).then_inc(knew_done, 1)
                if e == 2:
                    act.wait_ge(swa_pe, 1)
                    act.activation(sT, bank[2][:, 0:P], ACT.Copy).then_inc(swa_act, 1)
                    act.activation(sT_meta, bank[3][0:NM, 0:P], ACT.Copy).then_inc(swa_act, 1)
                if e == 3:
                    act.wait_ge(swa_dve, 5)
                    act.activation(ssc, ssc, ACT.Exp, bias=stat[:, 3:4], accum_out=stat[:, 5:6]).then_inc(swa_act, 1)
                    act.activation(stat[:, 6:7], stat[:, 4:5], ACT.Exp).then_inc(swa_act, 1)
                if e == 4:
                    act.wait_ge(swa_pe, 3)
                    act.activation(pTs, bank[5][:, 0:P], ACT.Copy).then_inc(swa_act, 1)
                    act.activation(pTs_meta, bank[6][0:NM, 0:P], ACT.Copy).then_inc(swa_act, 1)
                if e == 5:
                    act.wait_ge(swa_pe, 4)
                    for gp in range(2):
                        for jp in range(2):
                            dst, src = decode_out(gp, jp, y3_hi)
                            act.activation(dst, src, ACT.Copy).then_inc(swa_act, 1)
                if e == 6:
                    act.wait_ge(z_done, 1)
                    act.wait_ge(swa_dve, 12)
                    for h in range(GH):
                        act.activation(spl[:, h], bank[2 + h][:, 0:TA], ACT.Abs, bias=a_bias[:, h:h + 1]).then_inc(prep_act, 1)
                    act.wait_ge(prep_act, 4)
                    act.activation(spl, spl, ACT.Exp, scale=-1.0).then_inc(prep_act, 1)
                    act.wait_ge(prep_act, 5)
                    act.activation(spl, spl, ACT.Ln, bias=1.0).then_inc(prep_act, 1)
                if e == 7:
                    act.wait_ge(prep_dve, 9)
                    act.activation(a_smp, bc[:, :, NP_:TR], ACT.Exp, scale=1.0 / TAU).then_inc(prep_act, 1)
                    gla_exp(act, None, 0)
                    gla_moves(act, None, 0)
                act.wait_ge(bank_free, 2 * half + b + 1)
                gate_a(half, slice(e, e + 1))

            def chunks(i, first):
                for b in range(2):
                    half = GATE_A + 4 + i
                    split_hi(half + 1, b, KD)
                    for q in range(2):
                        c = 4 * i + 2 * b + q
                        gla_exp(act, c, c + 1)
                        gla_moves(act, c, c + 1)
                    act.wait_ge(bank_free, 2 * half + b + 1)
                    gate_a(half, bass.ds(8 + 2 * i + b, 1))

            chunks(0, True)
            with act.Fori(1, 4) as i:
                chunks(i, False)

            for i in range(4):
                half = GLA_R + i
                for b in range(2):
                    u, m = 2 * i + b, 2 * i + b
                    split_hi(half + 1, b, KD)
                    if u == 0:
                        act.wait_ge(nv_tr, 1)
                        act.activation(gv_new[:, 0:512], bank[4][0:NS, :], ACT.Copy).then_inc(nv_done, 1)
                        act.activation(gv_new[:, 512:], bank[5][0:NS, :], ACT.Copy).then_inc(nv_done, 1)
                        act.wait_ge(nv_done, 2)
                        act.wait_ge(state_out, 16)
                    else:
                        act.wait_ge(n_vbc, u)
                    act.activation(vmask, gv_new, ACT.Copy, scale=ident[0:NS, u:u + 1]).then_inc(n_vmask, 1)
                    act.wait_ge(s0_loaded[b], 16 * (u // 2 + 1))
                    for h in range(GH):
                        act.activation(S0[:, b, h], S0[:, b, h], ACT.Copy, scale=a_smp[:, h, u:u + 1]).then_inc(n_decay, 1)
                    act.wait_ge(bank_free, 2 * half + b + 1)
                    if m:
                        act.wait_ge(r_done, m)
                    act.activation(sg_r, proj[:, GV + m, 0:TR], ACT.Sigmoid).then_inc(r_sig, 1)
                    act.wait_ge(n_o, u + 1)
                    act.activation(oT[:, :, NP_ + u], bank[3][:, 0:8], ACT.Copy).then_inc(n_oT, 1)

            act.wait_ge(n_oT, NS)
            act.wait_ge(g_oT, NCK)
            for h in range(GH):
                if h:
                    act.wait_ge(on_sum, h)
                act.activation(osq, oT[:, 2 * h:2 * h + 2, :], ACT.Square).then_inc(on_sq, 1)
                act.wait_ge(on_sum, h + 1)
                if h:
                    act.wait_ge(on_rs, h)
                act.activation(ostd, bank[2 + h][:, 0:TR], ACT.Sqrt, bias=eps[:, 0:1], scale=1.0 / DV).then_inc(on_std, 1)
                for q in range(2):
                    act.wait_ge(on_g, 2 * h + q + 1)
                    act.activation(y3_hi[:, 2 * h + q], ow[:, q], ACT.Copy).then_inc(ohi_done, 1)

            def merge(m, kt_next):
                split_hi(MERGE + m + 1, 0, kt_next)
                act.wait_ge(bank_free, 2 * (MERGE + m) + 1)
                act.activation(sigb, gb_n, ACT.Sigmoid, bias=gbias[:, 1, bass.ds(m, 1)]).then_inc(sigb_done, 1)
                split_hi(MERGE + m + 1, 1, kt_next)

            with act.Fori(0, KD) as m:
                merge(m, KD)
            for q in range(4):
                act.wait_ge(merged_done, 4 * q + 4)
                if q == 0:
                    act.wait_ge(slab_done, 2 * W_OUT)
                act.activation(x_hi[:, 4 * q:4 * q + 4, 0:TR], merged[:, 4 * q:4 * q + 4, :], ACT.Copy).then_inc(mhi_done, 1)

            def w_out(i):
                for b in range(2):
                    split_hi(W_OUT + i + 1, b, KD)
                    act.wait_ge(bank_free, 2 * (W_OUT + i) + b + 1)
                    tile_hi(2, bass.ds(2 * i + b, 1), y3_hi, TR)

            with act.Fori(0, KD // 2) as i:
                w_out(i)
            root(2, TR)
            ffn(FFN2, FT, x_hi, TR)
            root(3, TR)

        @block.vector
        def _(dve):
            def split_lo(half, b, kt):
                dve.wait_ge(hi_split, 2 * half + b + 1)
                dve.tensor_tensor(w_lo[:, b, 0:kt * P], raw[:, b, 0:kt * P], w_hi[:, b, 0:kt * P].bitcast(F32),
                                  ALU.subtract).then_inc(lo_split, 1)

            def tile_lo(r, m, x, T, n):
                dve.wait_ge(xhi_done, n)
                dve.scalar_tensor_tensor(x[1][:, m, 0:T], hT[:, m, 0:T], gains[:, r, m],
                                         x[0][:, m, 0:T].bitcast(F32), ALU.mult, ALU.subtract).then_inc(xlo_done, 1)

            def inverse(r, T):
                dve.wait_ge(std_done, r + 1)
                dve.reciprocal(rstd[:, 0:T], std[:, 0:T]).then_inc(rstd_done, 1)
                dve.wait_ge(rstd_done, r + 1)

            def ffn(half0, f0, s_hi, s_lo, T, r_next=None, x_next=None, kt_after=KD):
                for c in range(CH):
                    h0 = half0 + c * (FC + KD // 2)

                    def inner(i, kt_next):
                        half, f = h0 + i, f0 + c * FC + i
                        dve.wait_ge(slab_done, 2 * half + 1)
                        dve.tensor_tensor(a_n[:, 0:T], bank[0][:, 0:T], rstd[:, 0:T], ALU.mult).then_inc(bank_free, 1)
                        split_lo(half + 1, 0, kt_next)
                        dve.wait_ge(sig_done, f + 1)
                        dve.tensor_tensor(act_a[:, 0:T], a_n[:, 0:T], sig[:, 0:T], ALU.mult).then_inc(acta_done, 1)
                        dve.wait_ge(slab_done, 2 * half + 2)
                        dve.tensor_tensor(b_n[:, 0:T], bank[1][:, 0:T], rstd[:, 0:T], ALU.mult).then_inc(bank_free, 1)
                        dve.wait_ge(bank_free, 2 * half + 2)
                        dve.wait_ge(acta_done, f + 1)
                        dve.tensor_tensor(s32[:, 0:T], act_a[:, 0:T], b_n[:, 0:T], ALU.mult).then_inc(s_done, 1)
                        split_lo(half + 1, 1, kt_next)
                        dve.wait_ge(shi_done, f + 1)
                        dve.tensor_tensor(s_lo[:, bass.ds(i, 1), 0:T], s32[:, 0:T],
                                          s_hi[:, bass.ds(i, 1), 0:T].bitcast(F32), ALU.subtract).then_inc(slo_done, 1)

                    with dve.Fori(0, FC - 1) as i:
                        inner(i, KD)
                    inner(FC - 1, FC)
                    h1 = h0 + FC
                    last = c == CH - 1

                    def outer(i, kt_next, split=True):
                        for b in range(2):
                            n, m = 2 * (h1 + i) + b, bass.ds(2 * i + b, 1)
                            dve.wait_ge(slab_done, n + 1)
                            dve.scalar_tensor_tensor(hT[:, m, 0:T], bank[b][:, 0:T], 0.5, hT[:, m, 0:T],
                                                     ALU.mult, ALU.add).then_inc(bank_free, 1)
                            if split:
                                split_lo(h1 + i + 1, b, kt_next)
                            if last and x_next is not None:
                                tile_lo(r_next, m, x_next, T, KD * r_next + 2 * i + b + 1)

                    with dve.Fori(0, KD // 2 - 1) as i:
                        outer(i, FC)
                    outer(KD // 2 - 1, kt_after, split=h1 + KD // 2 < N_PAIRS)

            split_lo(0, 0, KD)
            dve.wait_ge(consts_loaded, 16 * N_CONST)
            for m in range(KD):
                tile_lo(0, slice(m, m + 1), (x_hi, x_lo), TA, m + 1)
                if m == 3:
                    split_lo(0, 1, KD)
            dve.wait_ge(gahi_done, 1)
            dve.tensor_tensor(ga_lo[:], ga_raw, ga_hi[:].bitcast(F32), ALU.subtract).then_inc(galo_done, 1)
            inverse(0, TA)
            ffn(0, 0, s1_hi, s1_lo, TA, 1, (x_hi, x_lo))
            inverse(1, TA)

            def project(half, b, dst, scale, T):
                dve.wait_ge(slab_done, 2 * half + b + 1)
                dve.scalar_tensor_tensor(dst, bank[b][:, 0:T], scale, rstd[:, 0:T], ALU.mult, ALU.mult).then_inc(bank_free, 1)
                split_lo(half + 1, b, KD)

            for i in range(6):
                for b in range(2):
                    T, scale = (TR, HD ** -0.5) if i < 4 else (TA, 1.0)
                    project(SWA_IN + i, b, proj[:, SQ + 2 * i + b, 0:T], scale, T)
                    if i == 0 and b == 0:
                        dve.wait_ge(gad_done, 1)
                        dve.tensor_tensor(gadT[:], bank[6][0:RANK, 0:TA], rstd[0:RANK, :], ALU.mult).then_inc(gadT_done, 1)

            def soft_max(u):
                g, blk = u // 2, u % 2
                nk, dist = (272, dist1) if blk else (144, dist0)
                dve.wait_ge(scores_done, u + 1)
                for j in range(4):
                    h = 4 * g + j
                    dve.scalar_tensor_tensor(sc[:, u % 2, j, 0:nk], dist, nslope[:, h:h + 1], bank[2 + j][:, 0:nk],
                                             ALU.mult, ALU.add).then_inc(sc_done, 1)
                dve.wait_ge(sc_done, 4 * u + 4)
                dve.tensor_reduce(stat[:, 0:4], sc[:, u % 2, :, 0:nk], AX.X, ALU.max).then_inc(soft_step, 1)
                dve.wait_ge(soft_step, 4 * u + 1)
                dve.tensor_tensor(stat[:, 4:8], stat[:, 0:4], sinks[:, 4 * g:4 * g + 4], ALU.max).then_inc(soft_step, 1)
                dve.wait_ge(soft_step, 4 * u + 2)
                dve.tensor_scalar(stat[:, 8:12], stat[:, 4:8], -1.0, None, ALU.mult).then_inc(soft_step, 1)
                dve.tensor_tensor(stat[:, 12:16], sinks[:, 4 * g:4 * g + 4], stat[:, 4:8], ALU.subtract).then_inc(soft_step, 1)

            def soft_norm(u):
                nk = 272 if u % 2 else 144
                dve.wait_ge(exp_done, 5 * u + 5)
                dve.tensor_tensor(stat[:, 24:28], stat[:, 16:20], stat[:, 20:24], ALU.add).then_inc(p_ready, 1)
                dve.wait_ge(p_ready, 6 * u + 1)
                dve.reciprocal(stat[:, 28:32], stat[:, 24:28]).then_inc(p_ready, 1)
                dve.wait_ge(p_ready, 6 * u + 2)
                for j in range(4):
                    dve.tensor_scalar(sc[:, u % 2, j, 0:nk], sc[:, u % 2, j, 0:nk], stat[:, 28 + j:29 + j], None,
                                      ALU.mult).then_inc(p_ready, 1)

            def out_lo(u):
                g, q0 = u // 2, (u % 2) * WIN
                dve.wait_ge(sohi_done, 2 * u + 2)
                for jp in range(2):
                    src = bank[6][0:HD, :].rearrange("p (j e q) -> p e j q", j=2, e=2)[:, jp]
                    rows, tiles = slice(64 * jp, 64 * jp + 64), slice(8 + 2 * g, 10 + 2 * g)
                    dve.tensor_tensor(y3_lo[rows, tiles, q0:q0 + WIN], src,
                                      y3_hi[rows, tiles, q0:q0 + WIN].bitcast(F32), ALU.subtract).then_inc(solo_done, 1)

            dve.wait_ge(tables_loaded, 16 * 4)
            for u in range(8):
                T, scale = (TR, DK ** -0.5) if u < 2 else (TA, 1.0)
                project(GLA_IN + u, 0, proj[:, 2 * u, 0:T], scale, T)
                soft_max(u)
                project(GLA_IN + u, 1, proj[:, 2 * u + 1, 0:T], scale, T)
                if u:
                    out_lo(u - 1)
                soft_norm(u)

            def gate_a(half, b, m):
                dve.wait_ge(slab_done, 2 * half + b + 1)
                dve.tensor_tensor(siga[:, m], bank[b][:, 0:TR], rstd[:, 0:TR], ALU.mult).then_inc(bank_free, 1)
                split_lo(half + 1, b, KD)

            dve.wait_ge(kv_out, 32)
            dve.wait_ge(qpad_done, 5)
            dve.wait_ge(knew_done, 1)
            for e in range(8):
                half, b = GATE_A + e // 2, e % 2
                gate_a(half, b, slice(e, e + 1))
                if e == 1:
                    out_lo(7)
                if e == 3:
                    dve.wait_ge(swa_pe, 2)
                    dve.tensor_tensor(ssc, bank[4][:, 0:144], bias_s, ALU.add).then_inc(swa_dve, 1)
                    dve.wait_ge(swa_dve, 1)
                    dve.tensor_reduce(stat[:, 0:1], ssc, AX.X, ALU.max).then_inc(swa_dve, 1)
                    dve.wait_ge(swa_dve, 2)
                    dve.tensor_tensor(stat[:, 2:3], stat[:, 0:1], sink_bh[:], ALU.max).then_inc(swa_dve, 1)
                    dve.wait_ge(swa_dve, 3)
                    dve.tensor_scalar(stat[:, 3:4], stat[:, 2:3], -1.0, None, ALU.mult).then_inc(swa_dve, 1)
                    dve.tensor_tensor(stat[:, 4:5], sink_bh[:], stat[:, 2:3], ALU.subtract).then_inc(swa_dve, 1)
                    dve.wait_ge(swa_act, 4)
                    dve.tensor_tensor(stat[:, 7:8], stat[:, 5:6], stat[:, 6:7], ALU.add).then_inc(swa_dve, 1)
                    dve.wait_ge(swa_dve, 6)
                    dve.reciprocal(stat[:, 8:9], stat[:, 7:8]).then_inc(swa_dve, 1)
                    dve.wait_ge(swa_dve, 7)
                    dve.tensor_scalar(ssc, ssc, stat[:, 8:9], None, ALU.mult).then_inc(swa_dve, 1)
                if e == 5:
                    dve.wait_ge(swa_act, 10)
                    for gp in range(2):
                        for jp in range(2):
                            hi, src = decode_out(gp, jp, y3_hi)
                            lo, _ = decode_out(gp, jp, y3_lo)
                            dve.tensor_tensor(lo, src, hi.bitcast(F32), ALU.subtract).then_inc(swa_dve, 1)
                if e == 6:
                    dve.wait_ge(prep_act, 4)
                    dve.wait_ge(win_out, 32)
                    for h in range(GH):
                        dve.tensor_scalar(mnz[:, h], bank[2 + h][:, 0:TA], a_bias[:, h:h + 1], 0.0,
                                          ALU.add, ALU.min).then_inc(prep_dve, 1)
                    dve.wait_ge(prep_dve, 4)
                    dve.wait_ge(prep_act, 6)
                    dve.tensor_tensor(mnz, mnz, spl, ALU.subtract).then_inc(prep_dve, 1)
                    dve.wait_ge(prep_dve, 5)
                    dve.wait_ge(scan_loaded, 16)
                    for h in range(GH):
                        dve.tensor_tensor_scan(bc[:, h], scan_keep, mnz[:, h], 0.0, ALU.mult,
                                               ALU.add).then_inc(prep_dve, 1)
                    dve.wait_ge(prep_dve, 9)
                if e == 7:
                    gla_decays(dve, None, 0)
                    gla_state(dve, None, 0)

            def gate_and_chunks(i):
                for b in range(2):
                    gate_a(GATE_A + 4 + i, b, bass.ds(8 + 2 * i + b, 1))
                    for q in range(2):
                        c = 4 * i + 2 * b + q
                        gla_decays(dve, c, c + 1)
                        gla_state(dve, c, c + 1)

            gate_and_chunks(0)
            with dve.Fori(1, 4) as i:
                gate_and_chunks(i)

            dve.wait_ge(nv_tr, 1)
            dve.wait_ge(g_vbuf, NCK + 1)
            for i in range(4):
                half = GLA_R + i
                for b in range(2):
                    u = m = 2 * i + b
                    dve.wait_ge(slab_done, 2 * half + b + 1)
                    dve.tensor_tensor(proj[:, GV + m, 0:TR], bank[b][:, 0:TR], rstd[:, 0:TR], ALU.mult).then_inc(bank_free, 1)
                    split_lo(half + 1, b, KD)
                    dve.wait_ge(n_vbc, u + 1)
                    for h in range(GH):
                        dve.wait_ge(n_decay, 4 * u + h + 1)
                        dve.scalar_tensor_tensor(S0[:, b, h], bank[4 + h // 2][:, (h % 2) * DV:(h % 2 + 1) * DV],
                                                 proj[:, GK + h, NP_ + u:NP_ + u + 1], S0[:, b, h],
                                                 ALU.mult, ALU.add).then_inc(n_state, 1)
                    dve.wait_ge(r_sig, m + 1)
                    dve.tensor_tensor(proj[:, GV + m, 0:TR], proj[:, GV + m, 0:TR], sg_r, ALU.mult).then_inc(r_done, 1)

            dve.wait_ge(r_done, 8)
            for h in range(GH):
                dve.wait_ge(on_std, h + 1)
                if h:
                    dve.wait_ge(on_w, 2 * h)
                dve.reciprocal(ors, ostd).then_inc(on_rs, 1)
                dve.wait_ge(on_rs, h + 1)
                for q in range(2):
                    j = 2 * h + q
                    dve.scalar_tensor_tensor(ow[:, q], oT[:, j, :], onorm[:, j:j + 1], ors, ALU.mult, ALU.mult).then_inc(on_w, 1)
                for q in range(2):
                    j = 2 * h + q
                    dve.wait_ge(on_w, j + 1)
                    dve.tensor_tensor(ow[:, q], ow[:, q], proj[:, GV + j, 0:TR], ALU.mult).then_inc(on_g, 1)
                for q in range(2):
                    j = 2 * h + q
                    dve.wait_ge(ohi_done, j + 1)
                    dve.tensor_tensor(y3_lo[:, j], ow[:, q], y3_hi[:, j].bitcast(F32), ALU.subtract).then_inc(olo_done, 1)

            dve.wait_ge(siga_done, KD)

            def merge(m):
                half = MERGE + m
                dve.wait_ge(slab_done, 2 * half + 1)
                dve.tensor_tensor(gb_n, bank[0][:, 0:TR], rstd[:, 0:TR], ALU.mult).then_inc(bank_free, 1)
                split_lo(half + 1, 0, KD)
                dve.wait_ge(slab_done, 2 * half + 2)
                dve.tensor_tensor(m1, siga[:, bass.ds(m, 1)], bank[1][:, 0:TR], ALU.mult).then_inc(m_step, 1)
                dve.wait_ge(sigb_done, m + 1)
                dve.tensor_tensor(m2, sigb, bank[2][:, 0:TR], ALU.mult).then_inc(bank_free, 1)
                dve.wait_ge(bank_free, 2 * half + 2)
                dve.tensor_tensor(merged[:, bass.ds(m, 1)], m1, m2, ALU.add).then_inc(merged_done, 1)
                split_lo(half + 1, 1, KD)

            with dve.Fori(0, KD) as m:
                merge(m)
            for q in range(4):
                dve.wait_ge(mhi_done, q + 1)
                dve.tensor_tensor(x_lo[:, 4 * q:4 * q + 4, 0:TR], merged[:, 4 * q:4 * q + 4, :],
                                  x_hi[:, 4 * q:4 * q + 4, 0:TR].bitcast(F32), ALU.subtract).then_inc(mlo_done, 1)

            with dve.Fori(0, KD // 2) as i:
                for b in range(2):
                    m = bass.ds(2 * i + b, 1)
                    dve.wait_ge(slab_done, 2 * (W_OUT + i) + b + 1)
                    dve.tensor_tensor(hT[:, m, 0:TR], bank[b][:, 0:TR], hT[:, m, 0:TR], ALU.add).then_inc(bank_free, 1)
                    split_lo(W_OUT + i + 1, b, KD)
                    tile_lo(2, m, (y3_hi, y3_lo), TR, 2 * KD + 2 * i + b + 1)
            inverse(2, TR)
            ffn(FFN2, FT, x_hi, x_lo, TR)
            inverse(3, TR)
            for m in range(KD):
                dve.scalar_tensor_tensor(hT[:, m, 0:TR], hT[:, m, 0:TR], gains[:, 3, m:m + 1], rstd[:, 0:TR],
                                         ALU.mult, ALU.mult).then_inc(y_done, 1)

        @block.tensor
        def _(pe):
            def product(out, b, k0, k1, x, T, n, ready=None):
                pe.wait_ge(hi_split, n + 1)
                for k in range(k0, k1):
                    if ready is not None:
                        ready(k)
                    w = w_hi[:, b, k * P:(k + 1) * P]
                    pe.matmul(out, w, x[0][:, k, 0:T], start=(k == k0), stop=False)
                    pe.matmul(out, w, x[1][:, k, 0:T], start=False, stop=False)
                pe.wait_ge(lo_split, n + 1)
                for k in range(k0, k1):
                    last = pe.matmul(out, w_lo[:, b, k * P:(k + 1) * P], x[0][:, k, 0:T], start=False, stop=(k == k1 - 1))
                return last

            def slab(half, b, kt, x, T, ready=None, first=False):
                if not first:
                    pe.wait_ge(bank_free, 2 * half + b - 1)
                product(bank[b][:, 0:T], b, 0, kt, x, T, 2 * half + b, ready).then_inc(slab_done, 1)

            def sum_squares(r, T):
                pe.wait_ge(acc_done, KD * (r + 1))
                pe.matmul(bank[7][:, 0:T], ones[:], acc[:, 0:T], start=True, stop=True).then_inc(sumsq_done, 1)

            def tiles_of_norm(r):
                def ready(k):
                    pe.wait_ge(xlo_done, KD * r + k + 1)
                return ready

            def ffn(half0, f0, x, s, T, r):
                for c in range(CH):
                    h0 = half0 + c * (FC + KD // 2)
                    i0 = 0
                    if c == 0:
                        slab(h0, 0, KD, x, T, ready=tiles_of_norm(r), first=half0 == 0)
                        sum_squares(r, T)
                        slab(h0, 1, KD, x, T, first=half0 == 0)
                        i0 = 1
                    with pe.Fori(i0, FC) as i:
                        for b in range(2):
                            slab(h0 + i, b, KD, x, T)
                    h1 = h0 + FC
                    slab(h1, 0, FC, s, T, ready=lambda k: pe.wait_ge(slo_done, f0 + c * FC + k + 1))
                    slab(h1, 1, FC, s, T)
                    with pe.Fori(1, KD // 2) as i:
                        for b in range(2):
                            slab(h1 + i, b, FC, s, T)

            x = (x_hi, x_lo)
            y = (y3_hi, y3_lo)
            pe.wait_ge(consts_loaded, 16 * N_CONST)
            ffn(0, 0, x, (s1_hi, s1_lo), TA, 0)

            slab(SWA_IN, 0, KD, x, TR, ready=tiles_of_norm(1))
            sum_squares(1, TA)
            pe.wait_ge(galo_done, 1)
            for k in range(KD):
                cols = slice(k * RANK, k * RANK + P)
                pe.matmul(bank[6][:, 0:TA], ga_hi[:, cols], x_hi[:, k, :], start=(k == 0), stop=False)
                pe.matmul(bank[6][:, 0:TA], ga_hi[:, cols], x_lo[:, k, :], start=False, stop=False)
                last = pe.matmul(bank[6][:, 0:TA], ga_lo[:, cols], x_hi[:, k, :], start=False, stop=(k == KD - 1))
            last.then_inc(gad_done, 1)
            slab(SWA_IN, 1, KD, x, TR)
            for i in range(1, 6):
                for b in range(2):
                    slab(SWA_IN + i, b, KD, x, TR if i < 4 else TA)

            def values_to_rows():
                pe.wait_ge(bank_free, 2 * GLA_IN)
                for ft in range(2):
                    for tt in range(2):
                        o = tt * 256 + ft * P
                        pe.transpose(bank[2][:, o:o + P], proj[:, SV + ft, tt * P:(tt + 1) * P], ident[:])
                    pe.transpose(bank[3][0:NM, ft * P:(ft + 1) * P], proj[:, SV + ft, M0:TA], ident[:])
                    last = pe.transpose(bank[4][0:NS, ft * P:(ft + 1) * P], proj[:, SV + ft, NP_:TR], ident[:])
                last.then_inc(vtr_done, 1)

            def scores(u):
                g, q0, nk = u // 2, (u % 2) * WIN, WIN * (u % 2 + 1)
                for j in range(4):
                    h = 4 * g + j
                    rows = slice(64 * (h % 2), 64 * (h % 2) + 64)
                    q = proj[rows, SQ + h // 2, q0:q0 + WIN]
                    if u and j == 3:
                        pe.wait_ge(pT_done, 3 * (u - 1) + 1)
                    pe.matmul(bank[2 + j][:, 0:nk], q, proj[rows, KDUP + g, 0:nk], start=True, stop=True)
                    last = pe.matmul(bank[2 + j][:, nk:nk + NM], q, proj[rows, KDUP + g, M0:TA], start=True, stop=True)
                last.then_inc(scores_done, 1)

            def turn_scores(u):
                nk = WIN * (u % 2 + 1)
                pe.wait_ge(p_ready, 6 * u + 6)
                if u:
                    pe.wait_ge(solo_done, 2 * u)
                for j in range(4):
                    pe.transpose(bank[5][0:NM, j * P:(j + 1) * P], sc[:, u % 2, j, nk:nk + NM], ident[:])
                for kc in range(u % 2 + 1):
                    for j in range(4):
                        last = pe.transpose(bank[6 + kc][:, j * P:(j + 1) * P], sc[:, u % 2, j, kc * P:(kc + 1) * P], ident[:])
                last.then_inc(ptr_done, 1)

            def weigh_values(u):
                g = u // 2
                cols = slice(g * HD, (g + 1) * HD)
                pe.wait_ge(pT_done, 3 * u + 3)
                out = bank[6][0:HD, :]
                pe.matmul(out, v_meta[:, cols], pT_meta, start=True, stop=False)
                for kc in range(u % 2 + 1):
                    last = pe.matmul(out, v_tok[:, kc, cols], pT[:, kc], start=False, stop=(kc == u % 2))
                last.then_inc(so_done, 1)

            for u in range(8):
                T = TR if u < 2 else TA
                slab(GLA_IN + u, 0, KD, x, T)
                if u == 0:
                    values_to_rows()
                    pe.wait_ge(kdup_done, 4)
                    pe.wait_ge(vtok_done, 3)
                else:
                    turn_scores(u - 1)
                scores(u)
                slab(GLA_IN + u, 1, KD, x, T)
                if u:
                    weigh_values(u - 1)

            for e in range(8):
                slab(GATE_A + e // 2, e % 2, KD, x, TR)
                if e == 0:
                    turn_scores(7)
                if e == 1:
                    weigh_values(7)
                if e == 2:
                    pe.wait_ge(knew_done, 2)
                    pe.wait_ge(qpad_done, 5)
                    for b in range(NS):
                        for g in range(2):
                            cols = slice(b * NH + 8 * g, b * NH + 8 * g + 8)
                            pe.matmul(bank[2][:, cols], kT_win[:, b, g, 1:WIN + 1], q_pad[:, b, 8 * g:8 * g + 8], start=True, stop=True)
                            last = pe.matmul(bank[3][0:NM, cols], kT_meta[:, g, b, :], q_pad[:, b, 8 * g:8 * g + 8], start=True, stop=True)
                    last.then_inc(swa_pe, 1)
                    pe.wait_ge(swa_act, 2)
                    pe.transpose(bank[4][:, 0:P], sT, ident[:])
                    pe.transpose(bank[4][:, P:P + NM], sT_meta, ident[0:NM, 0:NM]).then_inc(swa_pe, 1)
                if e == 4:
                    pe.wait_ge(swa_dve, 8)
                    pe.transpose(bank[5][:, 0:P], ssc[:, 0:P], ident[:])
                    pe.transpose(bank[6][0:NM, 0:P], ssc[:, P:P + NM], ident[:]).then_inc(swa_pe, 1)
                if e == 5:
                    pe.wait_ge(swa_act, 6)
                    pe.wait_ge(vwin_loaded, 16 * (1 + NS))
                    pe.wait_ge(vmeta_loaded, 16)
                    for b in range(NS):
                        for g in range(2):
                            cols = slice(b * NH + 8 * g, b * NH + 8 * g + 8)
                            pe.matmul(bank[2][:, cols], v_win[:, b, g * P:(g + 1) * P], pTs[:, cols], start=True, stop=False)
                            last = pe.matmul(bank[2][:, cols], v_meta_s[:, b, g * P:(g + 1) * P], pTs_meta[:, cols], start=False, stop=True)
                    last.then_inc(swa_pe, 1)
                if e == 6:
                    pe.wait_ge(swa_dve, 12)
                    pe.wait_ge(gadT_done, 1)
                    for h in range(GH):
                        last = pe.matmul(bank[2 + h][:, 0:TA], a_up[:, h * DK:(h + 1) * DK], gadT[:], start=True, stop=True)
                    last.then_inc(z_done, 1)
                if e == 7:
                    gla_turn(pe, None, 0)
                    gla_products(pe, None, 0)

            def gate_and_chunks(i):
                for b in range(2):
                    slab(GATE_A + 4 + i, b, KD, x, TR)
                    for q in range(2):
                        c = 4 * i + 2 * b + q
                        gla_turn(pe, c, c + 1)
                        gla_products(pe, c, c + 1)

            gate_and_chunks(0)
            with pe.Fori(1, 4) as i:
                gate_and_chunks(i)

            for j in range(8):
                last = pe.transpose(bank[4 + j // 4][0:NS, (j % 4) * P:(j % 4 + 1) * P], proj[:, GV + j, NP_:TR], ident[:])
            last.then_inc(nv_tr, 1)
            for i in range(4):
                for b in range(2):
                    u = 2 * i + b
                    slab(GLA_R + i, b, KD, x, TR)
                    pe.wait_ge(n_vmask, u + 1)
                    if u:
                        pe.wait_ge(n_state, 4 * u)
                    pe.matmul(bank[4][:], ones[0:NS, :], vmask[:, 0:512], start=True, stop=True)
                    pe.matmul(bank[5][:], ones[0:NS, :], vmask[:, 512:], start=True, stop=True).then_inc(n_vbc, 1)
                    pe.wait_ge(n_state, 4 * u + 4)
                    if u:
                        pe.wait_ge(n_oT, u)
                    else:
                        pe.wait_ge(g_oT, NCK)
                    for h in range(GH):
                        for q in range(2):
                            last = pe.matmul(bank[3][:, 2 * h + q:2 * h + q + 1], S0[:, b, h, q * P:(q + 1) * P],
                                             proj[:, GQ + h, NP_ + u:NP_ + u + 1], start=True, stop=True)
                    last.then_inc(n_o, 1)

            def branches(m):
                n = 2 * (MERGE + m) + 1
                pe.wait_ge(bank_free, n - 1)
                product(bank[1][:, 0:TR], 1, 0, 8, y, TR, n)
                product(bank[2][:, 0:TR], 1, 8, 16, y, TR, n).then_inc(slab_done, 1)

            slab(MERGE, 0, KD, x, TR)
            pe.wait_ge(n_oT, NS)
            for h in range(GH):
                pe.wait_ge(on_sq, h + 1)
                pe.matmul(bank[2 + h][:, 0:TR], ones[:], osq[:, 0], start=True, stop=False)
                pe.matmul(bank[2 + h][:, 0:TR], ones[:], osq[:, 1], start=False, stop=True).then_inc(on_sum, 1)
            pe.wait_ge(olo_done, 8)
            pe.wait_ge(solo_done, 16)
            branches(0)
            with pe.Fori(1, KD) as m:
                slab(MERGE + m, 0, KD, x, TR)
                branches(m)

            slab(W_OUT, 0, KD, x, TR, ready=lambda k: pe.wait_ge(mlo_done, k // 4 + 1))
            slab(W_OUT, 1, KD, x, TR)
            with pe.Fori(1, KD // 2) as i:
                for b in range(2):
                    slab(W_OUT + i, b, KD, x, TR)
            ffn(FFN2, FT, y, x, TR, 2)
            sum_squares(3, TR)


def _slabs(np_, w, kt):
    K, N = w.shape
    return np_.ascontiguousarray(w.reshape(kt, 128, N // 128, 128).transpose(2, 1, 0, 3)).reshape(N // 128, 128, kt * 128)


def _cols(np_, v):
    return np_.ascontiguousarray(v.reshape(-1, 128).T)


def kernel(**inputs):
    import numpy as _np
    import concourse.bacc as _bacc
    from concourse import mybir as _mybir
    from concourse.bass_utils import run_bass_kernel_spmd as _run

    x = {k: _np.asarray(v) for k, v in inputs.items()}
    cat, con = _np.concatenate, _np.ascontiguousarray
    a = {}
    tokens = cat([x["x_prompt"][0], x["x_sample"][:, 0], x["meta_tokens"]], 0)
    a["xT"] = con(tokens.T.reshape(KD, P, TA).transpose(1, 0, 2))
    for n in ("1", "2"):
        w = _slabs(_np, x[f"ffn{n}_w_in"][0], KD)
        a[f"w{n}_in"] = con(w.reshape(2, FT, P, ROW).transpose(1, 0, 2, 3))
        w = x[f"ffn{n}_w_out"][0].reshape(CH, FC, P, KD, P).transpose(0, 3, 2, 1, 4)
        a[f"w{n}_out"] = con(w).reshape(CH, KD // 2, 2, P, FC * P)
    w = x["w_in"][0]
    o_gla, o_r, o_ga, o_swa = 0, 2048, 3072, 3072 + RANK
    o_gate = o_swa + 1536
    order = [w[:, o_swa:o_gate], w[:, o_gla:o_r], w[:, o_gate:o_gate + D], w[:, o_r:o_ga]]
    a["w_proj"] = _slabs(_np, cat(order, 1), KD).reshape(26, 2, P, ROW)
    w_ga = w[:, o_ga:o_swa].reshape(KD, P, RANK).transpose(1, 0, 2).reshape(P, KD * RANK)
    a["w_ga"] = cat([w_ga, _np.zeros((P, GA_COLS - KD * RANK), w.dtype)], 1)
    gate_b = _slabs(_np, w[:, o_gate + D:], KD)
    both = _slabs(_np, cat([x["w_gla_o"][0], x["w_swa_o"][0]], 0), KD)
    a["w_merge"] = con(_np.stack([gate_b, both], 1))
    a["w_o"] = _slabs(_np, x["w_out"][0], KD).reshape(KD // 2, 2, P, ROW)
    norms = [x["ffn1_norm"][0], x["mix_norm"][0], x["ffn2_norm"][0], x["final_norm"]]
    a["gains"] = con(_np.stack([_cols(_np, v) for v in norms], 1))
    a["gbias"] = con(_cols(_np, x["gate_bias"][0]).reshape(P, 2, KD))
    a["onorm"] = _cols(_np, x["gla_out_norm"][0])
    a["a_up"] = con(x["gla_a_up"][0])
    a["a_bias"] = _cols(_np, x["gla_a_bias"][0])
    a["sinks"] = con(x["swa_sinks"])
    a["sink_bh"] = con(_np.tile(x["swa_sinks"][0], NS)[:, None])
    a["kT_cache"] = con(x["cache_win_k"][0].transpose(2, 3, 0, 1).reshape(2, P, NS, WIN).transpose(1, 2, 0, 3))
    a["kT_meta"] = con(x["cache_meta_k"][0].transpose(2, 3, 0, 1).reshape(2, P, NS, NM).transpose(1, 0, 2, 3))
    a["v_cache"] = con(x["cache_win_v"][0, :, 1:].reshape(NS, WIN - 1, 256).transpose(1, 0, 2))
    a["v_meta"] = con(x["cache_meta_v"][0].reshape(NS, NM, 256).transpose(1, 0, 2))
    a["state_in"] = con(x["state_gla"][0].transpose(0, 2, 1, 3))
    f = _np.float32
    slope = _np.exp2(-8.0 * _np.arange(1, NH + 1, dtype=f) / NH).astype(f)
    i, j = _np.arange(WIN)[:, None], _np.arange(2 * WIN)[None, :]
    dist = i + WIN - j
    dist = _np.where((dist >= 0) & (dist < WIN), dist, 1e36).astype(f)
    none = _np.zeros((P, NM), f)
    a["c_dist0"] = cat([dist[:, WIN:], none], 1)
    a["c_dist1"] = cat([dist, none], 1)
    a["c_nslope"] = con(_np.broadcast_to(-slope, (P, NH)))
    bias = -slope[:, None] * (WIN - 1 - _np.arange(WIN, dtype=f))[None, :]
    a["c_bias_s"] = cat([_np.tile(bias, (NS, 1)), none], 1).astype(f)
    a["c_ones"] = _np.ones((P, P), f)
    a["c_ident"] = _np.eye(P, dtype=f)
    a["c_onehot"] = con(_np.broadcast_to(_np.eye(CK, dtype=f), (P, CK, CK)))
    keep = _np.ones((P, TA), f)
    keep[:, 0:NP_:CK] = 0
    keep[:, NP_:M0 + 1] = 0
    a["c_scan"] = keep
    s, tt = _np.arange(CK)[:, None, None], _np.arange(CK)[None, None, :]
    a["c_causal"] = con(_np.broadcast_to((tt >= s).astype(f), (CK, GH, CK)))
    outs = {"yT": (P, KD, TR), "kvT": (P, 4, WIN + NM), "winkT": (P, NS, 2, WIN), "winv": (WIN, NS, 256),
            "state_p": (P, GH, DV), "state_s": (NS, P, GH, DV)}

    nc = _bacc.Bacc("TRN2", target_bir_lowering=False, num_devices=1)
    t = {n: nc.dram_tensor(f"in_{n}", v.shape, _mybir.dt.from_np(v.dtype), kind="ExternalInput").ap() for n, v in a.items()}
    t |= {n: nc.dram_tensor(f"out_{n}", s, _mybir.dt.float32, kind="ExternalOutput").ap() for n, s in outs.items()}
    build_layer(nc, t)
    r = _run(nc, [{f"in_{n}": v for n, v in a.items()}], core_ids=[0]).results[0]

    y = r["out_yT"].transpose(2, 1, 0).reshape(TR, D)
    kv = r["out_kvT"].transpose(2, 1, 0).reshape(WIN + NM, 2, 4, HD)
    wk = r["out_winkT"].transpose(1, 3, 2, 0).reshape(1, NS, WIN, 4, HD)
    wv = r["out_winv"].transpose(1, 0, 2).reshape(1, NS, WIN, 4, HD)
    return (con(y[:NP_])[None], con(y[NP_:])[:, None],
            con(kv[WIN:, 0])[None, None], con(kv[WIN:, 1])[None, None],
            con(kv[:WIN, 0])[None, None], con(kv[:WIN, 1])[None, None],
            con(r["out_state_p"].transpose(1, 0, 2))[None, None], con(wk), con(wv),
            con(r["out_state_s"].transpose(0, 2, 1, 3))[None])
```

```python
from contextlib import ExitStack

import numpy as np

import concourse.bass as bass
from concourse import mybir

ALU = mybir.AluOpType
ACT = mybir.ActivationFunctionType
AX = mybir.AxisListType
F32 = mybir.dt.float32
F32R = mybir.dt.float32r

P = 128
D = 2048
DFF = 5632
KD = D // P
FT = DFF // P
CH = 4
FC = FT // CH
NP_, NS, NM = 256, 8, 16
TR = NP_ + NS
TA = TR + NM
M0 = TR
GH, DK, DV, RANK = 4, 128, 256, 16
TAU = 16.0
CK = 16
NCK = NP_ // CK
NH, HD, WIN = 16, 64, 128
EPS = 1e-6
GA_COLS = (KD - 1) * RANK + P
ROW = 2048

FFN_PAIRS = CH * (FC + KD // 2)
SWA_IN = FFN_PAIRS
GLA_IN = SWA_IN + 6
GATE_A = GLA_IN + 8
GLA_R = GATE_A + 8
GATE_B = GLA_R + 4
MERGE1 = GATE_B + 6
MERGE2 = MERGE1 + 6
W_OUT = MERGE2 + 4
FFN2 = W_OUT + KD // 2
N_PAIRS = FFN2 + FFN_PAIRS

GQ, GK, GV, SQ, SK, SV, KDUP = 0, 4, 8, 16, 24, 26, 28


def build_layer(nc, t):
    ctx = ExitStack()
    with ctx:
        def sb(name, shape, dt=F32):
            return ctx.enter_context(nc.sbuf_tensor(name, shape, dt))

        def sem(name):
            return ctx.enter_context(nc.semaphore(name))

        x_hi = sb("x_hi", [P, KD, TA], F32R)
        x_lo = sb("x_lo", [P, KD, TA], F32R)
        y_hi = sb("y_hi", [P, KD * TR], F32R)
        y_lo = sb("y_lo", [P, KD * TR], F32R)
        w_hi = sb("w_hi", [P, 2, ROW], F32R)
        w_lo = sb("w_lo", [P, 2, ROW], F32R)
        small_r = sb("small_r", [P, 10 * P], F32R)
        ga_hi, ga_lo = small_r[:, 0:GA_COLS], small_r[:, GA_COLS:2 * GA_COLS]
        v_split, pick = small_r[0:32 + NS, 0:8 * P], small_r[0:32 + NS, 8 * P:].rearrange("p (a b) -> p a b", a=2)
        raw = sb("raw", [P, 2, ROW])
        hT = sb("hT", [P, KD, TA])
        proj = sb("proj", [P, 32, TA])
        rstd = sb("rstd", [P, TA])
        gadT = sb("gadT", [P, TA])
        y3_hi = y_hi[:].rearrange("p (k t) -> p k t", k=KD)
        y3_lo = y_lo[:].rearrange("p (k t) -> p k t", k=KD)
        s1_hi = y_hi[:, 0:FC * TA].rearrange("p (k t) -> p k t", k=FC)
        s1_lo = y_lo[:, 0:FC * TA].rearrange("p (k t) -> p k t", k=FC)

        ones = sb("ones", [P, P])
        ident = sb("ident", [P, P])
        onehot = sb("onehot", [P, CK, CK])
        gains = sb("gains", [P, 4, KD])
        gbias = sb("gbias", [P, 2, KD])
        onorm = sb("onorm", [P, 8])
        nslope = sb("nslope", [P, NH])
        sinks = sb("sinks", [P, NH])
        sink_bh = sb("sink_bh", [P, 1])
        causal = sb("causal", [CK, GH, CK])
        a_up = sb("a_up", [P, GH * DK])
        a_bias = sb("a_bias", [P, GH])
        eps = sb("eps", [P, 1])
        warm = sb("warm", [P, 1])
        pick_scale = sb("pick_scale", [P, NS])

        R = sb("scratch", [P, 6848])

        def at(o, *shape, parts=P):
            n = int(np.prod(shape))
            v = R[0:parts, o:o + n]
            if len(shape) == 2:
                v = v.rearrange("p (a b) -> p a b", a=shape[0])
            if len(shape) == 3:
                v = v.rearrange("p (a b c) -> p a b c", a=shape[0], b=shape[1])
            return v

        a_n, sig, act_a, b_n, s32 = (at(TA * i, TA) for i in range(5))
        acc, sq, std = (at(TA * i, TA) for i in range(5, 8))
        acc2, sq2 = act_a, b_n
        ga_raw = at(2240, GA_COLS)
        stat = at(256, 64)
        v_new = at(0, 256, parts=NS)
        pT_meta = at(512, 512, parts=NM)
        v_meta = at(2240, 256, parts=NM)
        dist0, dist1 = at(2500, 144), at(2644, 272)
        bias_s = at(336, 144)
        sc = at(3060, 2, 4, 272)
        pT = at(5236, 3, 512)
        v_tok = at(1408, 2, 256)
        kT_win = at(3232, NS, 2, WIN + 1)
        kT_meta = at(1024, 2, NS, NM)
        q_pad = at(1280, NS, NH)
        ssc = at(1408, 144)
        sT, sT_meta = at(1552, P), at(1680, P, parts=NM)
        k_new = at(320, 2, NS)
        pTs, pTs_meta = at(1808, P), at(1936, P, parts=NM)
        v_win = proj[:, SK:SK + NS, 0:256]
        v_meta_s = at(3232, NS, 256, parts=NM)
        oT = at(0, 8, TR)
        spl, mnz = at(5300, GH, TA), at(2112, GH, TA)
        bc = mnz
        scan_keep = at(512, TA)
        S = at(3232, GH, DV)
        Pd = at(4256, CK, GH, CK)
        k_tok = at(5280, 512, parts=CK)
        gv_tok = at(5792, 1024, parts=CK)
        a_smp = at(6816, GH, NS)
        kd, edl, eb, qd = (hT[:, GH * i:GH * i + GH, M0:TA] for i in range(4))
        vbuf, dl, attT = proj[:, 16:24, M0:TA], proj[:, 24:28, M0:TA], proj[0:CK, 28:32, M0:TA]
        S0 = R[:, 3136:3136 + 3 * GH * DV].rearrange("p (n h v) -> p n h v", n=3, h=GH)
        osq = [proj[:, 0:4, 0:TR], at(5184, 4, TR)]
        ostd, ors = at(2112, GH, TR), at(3168, GH, TR)
        ow, rsum = at(5184, 4, TR), proj[:, 0:4, 0:TR]
        gb_n, sigb, m1, m2 = (at(5184 + TR * i, TR) for i in range(4))
        r_act, r_sg = a_up[:, 0:TR], gadT[:, 0:TR]
        siga = proj[:, 16:32, 0:TR]
        merged = proj[:, 0:16, 0:TR]

        bank = [ctx.enter_context(nc.psum_tensor(f"bank{i}", [P, 512], F32)) for i in range(8)]

        raw_loaded = [sem("raw_loaded0"), sem("raw_loaded1")]
        hi_split, lo_split = sem("hi_split"), sem("lo_split")
        slab_done, bank_free = sem("slab_done"), sem("bank_free")
        gains_loaded = sem("gains_loaded")
        x_loaded = [sem(f"x_loaded{i}") for i in range(4)]
        consts_loaded, tables_loaded = sem("consts_loaded"), sem("tables_loaded")
        eps_set, acc_zero, sq_done, acc_done = sem("eps_set"), sem("acc_zero"), sem("sq_done"), sem("acc_done")
        sq2_done, acc2_done = sem("sq2_done"), sem("acc2_done")
        xhi_done, xlo_done = sem("xhi_done"), sem("xlo_done")
        sumsq_done, std_done, rstd_done = sem("sumsq_done"), sem("std_done"), sem("rstd_done")
        sig_done, acta_done, s_done, shi_done, slo_done = (
            sem(n) for n in ("sig_done", "acta_done", "s_done", "shi_done", "slo_done"))
        gahi_done, galo_done, gad_done, gadT_done = (
            sem(n) for n in ("gahi_done", "galo_done", "gad_done", "gadT_done"))
        kv_out, kdup_done, vtr_done, vtok_done = (sem(n) for n in ("kv_out", "kdup_done", "vtr_done", "vtok_done"))
        scores_done, sc_done, soft_step, exp_done = (
            sem(n) for n in ("scores_done", "sc_done", "soft_step", "exp_done"))
        p_ready, ptr_done, pT_done, so_done, sohi_done, solo_done = (
            sem(n) for n in ("p_ready", "ptr_done", "pT_done", "so_done", "sohi_done", "solo_done"))
        kwin_loaded, vwin_loaded, vmeta_loaded, knew_done, qpad_done = (
            sem(n) for n in ("kwin_loaded", "vwin_loaded", "vmeta_loaded", "knew_done", "qpad_done"))
        swa_pe, swa_act, swa_dve, win_out = (sem(n) for n in ("swa_pe", "swa_act", "swa_dve", "win_out"))
        scan_loaded, bias_loaded = sem("scan_loaded"), sem("bias_loaded")
        z_done, prep_act, prep_dve = sem("z_done"), sem("prep_act"), sem("prep_dve")
        (g_eb, g_dl, g_edl, g_kd, g_diff, g_exp, g_pk, g_P, g_att, g_attT, g_kt, g_vt, g_ktok, g_vtok,
         g_vbuf, g_qd, g_o, g_oT, g_kv, g_S) = (sem(n) for n in (
            "g_eb", "g_dl", "g_edl", "g_kd", "g_diff", "g_exp", "g_pk", "g_P", "g_att", "g_attT", "g_kt",
            "g_vt", "g_ktok", "g_vtok", "g_vbuf", "g_qd", "g_o", "g_oT", "g_kv", "g_S"))
        state_out, nv_tr, nv_zero, nv_hi, nv_lo = (
            sem(n) for n in ("state_out", "nv_tr", "nv_zero", "nv_hi", "nv_lo"))
        s0_loaded = [sem(f"s0_loaded{i}") for i in range(3)]
        s0_stored = [sem(f"s0_stored{i}") for i in range(3)]
        rhi_done, rlo_done, r_sum = sem("rhi_done"), sem("rlo_done"), sem("r_sum")
        n_pick, n_vbc, n_decay, n_state, n_o, n_oT = (
            sem(n) for n in ("n_pick", "n_vbc", "n_decay", "n_state", "n_o", "n_oT"))
        r_sig, siga_done = sem("r_sig"), sem("siga_done")
        r_done = sem("r_done")
        on_sq, on_sum, on_std, on_rs, on_w, on_g, ohi_done, olo_done = (
            sem(n) for n in ("on_sq", "on_sum", "on_std", "on_rs", "on_w", "on_g", "ohi_done", "olo_done"))
        sigb_done, m_step, merged_done, mhi_done, mlo_done = (
            sem(n) for n in ("sigb_done", "m_step", "merged_done", "mhi_done", "mlo_done"))
        y_done, y_out = sem("y_done"), sem("y_out")

        def decode_out(gp, jp, dst):
            d = dst[64 * jp:64 * jp + 64, 8:16, NP_:TR].rearrange("p (g a j) b -> p a b g j", g=2, a=2)[:, gp]
            s = bank[2][64 * gp:64 * gp + 64, 0:P].rearrange("p (b g a j e) -> p a e b g j", b=NS, g=2, a=2, j=2)[:, gp, jp]
            return d, s

        def chunk_cols(c):
            return slice(M0, TA) if c is None else (
                slice(c * CK, (c + 1) * CK) if isinstance(c, int) else bass.ds(c * CK, CK))

        def later(u, n=1):
            return not isinstance(u, int) or u > n

        def key_decay(act, u):
            act.wait_ge(g_dl, u + 1)
            act.activation(edl, dl, ACT.Exp, scale=1.0 / TAU).then_inc(g_edl, 1)

        def pair_decay(act, u):
            act.wait_ge(g_diff, 2 * u)
            act.activation(Pd, Pd, ACT.Exp, scale=1.0 / TAU).then_inc(g_exp, 1)

        def start_decay(act, cols, u):
            if later(u, 0):
                act.wait_ge(g_S, 4 * u)
            if later(u):
                act.wait_ge(g_qd, u - 1)
            act.activation(eb, bc[:, :, cols], ACT.Exp, scale=1.0 / TAU).then_inc(g_eb, 1)

        def to_tokens(act, u):
            act.wait_ge(g_vt, u + 1)
            if later(u, 0):
                act.wait_ge(g_kv, u)
            if later(u):
                act.wait_ge(g_o, u - 1)
            act.activation(gv_tok[:, 0:512], bank[4][0:CK, :], ACT.Copy).then_inc(g_vtok, 1)
            act.activation(gv_tok[:, 512:], bank[5][0:CK, :], ACT.Copy).then_inc(g_vtok, 1)
            act.wait_ge(g_kt, u + 1)
            act.activation(k_tok, bank[3][0:CK, :], ACT.Copy).then_inc(g_ktok, 1)

        def out_tile(act, c):
            act.wait_ge(g_o, c + 1)
            act.activation(oT[:, :, chunk_cols(c)], bank[2][:, P:2 * P].rearrange("p (a b) -> p a b", a=8),
                           ACT.Copy).then_inc(g_oT, 1)

        def end_col(c):
            if c is None:
                return slice(TA - 1, TA)
            return slice(c * CK + CK - 1, c * CK + CK) if isinstance(c, int) else bass.ds(c * CK + CK - 1, 1)

        def decay_to_end(dve, c, u):
            if later(u, 0):
                dve.wait_ge(g_kd, u)
            dve.tensor_tensor(dl, bc[:, :, end_col(c)].broadcast_to([P, GH, CK]), bc[:, :, chunk_cols(c)],
                              ALU.subtract).then_inc(g_dl, 1)

        def decayed_keys(dve, c, u):
            if later(u, 0):
                dve.wait_ge(g_kt, u)
            dve.wait_ge(g_edl, u + 1)
            dve.tensor_tensor(kd, proj[:, GK:GK + 4, chunk_cols(c)], edl, ALU.mult).then_inc(g_kd, 1)

        def by_s(a):
            return a.rearrange("p h s -> p s h").unsqueeze(3).broadcast_to([P, CK, GH, CK])

        def by_t(a):
            return a.unsqueeze(1).broadcast_to([P, CK, GH, CK])

        def pair_diffs(dve, c, u):
            b = bc[:, :, chunk_cols(c)]
            if later(u):
                dve.wait_ge(g_att, u - 1)
            dve.tensor_tensor(Pd, by_t(b), by_s(b), ALU.subtract).then_inc(g_diff, 1)
            dve.wait_ge(g_diff, 2 * u - 1)
            dve.tensor_scalar(Pd, Pd, 0.0, None, ALU.min).then_inc(g_diff, 1)

        def pair_products(dve, c, u):
            cols = chunk_cols(c)
            dve.wait_ge(g_exp, u)
            dve.tensor_tensor(Pd, Pd, by_s(proj[:, GK:GK + 4, cols]), ALU.mult).then_inc(g_pk, 1)
            dve.wait_ge(g_pk, u)
            dve.tensor_tensor(Pd, Pd, by_t(proj[:, GQ:GQ + 4, cols]), ALU.mult).then_inc(g_P, 1)

        def attention(dve, u):
            dve.wait_ge(g_att, u)
            dve.tensor_tensor(attT, bank[2][0:CK, 0:GH * CK].rearrange("p (h t) -> p h t", h=GH), causal[:],
                              ALU.mult).then_inc(g_attT, 1)

        def new_state(dve, u):
            dve.wait_ge(g_kv, u + 1)
            if later(u, 0):
                dve.wait_ge(g_o, u)
                dve.wait_ge(g_S, 4 * u)
                dve.wait_ge(g_eb, u + 1)
            for h in range(GH):
                kv = bank[6 + h // 2][:, (h % 2) * DV:(h % 2 + 1) * DV]
                if later(u, 0):
                    dve.scalar_tensor_tensor(S[:, h], S[:, h], eb[:, h, CK - 1:CK], kv, ALU.mult, ALU.add).then_inc(g_S, 1)
                else:
                    dve.tensor_copy(S[:, h], kv).then_inc(g_S, 1)

        def turn(pe, u):
            pe.wait_ge(g_vbuf, u + 1)
            if later(u, 0):
                pe.wait_ge(g_vtok, 2 * u)
            for j in range(8):
                last = pe.transpose(bank[4 + j // 4][0:CK, (j % 4) * P:(j % 4 + 1) * P], vbuf[:, j], ident[:])
            last.then_inc(g_vt, 1)
            pe.wait_ge(g_kd, u + 1)
            if later(u, 0):
                pe.wait_ge(g_ktok, u)
            for h in range(GH):
                last = pe.transpose(bank[3][0:CK, h * DK:(h + 1) * DK], kd[:, h], ident[:])
            last.then_inc(g_kt, 1)

        def attend(pe, u):
            pe.wait_ge(g_P, u)
            if later(u):
                pe.wait_ge(g_oT, u - 1)
            for s in range(CK):
                last = pe.matmul(bank[2][0:CK, 0:GH * CK], onehot[:, s], Pd[:, s].rearrange("p h t -> p (h t)"),
                                 start=(s == 0), stop=(s == CK - 1))
            last.then_inc(g_att, 1)

        def keys_by_values(pe, u, h):
            if h == 0:
                if later(u, 0):
                    pe.wait_ge(g_S, 4 * u)
                pe.wait_ge(g_ktok, u + 1)
                pe.wait_ge(g_vtok, 2 * u + 2)
            last = pe.matmul(bank[6 + h // 2][:, (h % 2) * DV:(h % 2 + 1) * DV], k_tok[:, h * DK:(h + 1) * DK],
                             gv_tok[:, h * DV:(h + 1) * DV], start=True, stop=True)
            if h == GH - 1:
                last.then_inc(g_kv, 1)

        def outputs(pe, u, n):
            if n == 0:
                pe.wait_ge(g_qd, u)
                pe.wait_ge(g_S, 4 * u)
                pe.wait_ge(g_attT, u)
            if n == 1:
                pe.wait_ge(g_vtok, 2 * u + 2)
            j, h, q = n // 2, n // 4, n // 2 % 2
            out = bank[2][:, P + j * CK:P + (j + 1) * CK]
            if n % 2 == 0:
                pe.matmul(out, S[:, h, q * P:(q + 1) * P], qd[:, h], start=True, stop=False)
            else:
                last = pe.matmul(out, gv_tok[:, j * P:(j + 1) * P], attT[:, h], start=False, stop=True)
                if n == 15:
                    last.then_inc(g_o, 1)

        block = ctx.enter_context(nc.Block())

        N_CONST = 12

        @block.sync
        def _(sp):
            def load_slab(src, half, b, kt, first=False):
                if not first:
                    sp.wait_ge(lo_split, 2 * half + b - 1)
                sp.dma_start(raw[:, b, 0:kt * P], src).then_inc(raw_loaded[b], 16)

            def load_pairs(w, half0, pairs, kt, i0=0):
                with sp.Fori(i0, pairs) as i:
                    for b in range(2):
                        load_slab(w[bass.ds(i, 1), b], half0 + i, b, kt)

            def load_tokens(q):
                sp.dma_start(hT[:, 4 * q:4 * q + 4, :], t["xT"][:, 4 * q:4 * q + 4, :]).then_inc(x_loaded[q], 16)

            sp.dma_start(gains[:], t["gains"]).then_inc(gains_loaded, 16)
            load_tokens(0)
            load_slab(t["w1_in"][0:1, 0], 0, 0, KD, first=True)
            for q in range(1, 4):
                load_tokens(q)
            load_slab(t["w1_in"][0:1, 1], 0, 1, KD, first=True)
            for dst, name in ((ones, "c_ones"), (ident, "c_ident"), (onehot, "c_onehot"), (gbias, "gbias"),
                              (onorm, "onorm"), (nslope, "c_nslope"),
                              (causal, "c_causal"), (a_up[0:RANK], "a_up"), (a_bias, "a_bias"), (sink_bh, "sink_bh"),
                              (pick_scale, "c_pick")):
                sp.dma_start(dst[:] if name != "a_up" else dst, t[name]).then_inc(consts_loaded, 16)
            sp.dma_start(sinks[:], t["sinks"].partition_broadcast(P)).then_inc(consts_loaded, 16)
            sp.dma_start(ga_raw, t["w_ga"]).then_inc(tables_loaded, 16)

            def ffn(w_in, w_out, half0, first=False):
                for c in range(CH):
                    h = half0 + c * (FC + KD // 2)
                    load_pairs(w_in[c * FC:(c + 1) * FC], h, FC, KD, i0=1 if first and c == 0 else 0)
                    load_pairs(w_out[c], h + FC, KD // 2, FC)

            ffn(t["w1_in"], t["w1_out"], 0, first=True)
            sp.dma_start(dist0, t["c_dist0"]).then_inc(tables_loaded, 16)
            sp.dma_start(dist1, t["c_dist1"]).then_inc(tables_loaded, 16)
            load_pairs(t["w_proj"][0:6], SWA_IN, 6, KD)
            load_pairs(t["w_proj"][6:14], GLA_IN, 8, KD)
            load_pairs(t["w_proj"][14:22], GATE_A, 8, KD)
            load_pairs(t["w_proj"][22:26], GLA_R, 4, KD)
            load_pairs(t["w_merge"], GATE_B, KD, KD)
            load_pairs(t["w_o"], W_OUT, KD // 2, KD)
            ffn(t["w2_in"], t["w2_out"], FFN2)
            for q in range(4):
                sp.wait_ge(y_done, 4 * q + 4)
                sp.dma_start(t["yT"][:, 4 * q:4 * q + 4, :], hT[:, 4 * q:4 * q + 4, 0:TR]).then_inc(y_out, 16)
            sp.wait_ge(y_out, 64)
            sp.wait_ge(kv_out, 32)
            sp.wait_ge(win_out, 32)
            sp.wait_ge(state_out, 16)
            for b in range(3):
                sp.wait_ge(s0_stored[b], 16 * len(range(b, NS, 3)))

        @block.gpsimd
        def _(pool):
            pool.memset(eps[:], EPS).then_inc(eps_set, 1)

            def zero_acc(r):
                if r:
                    pool.wait_ge(sumsq_done, r)
                pool.memset(acc, 0.0).then_inc(acc_zero, 1)
                pool.wait_ge(acc_zero, r + 1)

            def add_square(h, n_sq, T, tiles=1):
                pool.tensor_tensor(sq[:, 0:T], h, h, ALU.mult).then_inc(sq_done, 1)
                pool.wait_ge(sq_done, n_sq)
                pool.tensor_tensor(acc[:, 0:T], acc[:, 0:T], sq[:, 0:T], ALU.add).then_inc(acc_done, tiles)

            zero_acc(0)
            for m in range(0, KD, 2):
                pool.wait_ge(x_loaded[m // 4], 16)
                if m:
                    pool.wait_ge(acc_done, m)
                add_square(hT[:, m, :], m // 2 + 1, TA, tiles=2)

            def residual_squares(r, half0, T):
                pool.wait_ge(bank_free, 2 * half0)
                zero_acc(r)
                with pool.Fori(0, KD) as m:
                    pool.wait_ge(bank_free, 2 * half0 + m + 1)
                    pool.wait_ge(acc_done, KD * r + m)
                    add_square(hT[:, bass.ds(m, 1), 0:T], KD * r - KD // 2 + m + 1, T)

            residual_squares(1, SWA_IN - KD // 2, TA)

            pool.wait_ge(bank_free, 2 * GLA_IN)
            pool.dma_start(t["kvT"][:, :, 0:WIN], proj[:, SK:SK + 4, NP_ - WIN:NP_]).then_inc(kv_out, 16)
            pool.dma_start(t["kvT"][:, :, WIN:], proj[:, SK:SK + 4, M0:TA]).then_inc(kv_out, 16)
            pool.dma_start(bias_s, t["c_bias_s"]).then_inc(bias_loaded, 16)
            pool.memset(q_pad, 0.0).then_inc(qpad_done, 1)

            pool.wait_ge(kv_out, 32)
            pool.wait_ge(knew_done, 1)
            pool.wait_ge(ptr_done, 8)
            pool.dma_start(kT_meta, t["kT_meta"]).then_inc(kwin_loaded, 16)
            pool.wait_ge(so_done, 8)
            pool.dma_start(kT_win[:, :, :, 0:WIN], t["kT_cache"]).then_inc(kwin_loaded, 16)
            pool.dma_start(scan_keep, t["c_scan"]).then_inc(scan_loaded, 16)
            pool.dma_start(v_win[0:WIN - 1], t["v_cache"]).then_inc(vwin_loaded, 16)
            for b in range(NS):
                pool.dma_start(v_win[WIN - 1:WIN, b, :], v_new[b:b + 1, :]).then_inc(vwin_loaded, 16)
            pool.wait_ge(knew_done, 2)
            pool.dma_start(t["winkT"], kT_win[:, :, :, 1:WIN + 1]).then_inc(win_out, 16)
            pool.wait_ge(vwin_loaded, 16 * (1 + NS))
            pool.dma_start(t["winv"], v_win).then_inc(win_out, 16)
            pool.wait_ge(win_out, 32)
            pool.wait_ge(swa_pe, 1)
            pool.dma_start(v_meta_s, t["v_meta"]).then_inc(vmeta_loaded, 16)

            pool.wait_ge(prep_dve, 9)
            pool.tensor_copy(vbuf, proj[:, GV:GV + 8, M0:TA]).then_inc(g_vbuf, 1)

            def store_state(u):
                pool.wait_ge(n_state, 4 * (u + 1))
                pool.wait_ge(n_o, u + 1)
                pool.dma_start(t["state_s"][u], S0[:, u % 3]).then_inc(s0_stored[u % 3], 16)

            def values(c):
                pool.wait_ge(g_vt, c + 1)
                pool.tensor_copy(vbuf, proj[:, GV:GV + 8, chunk_cols(c)]).then_inc(g_vbuf, 1)

            def queries(c):
                pool.wait_ge(g_eb, c + 2)
                if later(c, 0):
                    pool.wait_ge(g_o, c)
                pool.tensor_tensor(qd, proj[:, GQ:GQ + 4, chunk_cols(c)], eb, ALU.mult).then_inc(g_qd, 1)

            values(0)
            values(1)
            queries(0)
            with pool.Fori(1, NCK - 1) as c:
                values(c + 1)
                queries(c)
            queries(NCK - 1)
            pool.wait_ge(g_S, 4 * (NCK + 1))
            pool.dma_start(t["state_p"], S).then_inc(state_out, 16)

            pool.wait_ge(state_out, 16)
            for u in range(NS):
                b = u % 3
                if u >= 3:
                    pool.wait_ge(s0_stored[b], 16 * (u // 3))
                pool.dma_start(S0[:, b], t["state_in"][u]).then_inc(s0_loaded[b], 16)
                if u >= 2:
                    store_state(u - 2)
            for u in range(NS - 2, NS):
                store_state(u)

            pool.wait_ge(on_std, GH)
            for j in range(8):
                if j >= 4:
                    pool.wait_ge(on_g, j - 3)
                pool.tensor_tensor(rsum[:, j % 4], y3_hi[:, j].bitcast(F32), y3_lo[:, j].bitcast(F32),
                                   ALU.add).then_inc(r_sum, 1)
                pool.wait_ge(r_sum, j + 1)
                pool.wait_ge(on_w, j + 1)
                pool.tensor_tensor(ow[:, j % 4], ow[:, j % 4], rsum[:, j % 4], ALU.mult).then_inc(on_g, 1)

            residual_squares(2, W_OUT, TR)
            residual_squares(3, N_PAIRS - KD // 2, TR)

        @block.scalar
        def _(act):
            def split_hi(half, b, kt, first=False):
                act.wait_ge(raw_loaded[b], 16 * (half + 1))
                if not first:
                    act.wait_ge(slab_done, 2 * half + b - 1)
                act.activation(w_hi[:, b, 0:kt * P], raw[:, b, 0:kt * P], ACT.Copy).then_inc(hi_split, 1)

            def tile_hi(r, m, x, T):
                act.activation(x[:, m, 0:T], hT[:, m, 0:T], ACT.Copy,
                               scale=gains[:, r, m]).then_inc(xhi_done, 1)

            def root(r, T):
                act.activation(warm[:], eps[:, 0:1], ACT.Sqrt)
                act.wait_ge(sumsq_done, r + 1)
                act.activation(std[:, 0:T], bank[7][:, 0:T], ACT.Sqrt, bias=eps[:, 0:1],
                               scale=1.0 / D).then_inc(std_done, 1)

            def ffn(half0, f0, s_hi, T, r_next=None, x_next=None, kt_after=KD):
                for c in range(CH):
                    h0 = half0 + c * (FC + KD // 2)

                    def inner(i, kt_next):
                        half, f = h0 + i, f0 + c * FC + i
                        split_hi(half + 1, 0, kt_next)
                        act.wait_ge(bank_free, 2 * half + 1)
                        act.activation(sig[:, 0:T], a_n[:, 0:T], ACT.Sigmoid).then_inc(sig_done, 1)
                        split_hi(half + 1, 1, kt_next)
                        act.wait_ge(s_done, f + 1)
                        act.activation(s_hi[:, bass.ds(i, 1), 0:T], s32[:, 0:T], ACT.Copy).then_inc(shi_done, 1)

                    with act.Fori(0, FC - 1) as i:
                        inner(i, KD)
                    inner(FC - 1, FC)
                    h1 = h0 + FC
                    last = c == CH - 1

                    def outer(i, kt_next, split=True):
                        for b in range(2):
                            if split:
                                split_hi(h1 + i + 1, b, kt_next)
                            if last and x_next is not None:
                                act.wait_ge(bank_free, 2 * (h1 + i) + b + 1)
                                tile_hi(r_next, bass.ds(2 * i + b, 1), x_next, T)

                    with act.Fori(0, KD // 2 - 1) as i:
                        outer(i, FC)
                    outer(KD // 2 - 1, kt_after, split=h1 + KD // 2 < N_PAIRS)

            act.wait_ge(gains_loaded, 16)
            for m in range(KD):
                act.wait_ge(x_loaded[m // 4], 16)
                tile_hi(0, slice(m, m + 1), x_hi, TA)
                if m == 3:
                    split_hi(0, 0, KD, first=True)
            split_hi(0, 1, KD, first=True)
            act.wait_ge(eps_set, 1)
            root(0, TA)
            act.wait_ge(consts_loaded, 16 * N_CONST)
            act.wait_ge(tables_loaded, 16)
            act.activation(ga_hi, ga_raw, ACT.Copy).then_inc(gahi_done, 1)
            ffn(0, 0, s1_hi, TA, 1, x_hi)

            root(1, TA)
            for i in range(6):
                for b in range(2):
                    split_hi(SWA_IN + i + 1, b, KD)
            act.wait_ge(bank_free, 2 * GLA_IN)
            for a in range(2):
                for b in range(2):
                    act.activation(proj[64 * b:64 * b + 64, KDUP + a:KDUP + 4:2, :],
                                   proj[64 * a:64 * a + 64, SK:SK + 2, :], ACT.Copy).then_inc(kdup_done, 1)

            def soft_exp(u):
                nk = 144 if u % 2 == 0 else 272
                act.wait_ge(soft_step, 4 * u + 4)
                for j in range(4):
                    act.activation(sc[:, u % 2, j, 0:nk], sc[:, u % 2, j, 0:nk], ACT.Exp,
                                   bias=stat[:, 8 + j:9 + j], accum_out=stat[:, 16 + j:17 + j]).then_inc(exp_done, 1)
                act.activation(stat[:, 20:24], stat[:, 12:16], ACT.Exp).then_inc(exp_done, 1)

            def move_pT(u):
                act.wait_ge(ptr_done, u + 1)
                if u:
                    act.wait_ge(so_done, u)
                act.activation(pT_meta, bank[5][0:NM, :], ACT.Copy).then_inc(pT_done, 1)
                act.activation(pT[:, 0], bank[6][:], ACT.Copy).then_inc(pT_done, 1)
                src = bank[7] if u % 2 else bank[6]
                act.activation(pT[:, 1 if u % 2 else 2], src[:], ACT.Copy).then_inc(pT_done, 1)

            def out_hi(u):
                g, q0 = u // 2, (u % 2) * WIN
                act.wait_ge(so_done, u + 1)
                for jp in range(2):
                    src = bank[6][0:HD, :].rearrange("p (j e q) -> p e j q", j=2, e=2)[:, jp]
                    act.activation(y3_hi[64 * jp:64 * jp + 64, 8 + 2 * g:10 + 2 * g, q0:q0 + WIN], src,
                                   ACT.Copy).then_inc(sohi_done, 1)

            for u in range(8):
                half = GLA_IN + u
                split_hi(half + 1, 0, KD)
                if u == 0:
                    act.wait_ge(vtr_done, 1)
                    act.activation(v_tok, bank[2][:].rearrange("p (a b) -> p a b", a=2), ACT.Copy).then_inc(vtok_done, 1)
                    act.activation(v_meta, bank[3][0:NM, 0:256], ACT.Copy).then_inc(vtok_done, 1)
                    act.activation(v_new, bank[4][0:NS, 0:256], ACT.Copy).then_inc(vtok_done, 1)
                if u:
                    move_pT(u - 1)
                soft_exp(u)
                split_hi(half + 1, 1, KD)
                if u:
                    out_hi(u - 1)

            act.activation(k_new, proj[:, SK:SK + 2, NP_:TR], ACT.Copy).then_inc(knew_done, 1)
            act.wait_ge(qpad_done, 1)
            for gp in range(2):
                for jp in range(2):
                    src = proj[64 * jp:64 * jp + 64, SQ:SQ + 8, NP_:TR].rearrange(
                        "p (g a j) b -> p a b g j", g=2, a=2)[:, gp]
                    dst = q_pad[64 * gp:64 * gp + 64].rearrange(
                        "p b (g a j e) -> p a e b g j", g=2, a=2, j=2)[:, gp, jp]
                    act.activation(dst, src, ACT.Copy).then_inc(qpad_done, 1)

            def gate_a(half, m):
                act.activation(siga[:, m], siga[:, m], ACT.Sigmoid, bias=gbias[:, 0, m]).then_inc(siga_done, 1)

            for e in range(8):
                half, b = GATE_A + e // 2, e % 2
                split_hi(half + 1, b, KD)
                if e == 0:
                    move_pT(7)
                if e == 1:
                    out_hi(7)
                if e == 3:
                    act.wait_ge(z_done, 1)
                    for h in range(GH):
                        act.activation(spl[:, h], bank[4 + h][:, 0:TA], ACT.Abs, bias=a_bias[:, h:h + 1]).then_inc(prep_act, 1)
                    act.wait_ge(prep_act, 4)
                    act.activation(spl, spl, ACT.Exp, scale=-1.0).then_inc(prep_act, 1)
                    act.wait_ge(prep_act, 5)
                    act.activation(spl, spl, ACT.Ln, bias=1.0).then_inc(prep_act, 1)
                if e == 7:
                    to_tokens(act, 0)
                act.wait_ge(bank_free, 2 * half + b + 1)
                gate_a(half, slice(e, e + 1))
                if e == 2:
                    act.wait_ge(kwin_loaded, 32)
                    act.wait_ge(knew_done, 1)
                    act.activation(kT_win[:, :, :, WIN].rearrange("p b g -> p g b"), k_new, ACT.Copy).then_inc(knew_done, 1)
                if e == 3:
                    act.wait_ge(swa_pe, 1)
                    act.activation(sT, bank[2][:, 0:P], ACT.Copy).then_inc(swa_act, 1)
                    act.activation(sT_meta, bank[3][0:NM, 0:P], ACT.Copy).then_inc(swa_act, 1)
                if e == 4:
                    act.wait_ge(swa_dve, 5)
                    act.activation(ssc, ssc, ACT.Exp, bias=stat[:, 3:4], accum_out=stat[:, 5:6]).then_inc(swa_act, 1)
                    act.activation(stat[:, 6:7], stat[:, 4:5], ACT.Exp).then_inc(swa_act, 1)
                if e == 5:
                    act.wait_ge(prep_dve, 9)
                    act.activation(a_smp, bc[:, :, NP_:TR], ACT.Exp, scale=1.0 / TAU).then_inc(prep_act, 1)
                    key_decay(act, 0)
                    start_decay(act, slice(M0, TA), 0)
                if e == 6:
                    act.wait_ge(swa_pe, 3)
                    act.activation(pTs, bank[3][:, 0:P], ACT.Copy).then_inc(swa_act, 1)
                    act.activation(pTs_meta, bank[3][0:NM, P:2 * P], ACT.Copy).then_inc(swa_act, 1)
                    key_decay(act, 1)

            act.wait_ge(swa_pe, 4)
            for gp in range(2):
                for jp in range(2):
                    dst, src = decode_out(gp, jp, y3_hi)
                    act.activation(dst, src, ACT.Copy).then_inc(swa_act, 1)
            pair_decay(act, 1)
            key_decay(act, 2)

            def is_in(u):
                return not isinstance(u, int) or u <= NCK

            def chunk(half, b, c, gate):
                to_tokens(act, c + 1)
                start_decay(act, chunk_cols(c), c + 1)
                split_hi(half + 1, b, KD)
                if is_in(c + 2):
                    pair_decay(act, c + 2)
                if is_in(c + 3):
                    key_decay(act, c + 3)
                gate(half, b, c)
                out_tile(act, c)

            def gate_a_slab(half, b, c):
                act.wait_ge(bank_free, 2 * half + b + 1)
                gate_a(half, slice(c + 8, c + 9) if isinstance(c, int) else bass.ds(c + 8, 1))

            def gate_r_slab(half, b, c):
                m = c - 8
                act.wait_ge(bank_free, 2 * half + b + 1)
                act.activation(r_sg, r_act, ACT.Sigmoid).then_inc(r_sig, 1)
                act.wait_ge(r_done, m + 1)
                act.activation(y3_hi[:, slice(m, m + 1) if isinstance(m, int) else bass.ds(m, 1)], r_act,
                               ACT.Copy).then_inc(rhi_done, 1)

            for b in range(2):
                chunk(GATE_A + 4, b, b, gate_a_slab)
            with act.Fori(1, 4) as i:
                for b in range(2):
                    chunk(GATE_A + 4 + i, b, 2 * i + b, gate_a_slab)
            with act.Fori(4, 7) as i:
                for b in range(2):
                    chunk(GATE_A + 4 + i, b, 2 * i + b, gate_r_slab)
            for b in range(2):
                chunk(GATE_A + 4 + 7, b, NCK - 2 + b, gate_r_slab)

            def gate_b(m):
                act.activation(merged[:, m], merged[:, m], ACT.Sigmoid, bias=gbias[:, 1, m:m + 1]).then_inc(sigb_done, 1)

            def pick_token(u):
                if u >= 2:
                    act.wait_ge(n_vbc, u - 1)
                act.activation(pick[:, u % 2], ones[0:32 + NS, :], ACT.Copy,
                               scale=pick_scale[0:32 + NS, u:u + 1]).then_inc(n_pick, 1)

            act.activation(v_split.rearrange("p (a b) -> p a b", a=8),
                           ones[0:32 + NS, :].unsqueeze(1).broadcast_to([32 + NS, 8, P]), ACT.Copy,
                           scale=0.0).then_inc(nv_zero, 1)
            act.wait_ge(nv_tr, 1)
            act.wait_ge(nv_zero, 1)
            for q in range(2):
                act.activation(v_split[0:NS, 512 * q:512 * q + 512], bank[4 + q][0:NS, :], ACT.Copy).then_inc(nv_hi, 1)
            pick_token(0)
            for u in range(NS):
                half, b = GATE_B + u // 2, u % 2
                act.wait_ge(s0_loaded[u % 3], 16 * (u // 3 + 1))
                for h in range(GH):
                    act.activation(S0[:, u % 3, h], S0[:, u % 3, h], ACT.Copy, scale=a_smp[:, h, u:u + 1]).then_inc(n_decay, 1)
                if u + 1 < NS:
                    pick_token(u + 1)
                if u:
                    act.wait_ge(n_o, u)
                    act.activation(oT[:, :, NP_ + u - 1], bank[3][:, 0:8], ACT.Copy).then_inc(n_oT, 1)
                split_hi(half + 1, b, KD)
                act.wait_ge(bank_free, 2 * half + b + 1)
                gate_b(8 + u)
            act.wait_ge(n_o, NS)
            act.activation(oT[:, :, NP_ + NS - 1], bank[3][:, 0:8], ACT.Copy).then_inc(n_oT, 1)

            act.wait_ge(n_oT, NS)
            act.wait_ge(g_oT, NCK)
            act.wait_ge(s0_stored[2], 16 * 2)
            for h in range(GH):
                act.activation(osq[h // 2][:, h % 2 * 2:h % 2 * 2 + 2], oT[:, 2 * h:2 * h + 2, :], ACT.Square).then_inc(on_sq, 1)
            for h in range(GH):
                half, b = GATE_B + 4 + h // 2, h % 2
                split_hi(half + 1, b, KD)
                if h == 0:
                    act.wait_ge(s0_stored[0], 16 * 3)
                    for g in range(GH):
                        act.wait_ge(on_sum, g + 1)
                        act.activation(ostd[:, g], bank[2 + g][:, 0:TR], ACT.Sqrt, bias=eps[:, 0:1],
                                       scale=1.0 / DV).then_inc(on_std, 1)
                if h:
                    for q in range(2 * h - 2, 2 * h):
                        act.wait_ge(on_g, q + 1)
                        act.activation(y3_hi[:, q], ow[:, q % 4], ACT.Copy).then_inc(ohi_done, 1)
                act.wait_ge(bank_free, 2 * half + b + 1)
                gate_b(4 + h)
            for q in range(2 * GH - 2, 2 * GH):
                act.wait_ge(on_g, q + 1)
                act.activation(y3_hi[:, q], ow[:, q % 4], ACT.Copy).then_inc(ohi_done, 1)

            with act.Fori(0, 6) as i:
                for b in range(2):
                    split_hi(MERGE1 + i + 1, b, KD)

            def merged_hi(q):
                act.wait_ge(merged_done, 4 * q if q else KD)
                act.activation(x_hi[:, 4 * q:4 * q + 4, 0:TR], merged[:, 4 * q:4 * q + 4, :], ACT.Copy).then_inc(mhi_done, 1)

            for i in range(4):
                half = MERGE2 + i
                split_hi(half + 1, 0, KD)
                act.wait_ge(bank_free, 2 * half + 1)
                act.activation(sigb, gb_n, ACT.Sigmoid, bias=gbias[:, 1, i:i + 1]).then_inc(sigb_done, 1)
                if i == 3:
                    for q in range(1, 4):
                        merged_hi(q)
                split_hi(half + 1, 1, KD)
            merged_hi(0)

            def w_out(i):
                for b in range(2):
                    split_hi(W_OUT + i + 1, b, KD)
                    act.wait_ge(bank_free, 2 * (W_OUT + i) + b + 1)
                    tile_hi(2, bass.ds(2 * i + b, 1), y3_hi, TR)

            with act.Fori(0, KD // 2) as i:
                w_out(i)
            root(2, TR)
            ffn(FFN2, FT, x_hi, TR)
            root(3, TR)

        @block.vector
        def _(dve):
            def split_lo(half, b, kt):
                dve.wait_ge(hi_split, 2 * half + b + 1)
                dve.tensor_tensor(w_lo[:, b, 0:kt * P], raw[:, b, 0:kt * P], w_hi[:, b, 0:kt * P].bitcast(F32),
                                  ALU.subtract).then_inc(lo_split, 1)

            def tile_lo(r, m, x, T, n):
                dve.wait_ge(xhi_done, n)
                dve.scalar_tensor_tensor(x[1][:, m, 0:T], hT[:, m, 0:T], gains[:, r, m],
                                         x[0][:, m, 0:T].bitcast(F32), ALU.mult, ALU.subtract).then_inc(xlo_done, 1)

            def inverse(r, T):
                dve.wait_ge(std_done, r + 1)
                dve.reciprocal(rstd[:, 0:T], std[:, 0:T]).then_inc(rstd_done, 1)
                dve.wait_ge(rstd_done, r + 1)

            def ffn(half0, f0, s_hi, s_lo, T, r_next=None, x_next=None, kt_after=KD):
                for c in range(CH):
                    h0 = half0 + c * (FC + KD // 2)

                    def inner(i, kt_next):
                        half, f = h0 + i, f0 + c * FC + i
                        dve.wait_ge(slab_done, 2 * half + 1)
                        dve.tensor_tensor(a_n[:, 0:T], bank[0][:, 0:T], rstd[:, 0:T], ALU.mult).then_inc(bank_free, 1)
                        split_lo(half + 1, 0, kt_next)
                        dve.wait_ge(sig_done, f + 1)
                        dve.tensor_tensor(act_a[:, 0:T], a_n[:, 0:T], sig[:, 0:T], ALU.mult).then_inc(acta_done, 1)
                        dve.wait_ge(slab_done, 2 * half + 2)
                        dve.tensor_tensor(b_n[:, 0:T], bank[1][:, 0:T], rstd[:, 0:T], ALU.mult).then_inc(bank_free, 1)
                        dve.wait_ge(bank_free, 2 * half + 2)
                        dve.wait_ge(acta_done, f + 1)
                        dve.tensor_tensor(s32[:, 0:T], act_a[:, 0:T], b_n[:, 0:T], ALU.mult).then_inc(s_done, 1)
                        split_lo(half + 1, 1, kt_next)
                        dve.wait_ge(shi_done, f + 1)
                        dve.tensor_tensor(s_lo[:, bass.ds(i, 1), 0:T], s32[:, 0:T],
                                          s_hi[:, bass.ds(i, 1), 0:T].bitcast(F32), ALU.subtract).then_inc(slo_done, 1)

                    with dve.Fori(0, FC - 1) as i:
                        inner(i, KD)
                    inner(FC - 1, FC)
                    h1 = h0 + FC
                    last = c == CH - 1

                    def outer(i, kt_next, split=True):
                        for b in range(2):
                            n, m = 2 * (h1 + i) + b, bass.ds(2 * i + b, 1)
                            dve.wait_ge(slab_done, n + 1)
                            dve.scalar_tensor_tensor(hT[:, m, 0:T], bank[b][:, 0:T], 0.5, hT[:, m, 0:T],
                                                     ALU.mult, ALU.add).then_inc(bank_free, 1)
                            if split:
                                split_lo(h1 + i + 1, b, kt_next)
                            if last and x_next is not None:
                                tile_lo(r_next, m, x_next, T, KD * r_next + 2 * i + b + 1)

                    with dve.Fori(0, KD // 2 - 1) as i:
                        outer(i, FC)
                    outer(KD // 2 - 1, kt_after, split=h1 + KD // 2 < N_PAIRS)

            dve.wait_ge(gains_loaded, 16)
            for m in range(KD):
                tile_lo(0, slice(m, m + 1), (x_hi, x_lo), TA, m + 1)
                if m == 3:
                    split_lo(0, 0, KD)
                if m % 2:
                    if m > 1:
                        dve.wait_ge(acc2_done, m // 2)
                    dve.tensor_tensor(sq2 if m > 1 else acc2, hT[:, m], hT[:, m], ALU.mult).then_inc(
                        sq2_done if m > 1 else acc2_done, 1)
                    if m > 1:
                        dve.wait_ge(sq2_done, m // 2)
                        dve.tensor_tensor(acc2, acc2, sq2, ALU.add).then_inc(acc2_done, 1)
            split_lo(0, 1, KD)
            inverse(0, TA)
            dve.wait_ge(consts_loaded, 16 * N_CONST)
            dve.wait_ge(gahi_done, 1)
            dve.tensor_tensor(ga_lo, ga_raw, ga_hi.bitcast(F32), ALU.subtract).then_inc(galo_done, 1)
            ffn(0, 0, s1_hi, s1_lo, TA, 1, (x_hi, x_lo))
            inverse(1, TA)

            def project(half, b, dst, scale, T):
                dve.wait_ge(slab_done, 2 * half + b + 1)
                dve.scalar_tensor_tensor(dst, bank[b][:, 0:T], scale, rstd[:, 0:T], ALU.mult, ALU.mult).then_inc(bank_free, 1)
                split_lo(half + 1, b, KD)

            for i in range(6):
                for b in range(2):
                    T, scale = (TR, HD ** -0.5) if i < 4 else (TA, 1.0)
                    project(SWA_IN + i, b, proj[:, SQ + 2 * i + b, 0:T], scale, T)
                    if i == 0 and b == 0:
                        dve.wait_ge(gad_done, 1)
                        dve.tensor_tensor(gadT[0:RANK], bank[6][0:RANK, 0:TA], rstd[0:RANK, :], ALU.mult).then_inc(gadT_done, 1)

            def soft_max(u):
                g, blk = u // 2, u % 2
                nk, dist = (272, dist1) if blk else (144, dist0)
                dve.wait_ge(scores_done, u + 1)
                for j in range(4):
                    h = 4 * g + j
                    dve.scalar_tensor_tensor(sc[:, u % 2, j, 0:nk], dist, nslope[:, h:h + 1], bank[2 + j][:, 0:nk],
                                             ALU.mult, ALU.add).then_inc(sc_done, 1)
                dve.wait_ge(sc_done, 4 * u + 4)
                dve.tensor_reduce(stat[:, 0:4], sc[:, u % 2, :, 0:nk], AX.X, ALU.max).then_inc(soft_step, 1)
                dve.wait_ge(soft_step, 4 * u + 1)
                dve.tensor_tensor(stat[:, 4:8], stat[:, 0:4], sinks[:, 4 * g:4 * g + 4], ALU.max).then_inc(soft_step, 1)
                dve.wait_ge(soft_step, 4 * u + 2)
                dve.tensor_scalar(stat[:, 8:12], stat[:, 4:8], -1.0, None, ALU.mult).then_inc(soft_step, 1)
                dve.tensor_tensor(stat[:, 12:16], sinks[:, 4 * g:4 * g + 4], stat[:, 4:8], ALU.subtract).then_inc(soft_step, 1)

            def soft_norm(u):
                nk = 272 if u % 2 else 144
                dve.wait_ge(exp_done, 5 * u + 5)
                dve.tensor_tensor(stat[:, 24:28], stat[:, 16:20], stat[:, 20:24], ALU.add).then_inc(p_ready, 1)
                dve.wait_ge(p_ready, 6 * u + 1)
                dve.reciprocal(stat[:, 28:32], stat[:, 24:28]).then_inc(p_ready, 1)
                dve.wait_ge(p_ready, 6 * u + 2)
                for j in range(4):
                    dve.tensor_scalar(sc[:, u % 2, j, 0:nk], sc[:, u % 2, j, 0:nk], stat[:, 28 + j:29 + j], None,
                                      ALU.mult).then_inc(p_ready, 1)

            def out_lo(u):
                g, q0 = u // 2, (u % 2) * WIN
                dve.wait_ge(sohi_done, 2 * u + 2)
                for jp in range(2):
                    src = bank[6][0:HD, :].rearrange("p (j e q) -> p e j q", j=2, e=2)[:, jp]
                    rows, tiles = slice(64 * jp, 64 * jp + 64), slice(8 + 2 * g, 10 + 2 * g)
                    dve.tensor_tensor(y3_lo[rows, tiles, q0:q0 + WIN], src,
                                      y3_hi[rows, tiles, q0:q0 + WIN].bitcast(F32), ALU.subtract).then_inc(solo_done, 1)

            dve.wait_ge(tables_loaded, 16 * 3)
            for u in range(8):
                T, scale = (TR, DK ** -0.5) if u < 2 else (TA, 1.0)
                project(GLA_IN + u, 0, proj[:, 2 * u, 0:T], scale, T)
                soft_max(u)
                project(GLA_IN + u, 1, proj[:, 2 * u + 1, 0:T], scale, T)
                if u:
                    out_lo(u - 1)
                soft_norm(u)

            def gate_a(half, b, m):
                dve.wait_ge(slab_done, 2 * half + b + 1)
                dve.tensor_tensor(siga[:, m], bank[b][:, 0:TR], rstd[:, 0:TR], ALU.mult).then_inc(bank_free, 1)
                split_lo(half + 1, b, KD)

            dve.wait_ge(kv_out, 32)
            dve.wait_ge(qpad_done, 5)
            dve.wait_ge(knew_done, 1)
            for e in range(8):
                half, b = GATE_A + e // 2, e % 2
                gate_a(half, b, slice(e, e + 1))
                if e == 1:
                    out_lo(7)
                if e == 3:
                    dve.wait_ge(prep_act, 4)
                    for h in range(GH):
                        dve.tensor_scalar(mnz[:, h], bank[4 + h][:, 0:TA], a_bias[:, h:h + 1], 0.0,
                                          ALU.add, ALU.min).then_inc(prep_dve, 1)
                if e == 4:
                    dve.wait_ge(bias_loaded, 16)
                    dve.wait_ge(swa_pe, 2)
                    dve.tensor_tensor(ssc, bank[4][:, 0:144], bias_s, ALU.add).then_inc(swa_dve, 1)
                    dve.wait_ge(swa_dve, 1)
                    dve.tensor_reduce(stat[:, 0:1], ssc, AX.X, ALU.max).then_inc(swa_dve, 1)
                    dve.wait_ge(swa_dve, 2)
                    dve.tensor_tensor(stat[:, 2:3], stat[:, 0:1], sink_bh[:], ALU.max).then_inc(swa_dve, 1)
                    dve.wait_ge(swa_dve, 3)
                    dve.tensor_scalar(stat[:, 3:4], stat[:, 2:3], -1.0, None, ALU.mult).then_inc(swa_dve, 1)
                    dve.tensor_tensor(stat[:, 4:5], sink_bh[:], stat[:, 2:3], ALU.subtract).then_inc(swa_dve, 1)
                if e == 5:
                    dve.wait_ge(swa_act, 4)
                    dve.tensor_tensor(stat[:, 7:8], stat[:, 5:6], stat[:, 6:7], ALU.add).then_inc(swa_dve, 1)
                    dve.wait_ge(swa_dve, 6)
                    dve.reciprocal(stat[:, 8:9], stat[:, 7:8]).then_inc(swa_dve, 1)
                    dve.wait_ge(swa_dve, 7)
                    dve.tensor_scalar(ssc, ssc, stat[:, 8:9], None, ALU.mult).then_inc(swa_dve, 1)
                    dve.wait_ge(prep_dve, 4)
                    dve.wait_ge(prep_act, 6)
                    dve.tensor_tensor(spl, mnz, spl, ALU.subtract).then_inc(prep_dve, 1)
                    dve.wait_ge(prep_dve, 5)
                    dve.wait_ge(scan_loaded, 16)
                    for h in range(GH):
                        dve.tensor_tensor_scan(bc[:, h], scan_keep, spl[:, h], 0.0, ALU.mult,
                                               ALU.add).then_inc(prep_dve, 1)
                    dve.wait_ge(prep_dve, 9)
                    decay_to_end(dve, None, 0)
                if e == 6:
                    dve.wait_ge(win_out, 32)
                    decayed_keys(dve, None, 0)
                    decay_to_end(dve, 0, 1)
            decayed_keys(dve, 0, 1)
            dve.wait_ge(swa_pe, 4)
            pair_diffs(dve, 0, 1)
            dve.wait_ge(swa_act, 10)
            for gp in range(2):
                for jp in range(2):
                    hi, src = decode_out(gp, jp, y3_hi)
                    lo, _ = decode_out(gp, jp, y3_lo)
                    dve.tensor_tensor(lo, src, hi.bitcast(F32), ALU.subtract).then_inc(swa_dve, 1)
            new_state(dve, 0)
            pair_products(dve, 0, 1)
            decay_to_end(dve, 1, 2)
            decayed_keys(dve, 1, 2)

            def is_in(u):
                return not isinstance(u, int) or u <= NCK

            def tile(m):
                return slice(m, m + 1) if isinstance(m, int) else bass.ds(m, 1)

            def chunk(half, b, c, gate):
                dve.wait_ge(slab_done, 2 * half + b + 1)
                dve.tensor_tensor(siga[:, tile(c + 8)] if gate is None else r_act, bank[b][:, 0:TR], rstd[:, 0:TR],
                                  ALU.mult).then_inc(bank_free, 1)
                if later(c, 0):
                    new_state(dve, c)
                attention(dve, c + 1)
                if is_in(c + 2):
                    pair_diffs(dve, c + 1, c + 2)
                split_lo(half + 1, b, KD)
                if is_in(c + 3):
                    decay_to_end(dve, c + 2, c + 3)
                if is_in(c + 2):
                    pair_products(dve, c + 1, c + 2)
                if is_in(c + 3):
                    decayed_keys(dve, c + 2, c + 3)
                if gate is not None:
                    gate(c - 8)

            def silu_r(m):
                dve.wait_ge(r_sig, m + 1)
                dve.tensor_tensor(r_act, r_act, r_sg, ALU.mult).then_inc(r_done, 1)
                dve.wait_ge(rhi_done, m + 1)
                dve.tensor_tensor(y3_lo[:, tile(m)], r_act, y3_hi[:, tile(m)].bitcast(F32), ALU.subtract).then_inc(rlo_done, 1)
                dve.wait_ge(rlo_done, m + 1)

            for b in range(2):
                chunk(GATE_A + 4, b, b, None)
            with dve.Fori(1, 4) as i:
                for b in range(2):
                    chunk(GATE_A + 4 + i, b, 2 * i + b, None)
            with dve.Fori(4, 7) as i:
                for b in range(2):
                    chunk(GATE_A + 4 + i, b, 2 * i + b, silu_r)
            for b in range(2):
                chunk(GATE_A + 4 + 7, b, NCK - 2 + b, silu_r)
            new_state(dve, NCK)

            dve.wait_ge(nv_tr, 1)
            for q in range(2):
                dve.wait_ge(nv_hi, 2)
                dve.tensor_tensor(v_split[32:32 + NS, 512 * q:512 * q + 512], bank[4 + q][0:NS, :],
                                  v_split[0:NS, 512 * q:512 * q + 512].bitcast(F32), ALU.subtract).then_inc(nv_lo, 1)
            dve.wait_ge(g_vbuf, NCK + 1)
            for u in range(NS):
                half, b = GATE_B + u // 2, u % 2
                dve.wait_ge(n_vbc, u + 1)
                for h in range(GH):
                    dve.wait_ge(n_decay, 4 * u + h + 1)
                    dve.scalar_tensor_tensor(S0[:, u % 3, h], bank[4 + h // 2][:, (h % 2) * DV:(h % 2 + 1) * DV],
                                             proj[:, GK + h, NP_ + u:NP_ + u + 1], S0[:, u % 3, h],
                                             ALU.mult, ALU.add).then_inc(n_state, 1)
                dve.wait_ge(slab_done, 2 * half + b + 1)
                dve.tensor_tensor(merged[:, 8 + u], bank[b][:, 0:TR], rstd[:, 0:TR], ALU.mult).then_inc(bank_free, 1)
                split_lo(half + 1, b, KD)

            def gated_norm(h):
                dve.wait_ge(on_rs, h + 1)
                for q in range(2):
                    j = 2 * h + q
                    if j >= 4:
                        dve.wait_ge(olo_done, j - 3)
                    dve.scalar_tensor_tensor(ow[:, j % 4], oT[:, j], onorm[:, j:j + 1], ors[:, h], ALU.mult,
                                             ALU.mult).then_inc(on_w, 1)

            def branch_lo(h):
                for j in range(2 * h, 2 * h + 2):
                    dve.wait_ge(ohi_done, j + 1)
                    dve.tensor_tensor(y3_lo[:, j], ow[:, j % 4], y3_hi[:, j].bitcast(F32), ALU.subtract).then_inc(olo_done, 1)

            dve.wait_ge(rlo_done, 8)
            for h in range(GH):
                half, b = GATE_B + 4 + h // 2, h % 2
                if h == 0:
                    dve.wait_ge(n_o, NS)
                if h == 1:
                    dve.wait_ge(s0_stored[0], 16 * 3)
                    dve.wait_ge(s0_stored[1], 16 * 3)
                    for g in range(GH):
                        dve.wait_ge(on_std, g + 1)
                        dve.reciprocal(ors[:, g], ostd[:, g]).then_inc(on_rs, 1)
                if h:
                    gated_norm(h - 1)
                dve.wait_ge(slab_done, 2 * half + b + 1)
                dve.tensor_tensor(merged[:, 4 + h], bank[b][:, 0:TR], rstd[:, 0:TR], ALU.mult).then_inc(bank_free, 1)
                split_lo(half + 1, b, KD)
                if h:
                    branch_lo(h - 1)
            gated_norm(GH - 1)
            branch_lo(GH - 1)

            dve.wait_ge(siga_done, KD)
            dve.wait_ge(sigb_done, 12)

            with dve.Fori(0, 6) as i:
                for b in range(2):
                    n, half = 2 * i + b, MERGE1 + i
                    dve.wait_ge(slab_done, 2 * half + b + 1)
                    dve.tensor_tensor(m1, siga[:, bass.ds(n + 4, 1)], bank[b][:, 0:TR], ALU.mult).then_inc(m_step, 1)
                    dve.tensor_tensor(m2, merged[:, bass.ds(n + 4, 1)], bank[2 + b][:, 0:TR], ALU.mult).then_inc(bank_free, 1)
                    dve.wait_ge(m_step, n + 1)
                    dve.wait_ge(bank_free, 2 * half + b + 1)
                    dve.tensor_tensor(merged[:, bass.ds(n + 4, 1)], m1, m2, ALU.add).then_inc(merged_done, 1)
                    split_lo(half + 1, b, KD)
                    dve.wait_ge(merged_done, n + 1)

            def merged_lo(q):
                dve.wait_ge(mhi_done, q if q else 4)
                dve.tensor_tensor(x_lo[:, 4 * q:4 * q + 4, 0:TR], merged[:, 4 * q:4 * q + 4, :],
                                  x_hi[:, 4 * q:4 * q + 4, 0:TR].bitcast(F32), ALU.subtract).then_inc(mlo_done, 1)

            for i in range(4):
                half = MERGE2 + i
                dve.wait_ge(slab_done, 2 * half + 1)
                dve.tensor_tensor(gb_n, bank[0][:, 0:TR], rstd[:, 0:TR], ALU.mult).then_inc(bank_free, 1)
                split_lo(half + 1, 0, KD)
                if i == 3:
                    for q in range(1, 4):
                        merged_lo(q)
                dve.wait_ge(slab_done, 2 * half + 2)
                dve.tensor_tensor(m1, siga[:, i], bank[1][:, 0:TR], ALU.mult).then_inc(m_step, 1)
                dve.wait_ge(sigb_done, 13 + i)
                dve.tensor_tensor(m2, sigb, bank[3][:, 0:TR], ALU.mult).then_inc(bank_free, 1)
                dve.wait_ge(m_step, 13 + i)
                dve.wait_ge(bank_free, 2 * half + 2)
                dve.tensor_tensor(merged[:, i], m1, m2, ALU.add).then_inc(merged_done, 1)
                if i == 3:
                    merged_lo(0)
                split_lo(half + 1, 1, KD)
                dve.wait_ge(merged_done, 13 + i)

            with dve.Fori(0, KD // 2) as i:
                for b in range(2):
                    m = bass.ds(2 * i + b, 1)
                    dve.wait_ge(slab_done, 2 * (W_OUT + i) + b + 1)
                    dve.tensor_tensor(hT[:, m, 0:TR], bank[b][:, 0:TR], hT[:, m, 0:TR], ALU.add).then_inc(bank_free, 1)
                    split_lo(W_OUT + i + 1, b, KD)
                    tile_lo(2, m, (y3_hi, y3_lo), TR, 2 * KD + 2 * i + b + 1)
            inverse(2, TR)
            ffn(FFN2, FT, x_hi, x_lo, TR)
            inverse(3, TR)
            for m in range(KD):
                dve.scalar_tensor_tensor(hT[:, m, 0:TR], hT[:, m, 0:TR], gains[:, 3, m:m + 1], rstd[:, 0:TR],
                                         ALU.mult, ALU.mult).then_inc(y_done, 1)

        @block.tensor
        def _(pe):
            def product(out, b, ks, x, T, n, ready=None, beside=None):
                pe.wait_ge(hi_split, n + 1)
                for k in ks:
                    if ready is not None:
                        ready(k)
                    w = w_hi[:, b, k * P:(k + 1) * P]
                    pe.matmul(out, w, x[0][:, k, 0:T], start=(k == ks[0]), stop=False)
                    pe.matmul(out, w, x[1][:, k, 0:T], start=False, stop=False)
                    if beside is not None:
                        beside(k)
                pe.wait_ge(lo_split, n + 1)
                for k in ks:
                    last = pe.matmul(out, w_lo[:, b, k * P:(k + 1) * P], x[0][:, k, 0:T], start=False, stop=(k == ks[-1]))
                    if beside is not None and k != ks[-1]:
                        beside(len(ks) + k)
                return last

            def slab(half, b, kt, x, T, ready=None, first=False, beside=None):
                if not first:
                    pe.wait_ge(bank_free, 2 * half + b - 1)
                product(bank[b][:, 0:T], b, range(kt), x, T, 2 * half + b, ready, beside).then_inc(slab_done, 1)

            def sum_squares(r, T):
                pe.wait_ge(acc_done, KD * (r + 1))
                if r == 0:
                    pe.wait_ge(consts_loaded, 16 * N_CONST)
                    pe.wait_ge(acc2_done, KD // 2)
                    pe.matmul(bank[7][:, 0:T], ones[:], acc2[:, 0:T], start=True, stop=False)
                pe.matmul(bank[7][:, 0:T], ones[:], acc[:, 0:T], start=(r > 0), stop=True).then_inc(sumsq_done, 1)

            def tiles_of_norm(r):
                def ready(k):
                    pe.wait_ge(xlo_done, KD * r + k + 1)
                return ready

            def ffn(half0, f0, x, s, T, r):
                for c in range(CH):
                    h0 = half0 + c * (FC + KD // 2)
                    i0 = 0
                    if c == 0:
                        slab(h0, 0, KD, x, T, ready=tiles_of_norm(r), first=half0 == 0)
                        sum_squares(r, T)
                        slab(h0, 1, KD, x, T, first=half0 == 0)
                        i0 = 1
                    with pe.Fori(i0, FC) as i:
                        for b in range(2):
                            slab(h0 + i, b, KD, x, T)
                    h1 = h0 + FC
                    slab(h1, 0, FC, s, T, ready=lambda k: pe.wait_ge(slo_done, f0 + c * FC + k + 1))
                    slab(h1, 1, FC, s, T)
                    with pe.Fori(1, KD // 2) as i:
                        for b in range(2):
                            slab(h1 + i, b, FC, s, T)

            x = (x_hi, x_lo)
            y = (y3_hi, y3_lo)
            ffn(0, 0, x, (s1_hi, s1_lo), TA, 0)

            slab(SWA_IN, 0, KD, x, TR, ready=tiles_of_norm(1))
            sum_squares(1, TA)
            pe.wait_ge(galo_done, 1)
            for k in range(KD):
                cols = slice(k * RANK, k * RANK + P)
                pe.matmul(bank[6][:, 0:TA], ga_hi[:, cols], x_hi[:, k, :], start=(k == 0), stop=False)
                pe.matmul(bank[6][:, 0:TA], ga_hi[:, cols], x_lo[:, k, :], start=False, stop=False)
                last = pe.matmul(bank[6][:, 0:TA], ga_lo[:, cols], x_hi[:, k, :], start=False, stop=(k == KD - 1))
            last.then_inc(gad_done, 1)
            slab(SWA_IN, 1, KD, x, TR)
            for i in range(1, 6):
                for b in range(2):
                    slab(SWA_IN + i, b, KD, x, TR if i < 4 else TA)

            def values_to_rows():
                pe.wait_ge(bank_free, 2 * GLA_IN)
                for ft in range(2):
                    for tt in range(2):
                        o = tt * 256 + ft * P
                        pe.transpose(bank[2][:, o:o + P], proj[:, SV + ft, tt * P:(tt + 1) * P], ident[:])
                    pe.transpose(bank[3][0:NM, ft * P:(ft + 1) * P], proj[:, SV + ft, M0:TA], ident[:])
                    last = pe.transpose(bank[4][0:NS, ft * P:(ft + 1) * P], proj[:, SV + ft, NP_:TR], ident[:])
                last.then_inc(vtr_done, 1)

            def scores(u):
                g, q0, nk = u // 2, (u % 2) * WIN, WIN * (u % 2 + 1)
                for j in range(4):
                    h = 4 * g + j
                    rows = slice(64 * (h % 2), 64 * (h % 2) + 64)
                    q = proj[rows, SQ + h // 2, q0:q0 + WIN]
                    if u and j == 3:
                        pe.wait_ge(pT_done, 3 * (u - 1) + 1)
                    pe.matmul(bank[2 + j][:, 0:nk], q, proj[rows, KDUP + g, 0:nk], start=True, stop=True)
                    last = pe.matmul(bank[2 + j][:, nk:nk + NM], q, proj[rows, KDUP + g, M0:TA], start=True, stop=True)
                last.then_inc(scores_done, 1)

            def turn_scores(u):
                nk = WIN * (u % 2 + 1)
                pe.wait_ge(p_ready, 6 * u + 6)
                if u:
                    pe.wait_ge(solo_done, 2 * u)
                for j in range(4):
                    pe.transpose(bank[5][0:NM, j * P:(j + 1) * P], sc[:, u % 2, j, nk:nk + NM], ident[:])
                for kc in range(u % 2 + 1):
                    for j in range(4):
                        last = pe.transpose(bank[6 + kc][:, j * P:(j + 1) * P], sc[:, u % 2, j, kc * P:(kc + 1) * P], ident[:])
                last.then_inc(ptr_done, 1)

            def weigh_values(u):
                g = u // 2
                cols = slice(g * HD, (g + 1) * HD)
                pe.wait_ge(pT_done, 3 * u + 3)
                out = bank[6][0:HD, :]
                pe.matmul(out, v_meta[:, cols], pT_meta, start=True, stop=False)
                for kc in range(u % 2 + 1):
                    last = pe.matmul(out, v_tok[:, kc, cols], pT[:, kc], start=False, stop=(kc == u % 2))
                last.then_inc(so_done, 1)

            for u in range(8):
                T = TR if u < 2 else TA
                slab(GLA_IN + u, 0, KD, x, T)
                if u == 0:
                    values_to_rows()
                    pe.wait_ge(kdup_done, 4)
                    pe.wait_ge(vtok_done, 3)
                else:
                    turn_scores(u - 1)
                scores(u)
                slab(GLA_IN + u, 1, KD, x, T)
                if u:
                    weigh_values(u - 1)

            for e in range(8):
                slab(GATE_A + e // 2, e % 2, KD, x, TR)
                if e == 0:
                    turn_scores(7)
                if e == 1:
                    weigh_values(7)
                if e == 2:
                    pe.wait_ge(solo_done, 16)
                    pe.wait_ge(pT_done, 24)
                    pe.wait_ge(gadT_done, 1)
                    for h in range(GH):
                        last = pe.matmul(bank[4 + h][:, 0:TA], a_up[0:RANK, h * DK:(h + 1) * DK], gadT[0:RANK], start=True, stop=True)
                    last.then_inc(z_done, 1)
                if e == 3:
                    pe.wait_ge(knew_done, 2)
                    pe.wait_ge(qpad_done, 5)
                    for b in range(NS):
                        for g in range(2):
                            cols = slice(b * NH + 8 * g, b * NH + 8 * g + 8)
                            pe.matmul(bank[2][:, cols], kT_win[:, b, g, 1:WIN + 1], q_pad[:, b, 8 * g:8 * g + 8], start=True, stop=True)
                            last = pe.matmul(bank[3][0:NM, cols], kT_meta[:, g, b, :], q_pad[:, b, 8 * g:8 * g + 8], start=True, stop=True)
                    last.then_inc(swa_pe, 1)
                if e == 4:
                    pe.wait_ge(swa_act, 2)
                    pe.wait_ge(prep_dve, 4)
                    pe.transpose(bank[4][:, 0:P], sT, ident[:])
                    pe.transpose(bank[4][:, P:P + NM], sT_meta, ident[0:NM, 0:NM]).then_inc(swa_pe, 1)
                if e == 6:
                    pe.wait_ge(swa_dve, 8)
                    pe.transpose(bank[3][:, 0:P], ssc[:, 0:P], ident[:])
                    pe.transpose(bank[3][0:NM, P:2 * P], ssc[:, P:P + NM], ident[:]).then_inc(swa_pe, 1)
                if e == 7:
                    pe.wait_ge(swa_act, 6)
                    turn(pe, 0)
                    pe.wait_ge(vwin_loaded, 16 * (1 + NS))
                    pe.wait_ge(vmeta_loaded, 16)
                    for b in range(NS):
                        for g in range(2):
                            cols = slice(b * NH + 8 * g, b * NH + 8 * g + 8)
                            pe.matmul(bank[2][:, cols], v_win[:, b, g * P:(g + 1) * P], pTs[:, cols], start=True, stop=False)
                            last = pe.matmul(bank[2][:, cols], v_meta_s[:, b, g * P:(g + 1) * P], pTs_meta[:, cols], start=False, stop=True)
                    last.then_inc(swa_pe, 1)
            turn(pe, 1)
            for h in range(GH):
                keys_by_values(pe, 0, h)

            def chunk_and_slab(half, b, c, first=False):
                def beside(i):
                    if 8 <= i < 24:
                        outputs(pe, c, i - 8)
                    elif i >= 24 and i % 2 == 0:
                        keys_by_values(pe, c, (i - 24) // 2)

                slab(half, b, KD, x, TR, beside=None if first else beside)
                attend(pe, c + 1)
                if not isinstance(c, int) or c + 1 < NCK:
                    turn(pe, c + 2)

            chunk_and_slab(GATE_A + 4, 0, 0, first=True)
            chunk_and_slab(GATE_A + 4, 1, 1)
            with pe.Fori(1, 8 - 1) as i:
                for b in range(2):
                    chunk_and_slab(GATE_A + 4 + i, b, 2 * i + b)
            for b in range(2):
                chunk_and_slab(GATE_A + 4 + 7, b, NCK - 2 + b)
            for n in range(16):
                outputs(pe, NCK, n)
            for h in range(GH):
                keys_by_values(pe, NCK, h)

            pe.wait_ge(g_vtok, 2 * NCK + 2)
            for j in range(8):
                last = pe.transpose(bank[4 + j // 4][0:NS, (j % 4) * P:(j % 4 + 1) * P], proj[:, GV + j, NP_:TR], ident[:])
            last.then_inc(nv_tr, 1)

            def decode_outputs(u, n):
                if n == 0:
                    pe.wait_ge(n_state, 4 * u + 4)
                    if u:
                        pe.wait_ge(n_oT, u)
                h, q = n // 2, n % 2
                last = pe.matmul(bank[3][:, n:n + 1], S0[:, u % 3, h, q * P:(q + 1) * P],
                                 proj[:, GQ + h, NP_ + u:NP_ + u + 1], start=True, stop=True)
                if n == 7:
                    last.then_inc(n_o, 1)

            pe.wait_ge(nv_lo, 2)
            for u in range(NS):
                pe.wait_ge(n_pick, u + 1)
                if u:
                    pe.wait_ge(n_state, 4 * u)
                for q in range(2):
                    last = pe.matmul(bank[4 + q][:], pick[:, u % 2], v_split[:, 512 * q:512 * q + 512], start=True, stop=True)
                last.then_inc(n_vbc, 1)
                slab(GATE_B + u // 2, u % 2, KD, x, TR,
                     beside=(lambda i: decode_outputs(u - 1, i // 2) if i % 2 and i < 16 else None) if u else None)
            for n in range(8):
                decode_outputs(NS - 1, n)

            for h in range(GH):
                slab(GATE_B + 4 + h // 2, h % 2, KD, x, TR)
                if h == 0:
                    pe.wait_ge(n_oT, NS)
                    for g in range(GH):
                        pe.wait_ge(on_sq, g + 1)
                        pe.matmul(bank[2 + g][:, 0:TR], ones[:], osq[g // 2][:, g % 2 * 2], start=True, stop=False)
                        pe.matmul(bank[2 + g][:, 0:TR], ones[:], osq[g // 2][:, g % 2 * 2 + 1], start=False, stop=True).then_inc(on_sum, 1)

            def branches(half, b, ready=None):
                n = 2 * half + b
                pe.wait_ge(bank_free, n - 1)
                product(bank[2 + b][:, 0:TR], b, range(8, 16), y, TR, n)
                product(bank[b][:, 0:TR], b, range(8), y, TR, n, ready).then_inc(slab_done, 1)

            pe.wait_ge(solo_done, 16)
            pe.wait_ge(on_std, GH)
            branches(MERGE1, 0, ready=lambda k: pe.wait_ge(olo_done, k + 1))
            branches(MERGE1, 1)
            with pe.Fori(1, 6) as i:
                for b in range(2):
                    branches(MERGE1 + i, b)
            for i in range(4):
                slab(MERGE2 + i, 0, KD, x, TR)
                branches(MERGE2 + i, 1)

            pe.wait_ge(bank_free, 2 * W_OUT - 1)
            product(bank[0][:, 0:TR], 0, (*range(4, KD), *range(4)), x, TR, 2 * W_OUT,
                    ready=lambda k: pe.wait_ge(mlo_done, k // 4 or 4)).then_inc(slab_done, 1)
            slab(W_OUT, 1, KD, x, TR)
            with pe.Fori(1, KD // 2) as i:
                for b in range(2):
                    slab(W_OUT + i, b, KD, x, TR)
            ffn(FFN2, FT, y, x, TR, 2)
            sum_squares(3, TR)


def _slabs(np_, w, kt):
    K, N = w.shape
    return np_.ascontiguousarray(w.reshape(kt, 128, N // 128, 128).transpose(2, 1, 0, 3)).reshape(N // 128, 128, kt * 128)


def _cols(np_, v):
    return np_.ascontiguousarray(v.reshape(-1, 128).T)


def kernel(**inputs):
    import numpy as _np
    import concourse.bacc as _bacc
    from concourse import mybir as _mybir
    from concourse.bass_utils import run_bass_kernel_spmd as _run

    x = {k: _np.asarray(v) for k, v in inputs.items()}
    cat, con = _np.concatenate, _np.ascontiguousarray
    a = {}
    tokens = cat([x["x_prompt"][0], x["x_sample"][:, 0], x["meta_tokens"]], 0)
    a["xT"] = con(tokens.T.reshape(KD, P, TA).transpose(1, 0, 2))
    for n in ("1", "2"):
        w = _slabs(_np, x[f"ffn{n}_w_in"][0], KD)
        a[f"w{n}_in"] = con(w.reshape(2, FT, P, ROW).transpose(1, 0, 2, 3))
        w = x[f"ffn{n}_w_out"][0].reshape(CH, FC, P, KD, P).transpose(0, 3, 2, 1, 4)
        a[f"w{n}_out"] = con(w).reshape(CH, KD // 2, 2, P, FC * P)
    w = x["w_in"][0]
    o_gla, o_r, o_ga, o_swa = 0, 2048, 3072, 3072 + RANK
    o_gate = o_swa + 1536
    order = [w[:, o_swa:o_gate], w[:, o_gla:o_r], w[:, o_gate:o_gate + D], w[:, o_r:o_ga]]
    a["w_proj"] = _slabs(_np, cat(order, 1), KD).reshape(26, 2, P, ROW)
    w_ga = w[:, o_ga:o_swa].reshape(KD, P, RANK).transpose(1, 0, 2).reshape(P, KD * RANK)
    a["w_ga"] = cat([w_ga, _np.zeros((P, GA_COLS - KD * RANK), w.dtype)], 1)
    gate_b = _slabs(_np, w[:, o_gate + D:], KD)
    both = _slabs(_np, cat([x["w_gla_o"][0], x["w_swa_o"][0]], 0), KD)
    rest = con(_np.stack([gate_b[:4], both[:4]], 1)).reshape(8, P, ROW)
    a["w_merge"] = cat([gate_b[8:], gate_b[4:8], both[4:], rest], 0).reshape(KD, 2, P, ROW)
    a["w_o"] = _slabs(_np, x["w_out"][0], KD).reshape(KD // 2, 2, P, ROW)
    norms = [x["ffn1_norm"][0], x["mix_norm"][0], x["ffn2_norm"][0], x["final_norm"]]
    a["gains"] = con(_np.stack([_cols(_np, v) for v in norms], 1))
    a["gbias"] = con(_cols(_np, x["gate_bias"][0]).reshape(P, 2, KD))
    a["onorm"] = _cols(_np, x["gla_out_norm"][0])
    a["a_up"] = con(x["gla_a_up"][0])
    a["a_bias"] = _cols(_np, x["gla_a_bias"][0])
    a["sinks"] = con(x["swa_sinks"])
    a["sink_bh"] = con(_np.tile(x["swa_sinks"][0], NS)[:, None])
    a["kT_cache"] = con(x["cache_win_k"][0].transpose(2, 3, 0, 1).reshape(2, P, NS, WIN).transpose(1, 2, 0, 3))
    a["kT_meta"] = con(x["cache_meta_k"][0].transpose(2, 3, 0, 1).reshape(2, P, NS, NM).transpose(1, 0, 2, 3))
    a["v_cache"] = con(x["cache_win_v"][0, :, 1:].reshape(NS, WIN - 1, 256).transpose(1, 0, 2))
    a["v_meta"] = con(x["cache_meta_v"][0].reshape(NS, NM, 256).transpose(1, 0, 2))
    a["state_in"] = con(x["state_gla"][0].transpose(0, 2, 1, 3))
    f = _np.float32
    slope = _np.exp2(-8.0 * _np.arange(1, NH + 1, dtype=f) / NH).astype(f)
    i, j = _np.arange(WIN)[:, None], _np.arange(2 * WIN)[None, :]
    dist = i + WIN - j
    dist = _np.where((dist >= 0) & (dist < WIN), dist, 1e36).astype(f)
    none = _np.zeros((P, NM), f)
    a["c_dist0"] = cat([dist[:, WIN:], none], 1)
    a["c_dist1"] = cat([dist, none], 1)
    a["c_nslope"] = con(_np.broadcast_to(-slope, (P, NH)))
    bias = -slope[:, None] * (WIN - 1 - _np.arange(WIN, dtype=f))[None, :]
    a["c_bias_s"] = cat([_np.tile(bias, (NS, 1)), none], 1).astype(f)
    a["c_ones"] = _np.ones((P, P), f)
    pick = (_np.arange(P)[:, None] % 32 == _np.arange(NS)[None, :]) & (_np.arange(P)[:, None] < 64)
    a["c_pick"] = pick.astype(f)
    a["c_ident"] = _np.eye(P, dtype=f)
    a["c_onehot"] = con(_np.broadcast_to(_np.eye(CK, dtype=f), (P, CK, CK)))
    keep = _np.ones((P, TA), f)
    keep[:, 0:NP_:CK] = 0
    keep[:, NP_:M0 + 1] = 0
    a["c_scan"] = keep
    s, tt = _np.arange(CK)[:, None, None], _np.arange(CK)[None, None, :]
    a["c_causal"] = con(_np.broadcast_to((tt >= s).astype(f), (CK, GH, CK)))
    outs = {"yT": (P, KD, TR), "kvT": (P, 4, WIN + NM), "winkT": (P, NS, 2, WIN), "winv": (WIN, NS, 256),
            "state_p": (P, GH, DV), "state_s": (NS, P, GH, DV)}

    nc = _bacc.Bacc("TRN2", target_bir_lowering=False, num_devices=1)
    t = {n: nc.dram_tensor(f"in_{n}", v.shape, _mybir.dt.from_np(v.dtype), kind="ExternalInput").ap() for n, v in a.items()}
    t |= {n: nc.dram_tensor(f"out_{n}", s, _mybir.dt.float32, kind="ExternalOutput").ap() for n, s in outs.items()}
    build_layer(nc, t)
    r = _run(nc, [{f"in_{n}": v for n, v in a.items()}], core_ids=[0]).results[0]

    y = r["out_yT"].transpose(2, 1, 0).reshape(TR, D)
    kv = r["out_kvT"].transpose(2, 1, 0).reshape(WIN + NM, 2, 4, HD)
    wk = r["out_winkT"].transpose(1, 3, 2, 0).reshape(1, NS, WIN, 4, HD)
    wv = r["out_winv"].transpose(1, 0, 2).reshape(1, NS, WIN, 4, HD)
    return (con(y[:NP_])[None], con(y[NP_:])[:, None],
            con(kv[WIN:, 0])[None, None], con(kv[WIN:, 1])[None, None],
            con(kv[:WIN, 0])[None, None], con(kv[:WIN, 1])[None, None],
            con(r["out_state_p"].transpose(1, 0, 2))[None, None], con(wk), con(wv),
            con(r["out_state_s"].transpose(0, 2, 1, 3))[None])
```

```python
from contextlib import ExitStack

import numpy as np

import concourse.bass as bass
from concourse import mybir

ALU = mybir.AluOpType
ACT = mybir.ActivationFunctionType
AX = mybir.AxisListType
F32 = mybir.dt.float32
F32R = mybir.dt.float32r

P = 128
D = 2048
DFF = 5632
KD = D // P
FT = DFF // P
CH = 4
FC = FT // CH
NP_, NS, NM = 256, 8, 16
TR = NP_ + NS
TA = TR + NM
M0 = TR
GH, DK, DV, RANK = 4, 128, 256, 16
TAU = 16.0
CK = 16
CP = 2 * CK
NCP = NP_ // CP
NH, HD, WIN = 16, 64, 128
EPS = 1e-6
GA_COLS = (KD - 1) * RANK + P
ROW = 2048

FFN_PAIRS = CH * (FC + KD // 2)
SWA_IN = FFN_PAIRS
GLA_IN = SWA_IN + 6
GATE_A = GLA_IN + 8
GLA_R = GATE_A + 8
GATE_B = GLA_R + 4
MERGE1 = GATE_B + 6
MERGE2 = MERGE1 + 6
W_OUT = MERGE2 + 4
FFN2 = W_OUT + KD // 2
N_PAIRS = FFN2 + FFN_PAIRS

GQ, GK, GV, SQ, SK, SV, KDUP = 0, 4, 8, 16, 24, 26, 28


def build_layer(nc, t):
    ctx = ExitStack()
    with ctx:
        def sb(name, shape, dt=F32):
            return ctx.enter_context(nc.sbuf_tensor(name, shape, dt))

        def sem(name):
            return ctx.enter_context(nc.semaphore(name))

        x_hi = sb("x_hi", [P, KD, TA], F32R)
        x_lo = sb("x_lo", [P, KD, TA], F32R)
        y_hi = sb("y_hi", [P, KD * TR], F32R)
        y_lo = sb("y_lo", [P, KD * TR], F32R)
        w_hi = sb("w_hi", [P, 2, ROW], F32R)
        w_lo = sb("w_lo", [P, 2, ROW], F32R)
        small_r = sb("small_r", [P, 10 * P], F32R)
        ga_hi, ga_lo = small_r[:, 0:GA_COLS], small_r[:, GA_COLS:2 * GA_COLS]
        v_split, pick = small_r[0:32 + NS, 0:8 * P], small_r[0:32 + NS, 8 * P:].rearrange("p (a b) -> p a b", a=2)
        raw = sb("raw", [P, 2, ROW])
        hT = sb("hT", [P, KD, TA])
        proj = sb("proj", [P, 32, TA])
        rstd = sb("rstd", [P, TA])
        gadT = sb("gadT", [P, TA])
        y3_hi = y_hi[:].rearrange("p (k t) -> p k t", k=KD)
        y3_lo = y_lo[:].rearrange("p (k t) -> p k t", k=KD)
        s1_hi = y_hi[:, 0:FC * TA].rearrange("p (k t) -> p k t", k=FC)
        s1_lo = y_lo[:, 0:FC * TA].rearrange("p (k t) -> p k t", k=FC)

        ones = sb("ones", [P, P])
        ident = sb("ident", [P, P])
        band = sb("band", [P, 2 * CP - 1])
        gains = sb("gains", [P, 4, KD])
        gbias = sb("gbias", [P, 2, KD])
        onorm = sb("onorm", [P, 8])
        nslope = sb("nslope", [P, NH])
        sinks = sb("sinks", [P, NH])
        sink_bh = sb("sink_bh", [P, 1])
        causal = sb("causal", [CP, 2, GH, CK])
        a_up = sb("a_up", [P, GH * DK])
        a_bias = sb("a_bias", [P, GH])
        eps = sb("eps", [P, 1])
        warm = sb("warm", [P, 1])
        pick_scale = sb("pick_scale", [P, NS])
        vbuf = sb("vbuf", [P, 8, CP])
        eend = sb("eend", [P, GH])

        R = sb("scratch", [P, 6816])

        def at(o, *shape, parts=P):
            n = int(np.prod(shape))
            v = R[0:parts, o:o + n]
            if len(shape) == 2:
                v = v.rearrange("p (a b) -> p a b", a=shape[0])
            if len(shape) == 3:
                v = v.rearrange("p (a b c) -> p a b c", a=shape[0], b=shape[1])
            return v

        a_n, sig, act_a, b_n, s32 = (at(TA * i, TA) for i in range(5))
        acc, sq, std = (at(TA * i, TA) for i in range(5, 8))
        acc2, sq2 = act_a, b_n
        ga_raw = at(3060, GA_COLS)
        stat = at(256, 64)
        v_new = at(0, 256, parts=NS)
        pT_meta = at(512, 512, parts=NM)
        v_meta = at(2240, 256, parts=NM)
        dist0, dist1 = at(2500, 144), at(2644, 272)
        bias_s = at(336, 144)
        sc = at(3060, 2, 4, 272)
        pT = at(5236, 3, 512)
        v_tok = at(1408, 2, 256)
        kT_win = at(3232, NS, 2, WIN + 1)
        kT_meta = at(1024, 2, NS, NM)
        q_pad = at(1280, NS, NH)
        ssc = at(1408, 144)
        sT, sT_meta = at(1552, P), at(1680, P, parts=NM)
        k_new = at(320, 2, NS)
        pTs, pTs_meta = at(1808, P), at(1936, P, parts=NM)
        v_win = proj[:, SK:SK + NS, 0:256]
        v_meta_s = at(3232, NS, 256, parts=NM)
        oT = at(0, 8, TR)
        spl, mnz = at(5300, GH, TA), at(2112, GH, TA)
        bc = mnz
        scan_keep = at(512, TA)
        S = at(3232, GH, DV)
        Pd = at(4256, CK, GH, CK)
        k_tok = at(5280, 512, parts=CP)
        gv_tok = at(5792, 1024, parts=CP)
        a_smp = a_up[:, TR + GH * CP:TR + GH * CP + GH * NS].rearrange("p (h n) -> p h n", h=GH)
        kd = a_up[:, TR:TR + GH * CP].rearrange("p (h c) -> p h c", h=GH)

        def halves(tiles):
            return tiles.rearrange("p (x h) c -> p x h c", x=2)

        mid, edl = hT[:, 0:8, M0:TA], hT[:, 8:16, M0:TA]
        qd, attT = proj[:, 16:24, M0:TA], proj[0:CP, 24:32, M0:TA]
        S0 = R[:, 2112:2112 + 3 * GH * DV].rearrange("p (n h v) -> p n h v", n=3, h=GH)
        osq = [proj[:, 0:4, 0:TR], at(5216, 4, TR)]
        ostd, ors = at(4160, GH, TR), at(2112, GH, TR)
        ow, rsum = at(5216, 4, TR), proj[:, 0:4, 0:TR]
        gb_n, sigb, m1, m2 = (at(5184 + TR * i, TR) for i in range(4))
        r_act, r_sg = a_up[:, 0:TR], gadT[:, 0:TR]
        siga = proj[:, 16:32, 0:TR]
        merged = proj[:, 0:16, 0:TR]

        bank = [ctx.enter_context(nc.psum_tensor(f"bank{i}", [P, 512], F32)) for i in range(8)]

        raw_loaded = [sem("raw_loaded0"), sem("raw_loaded1")]
        hi_split, lo_split = sem("hi_split"), sem("lo_split")
        slab_done, bank_free = sem("slab_done"), sem("bank_free")
        gains_loaded = sem("gains_loaded")
        x_loaded = [sem(f"x_loaded{i}") for i in range(4)]
        consts_loaded, tables_loaded = sem("consts_loaded"), sem("tables_loaded")
        eps_set, acc_zero, sq_done, acc_done = sem("eps_set"), sem("acc_zero"), sem("sq_done"), sem("acc_done")
        sq2_done, acc2_done = sem("sq2_done"), sem("acc2_done")
        xhi_done, xlo_done = sem("xhi_done"), sem("xlo_done")
        sumsq_done, std_done, rstd_done = sem("sumsq_done"), sem("std_done"), sem("rstd_done")
        sig_done, acta_done, s_done, shi_done, slo_done = (
            sem(n) for n in ("sig_done", "acta_done", "s_done", "shi_done", "slo_done"))
        gahi_done, galo_done, gad_done, gadT_done = (
            sem(n) for n in ("gahi_done", "galo_done", "gad_done", "gadT_done"))
        kv_out, kdup_done, vtr_done, vtok_done = (sem(n) for n in ("kv_out", "kdup_done", "vtr_done", "vtok_done"))
        scores_done, sc_done, soft_step, exp_done = (
            sem(n) for n in ("scores_done", "sc_done", "soft_step", "exp_done"))
        p_ready, ptr_done, pT_done, so_done, sohi_done, solo_done = (
            sem(n) for n in ("p_ready", "ptr_done", "pT_done", "so_done", "sohi_done", "solo_done"))
        kwin_loaded, vwin_loaded, vmeta_loaded, knew_done, qpad_done = (
            sem(n) for n in ("kwin_loaded", "vwin_loaded", "vmeta_loaded", "knew_done", "qpad_done"))
        swa_pe, swa_act, swa_dve, win_out = (sem(n) for n in ("swa_pe", "swa_act", "swa_dve", "win_out"))
        scan_loaded, bias_loaded = sem("scan_loaded"), sem("bias_loaded")
        z_done, prep_act, prep_dve = sem("z_done"), sem("prep_act"), sem("prep_dve")
        (g_eb, g_dl, g_edl, g_kd, g_diff, g_exp, g_pk, g_P, g_att, g_attT, g_kt, g_vt, g_ktok, g_vtok,
         g_vbuf, g_qd, g_o, g_oT, g_kv, g_S) = (sem(n) for n in (
            "g_eb", "g_dl", "g_edl", "g_kd", "g_diff", "g_exp", "g_pk", "g_P", "g_att", "g_attT", "g_kt",
            "g_vt", "g_ktok", "g_vtok", "g_vbuf", "g_qd", "g_o", "g_oT", "g_kv", "g_S"))
        state_out, nv_tr, nv_zero, nv_hi, nv_lo = (
            sem(n) for n in ("state_out", "nv_tr", "nv_zero", "nv_hi", "nv_lo"))
        s0_loaded = [sem(f"s0_loaded{i}") for i in range(3)]
        s0_stored = [sem(f"s0_stored{i}") for i in range(3)]
        rhi_done, rlo_done, r_sum = sem("rhi_done"), sem("rlo_done"), sem("r_sum")
        n_pick, n_vbc, n_decay, n_state, n_o, n_oT = (
            sem(n) for n in ("n_pick", "n_vbc", "n_decay", "n_state", "n_o", "n_oT"))
        r_sig, siga_done = sem("r_sig"), sem("siga_done")
        r_done = sem("r_done")
        g_mid, g_emid, g_kq = sem("g_mid"), sem("g_emid"), sem("g_kq")
        on_sq, on_sum, on_std, on_rs, on_w, on_g, ohi_done, olo_done = (
            sem(n) for n in ("on_sq", "on_sum", "on_std", "on_rs", "on_w", "on_g", "ohi_done", "olo_done"))
        sigb_done, m_step, merged_done, mhi_done, mlo_done = (
            sem(n) for n in ("sigb_done", "m_step", "merged_done", "mhi_done", "mlo_done"))
        y_done, y_gain, y_last, y_out = (sem(n) for n in ("y_done", "y_gain", "y_last", "y_out"))

        def decode_out(gp, jp, dst):
            d = dst[64 * jp:64 * jp + 64, 8:16, NP_:TR].rearrange("p (g a j) b -> p a b g j", g=2, a=2)[:, gp]
            s = bank[2][64 * gp:64 * gp + 64, 0:P].rearrange("p (b g a j e) -> p a e b g j", b=NS, g=2, a=2, j=2)[:, gp, jp]
            return d, s

        def columns(v, width, start=0):
            return slice(v * width + start, (v + 1) * width) if isinstance(v, int) else bass.ds(v * width + start, width - start)

        def pair_cols(u):
            return slice(M0, TA) if isinstance(u, int) and u == 0 else columns(u - 1, CP)

        def by_half(a):
            return a.rearrange("p h (x c) -> p x h c", x=2)

        def later(u, n=1):
            return not isinstance(u, int) or u > n

        def key_decay(act, u):
            act.wait_ge(g_dl, u + 1)
            e = edl if later(u, 0) else edl[:, 0:GH]
            act.activation(e, e, ACT.Exp, scale=1.0 / TAU).then_inc(g_edl, 1)

        def mid_decay(act, u):
            act.wait_ge(g_mid, 2 * u)
            act.activation(mid, mid, ACT.Exp, scale=1.0 / TAU).then_inc(g_emid, 1)

        def token_decay(act, c):
            act.wait_ge(g_diff, 2 * c + 2)
            act.activation(Pd, Pd, ACT.Exp, scale=1.0 / TAU).then_inc(g_exp, 1)

        def start_decay(act, u):
            act.wait_ge(g_S, 4 * u)
            if later(u):
                act.wait_ge(g_o, u - 1)
            act.activation(eend[:].unsqueeze(2), bc[:, :, columns(u - 1, CP, CP - 1)], ACT.Exp, scale=1.0 / TAU)
            act.activation(halves(qd), by_half(bc[:, :, pair_cols(u)]), ACT.Exp, scale=1.0 / TAU).then_inc(g_eb, 1)

        def to_tokens(act, u):
            n = CP if later(u, 0) else CK
            act.wait_ge(g_vt, u + 1)
            if later(u, 0):
                act.wait_ge(g_kv, u)
            if later(u):
                act.wait_ge(g_o, u - 1)
            act.activation(gv_tok[0:n, 0:512], bank[4][0:n, :], ACT.Copy).then_inc(g_vtok, 1)
            act.activation(gv_tok[0:n, 512:], bank[5][0:n, :], ACT.Copy).then_inc(g_vtok, 1)
            act.wait_ge(g_kt, u + 1)
            act.activation(k_tok[0:n, :], bank[3][0:n, :], ACT.Copy).then_inc(g_ktok, 1)

        def out_tile(act, u):
            act.wait_ge(g_o, u)
            act.activation(oT[:, :, pair_cols(u)], bank[2][:, P:P + 8 * CP].rearrange("p (a b) -> p a b", a=8),
                           ACT.Copy).then_inc(g_oT, 1)

        def decay_to_end(dve, u):
            if later(u, 0):
                dve.wait_ge(g_kd, u)
                end = bc[:, :, columns(u - 1, CP, CP - 1)].unsqueeze(1).broadcast_to([P, 2, GH, CK])
                dve.tensor_tensor(halves(edl), end, by_half(bc[:, :, pair_cols(u)]), ALU.subtract).then_inc(g_dl, 1)
            else:
                dve.tensor_tensor(edl[:, 0:GH], bc[:, :, TA - 1:TA].broadcast_to([P, GH, CK]), bc[:, :, M0:TA],
                                  ALU.subtract).then_inc(g_dl, 1)

        def decayed_keys(dve, u):
            if later(u, 0):
                dve.wait_ge(g_kt, u)
            dve.wait_ge(g_edl, u + 1)
            k = proj[:, GK:GK + 4, pair_cols(u)]
            if later(u, 0):
                dve.tensor_tensor(by_half(kd), by_half(k), halves(edl), ALU.mult).then_inc(g_kd, 1)
            else:
                dve.tensor_tensor(kd[:, :, 0:CK], k, edl[:, 0:GH], ALU.mult).then_inc(g_kd, 1)

        def mid_diffs(dve, u):
            if later(u):
                dve.wait_ge(g_att, 2 * u - 2)
            c = 2 * u - 2
            to = bc[:, :, columns(c, CK, CK - 1)].broadcast_to([P, GH, CK])
            dve.tensor_tensor(mid[:, 0:GH], to, bc[:, :, columns(c, CK)], ALU.subtract).then_inc(g_mid, 1)
            dve.tensor_tensor(mid[:, GH:], bc[:, :, columns(c + 1, CK)], to, ALU.subtract).then_inc(g_mid, 1)

        def mid_products(dve, u):
            c = 2 * u - 2
            dve.wait_ge(g_emid, u)
            dve.tensor_tensor(mid[:, 0:GH], proj[:, GK:GK + 4, columns(c, CK)], mid[:, 0:GH], ALU.mult).then_inc(g_kq, 1)
            dve.tensor_tensor(mid[:, GH:], proj[:, GQ:GQ + 4, columns(c + 1, CK)], mid[:, GH:], ALU.mult).then_inc(g_kq, 1)

        def by_s(a):
            return a.rearrange("p h s -> p s h").unsqueeze(3).broadcast_to([P, CK, GH, CK])

        def by_t(a):
            return a.unsqueeze(1).broadcast_to([P, CK, GH, CK])

        def token_diffs(dve, c):
            b = bc[:, :, columns(c, CK)]
            if later(c, 0):
                dve.wait_ge(g_att, c)
            dve.tensor_tensor(Pd, by_t(b), by_s(b), ALU.subtract).then_inc(g_diff, 1)
            dve.wait_ge(g_diff, 2 * c + 1)
            dve.tensor_scalar(Pd, Pd, 0.0, None, ALU.min).then_inc(g_diff, 1)

        def token_products(dve, c):
            cols = columns(c, CK)
            dve.wait_ge(g_exp, c + 1)
            dve.tensor_tensor(Pd, Pd, by_s(proj[:, GK:GK + 4, cols]), ALU.mult).then_inc(g_pk, 1)
            dve.wait_ge(g_pk, c + 1)
            dve.tensor_tensor(Pd, Pd, by_t(proj[:, GQ:GQ + 4, cols]), ALU.mult).then_inc(g_P, 1)

        def attention(dve, u):
            dve.wait_ge(g_att, 2 * u)
            dve.tensor_tensor(halves(attT), bank[2][0:CP, 0:GH * CP].rearrange("p (h x t) -> p x h t", h=GH, x=2),
                              causal[:], ALU.mult).then_inc(g_attT, 1)

        def new_state(dve, u):
            dve.wait_ge(g_kv, u + 1)
            if later(u, 0):
                dve.wait_ge(g_o, u)
                dve.wait_ge(g_S, 4 * u)
                dve.wait_ge(g_eb, u)
            for h in range(GH):
                kv = bank[6 + h // 2][:, (h % 2) * DV:(h % 2 + 1) * DV]
                if later(u, 0):
                    dve.scalar_tensor_tensor(S[:, h], S[:, h], eend[:, h:h + 1], kv, ALU.mult, ALU.add).then_inc(g_S, 1)
                else:
                    dve.tensor_copy(S[:, h], kv).then_inc(g_S, 1)

        def turn(pe, u):
            n = CP if later(u, 0) else CK
            pe.wait_ge(g_vbuf, u + 1)
            if later(u, 0):
                pe.wait_ge(g_vtok, 2 * u)
            for j in range(8):
                last = pe.transpose(bank[4 + j // 4][0:n, (j % 4) * P:(j % 4 + 1) * P], vbuf[:, j, 0:n], ident[:])
            last.then_inc(g_vt, 1)
            pe.wait_ge(g_kd, u + 1)
            if later(u, 0):
                pe.wait_ge(g_ktok, u)
            for h in range(GH):
                last = pe.transpose(bank[3][0:n, h * DK:(h + 1) * DK], kd[:, h, 0:n], ident[:])
            last.then_inc(g_kt, 1)

        def attend(pe, c, half):
            pe.wait_ge(g_P, c + 1)
            cols = bank[2][0:CP, 0:GH * CP].rearrange("p (h x t) -> p x h t", h=GH, x=2)[:, half]
            for s in range(CK):
                m = half * CK + s
                last = pe.matmul(cols, band[:, CP - 1 - m:2 * CP - 1 - m], Pd[:, s],
                                 start=(s == 0), stop=(half == 0 and s == CK - 1))
            if half == 0:
                last.then_inc(g_att, 1)

        def attend_across(pe, u):
            pe.wait_ge(g_kq, 2 * u)
            for h in range(GH):
                last = pe.matmul(bank[2][0:CK, h * CP + CK:(h + 1) * CP], mid[:, h], mid[:, GH + h],
                                 start=False, stop=(h == GH - 1))
            last.then_inc(g_att, 1)

        def keys_by_values(pe, u, h):
            n = CP if later(u, 0) else CK
            if h == 0:
                if later(u, 0):
                    pe.wait_ge(g_S, 4 * u)
                pe.wait_ge(g_ktok, u + 1)
                pe.wait_ge(g_vtok, 2 * u + 2)
            last = pe.matmul(bank[6 + h // 2][:, (h % 2) * DV:(h % 2 + 1) * DV], k_tok[0:n, h * DK:(h + 1) * DK],
                             gv_tok[0:n, h * DV:(h + 1) * DV], start=True, stop=True)
            if h == GH - 1:
                last.then_inc(g_kv, 1)

        def outputs(pe, u, n):
            if n == 0:
                pe.wait_ge(g_qd, u)
                pe.wait_ge(g_S, 4 * u)
                pe.wait_ge(g_attT, u)
            if n == 1:
                pe.wait_ge(g_vtok, 2 * u + 2)
            j, h, q = n // 2, n // 4, n // 2 % 2
            out = bank[2][:, P + j * CP:P + (j + 1) * CP].rearrange("p (x c) -> p x c", x=2)
            if n % 2 == 0:
                pe.matmul(out, S[:, h, q * P:(q + 1) * P], halves(qd)[:, :, h], start=True, stop=False)
            else:
                last = pe.matmul(out, gv_tok[:, j * P:(j + 1) * P], halves(attT)[:, :, h], start=False, stop=True)
                if n == 15:
                    last.then_inc(g_o, 1)

        block = ctx.enter_context(nc.Block())

        N_CONST = 12

        @block.sync
        def _(sp):
            def load_slab(src, half, b, kt, first=False):
                if not first:
                    sp.wait_ge(lo_split, 2 * half + b - 1)
                sp.dma_start(raw[:, b, 0:kt * P], src).then_inc(raw_loaded[b], 16)

            def load_pairs(w, half0, pairs, kt, i0=0):
                with sp.Fori(i0, pairs) as i:
                    for b in range(2):
                        load_slab(w[bass.ds(i, 1), b], half0 + i, b, kt)

            def load_tokens(q):
                sp.dma_start(hT[:, 4 * q:4 * q + 4, :], t["xT"][:, 4 * q:4 * q + 4, :]).then_inc(x_loaded[q], 16)

            sp.dma_start(gains[:], t["gains"]).then_inc(gains_loaded, 16)
            load_tokens(0)
            load_slab(t["w1_in"][0:1, 0], 0, 0, KD, first=True)
            for q in range(1, 4):
                load_tokens(q)
            load_slab(t["w1_in"][0:1, 1], 0, 1, KD, first=True)
            for dst, name in ((ones, "c_ones"), (ident, "c_ident"), (band, "c_band"), (gbias, "gbias"),
                              (onorm, "onorm"), (nslope, "c_nslope"),
                              (causal, "c_causal"), (a_up[0:RANK], "a_up"), (a_bias, "a_bias"), (sink_bh, "sink_bh"),
                              (pick_scale, "c_pick")):
                sp.dma_start(dst[:] if name != "a_up" else dst, t[name]).then_inc(consts_loaded, 16)
            sp.dma_start(sinks[:], t["sinks"].partition_broadcast(P)).then_inc(consts_loaded, 16)
            sp.dma_start(ga_raw, t["w_ga"]).then_inc(tables_loaded, 16)

            def ffn(w_in, w_out, half0, first=False):
                for c in range(CH):
                    h = half0 + c * (FC + KD // 2)
                    load_pairs(w_in[c * FC:(c + 1) * FC], h, FC, KD, i0=1 if first and c == 0 else 0)
                    load_pairs(w_out[c], h + FC, KD // 2, FC)

            ffn(t["w1_in"], t["w1_out"], 0, first=True)
            sp.dma_start(dist0, t["c_dist0"]).then_inc(tables_loaded, 16)
            sp.dma_start(dist1, t["c_dist1"]).then_inc(tables_loaded, 16)
            load_pairs(t["w_proj"][0:6], SWA_IN, 6, KD)
            load_pairs(t["w_proj"][6:14], GLA_IN, 8, KD)
            load_pairs(t["w_proj"][14:22], GATE_A, 8, KD)
            load_pairs(t["w_proj"][22:26], GLA_R, 4, KD)
            load_pairs(t["w_merge"], GATE_B, KD, KD)
            load_pairs(t["w_o"], W_OUT, KD // 2, KD)
            ffn(t["w2_in"], t["w2_out"], FFN2)
            for q in range(4):
                if q < 3:
                    sp.wait_ge(y_done, 4 * q + 4)
                else:
                    sp.wait_ge(y_last, 4)
                sp.dma_start(t["yT"][:, 4 * q:4 * q + 4, :], hT[:, 4 * q:4 * q + 4, 0:TR]).then_inc(y_out, 16)
            sp.wait_ge(y_out, 64)
            sp.wait_ge(kv_out, 32)
            sp.wait_ge(win_out, 32)
            sp.wait_ge(state_out, 16)
            for b in range(3):
                sp.wait_ge(s0_stored[b], 16 * len(range(b, NS, 3)))

        @block.gpsimd
        def _(pool):
            pool.memset(eps[:], EPS).then_inc(eps_set, 1)

            def zero_acc(r):
                if r:
                    pool.wait_ge(sumsq_done, r)
                pool.memset(acc, 0.0).then_inc(acc_zero, 1)
                pool.wait_ge(acc_zero, r + 1)

            def add_square(h, n_sq, T, tiles=1):
                pool.tensor_tensor(sq[:, 0:T], h, h, ALU.mult).then_inc(sq_done, 1)
                pool.wait_ge(sq_done, n_sq)
                pool.tensor_tensor(acc[:, 0:T], acc[:, 0:T], sq[:, 0:T], ALU.add).then_inc(acc_done, tiles)

            zero_acc(0)
            for m in range(0, KD, 2):
                pool.wait_ge(x_loaded[m // 4], 16)
                if m:
                    pool.wait_ge(acc_done, m)
                add_square(hT[:, m, :], m // 2 + 1, TA, tiles=2)

            def residual_squares(r, half0, T):
                pool.wait_ge(bank_free, 2 * half0)
                zero_acc(r)
                with pool.Fori(0, KD) as m:
                    pool.wait_ge(bank_free, 2 * half0 + m + 1)
                    pool.wait_ge(acc_done, KD * r + m)
                    add_square(hT[:, bass.ds(m, 1), 0:T], KD * r - KD // 2 + m + 1, T)

            residual_squares(1, SWA_IN - KD // 2, TA)

            pool.wait_ge(bank_free, 2 * GLA_IN)
            pool.dma_start(t["kvT"][:, :, 0:WIN], proj[:, SK:SK + 4, NP_ - WIN:NP_]).then_inc(kv_out, 16)
            pool.dma_start(t["kvT"][:, :, WIN:], proj[:, SK:SK + 4, M0:TA]).then_inc(kv_out, 16)
            pool.dma_start(bias_s, t["c_bias_s"]).then_inc(bias_loaded, 16)
            pool.memset(q_pad, 0.0).then_inc(qpad_done, 1)

            pool.wait_ge(kv_out, 32)
            pool.wait_ge(knew_done, 1)
            pool.wait_ge(ptr_done, 8)
            pool.dma_start(kT_meta, t["kT_meta"]).then_inc(kwin_loaded, 16)
            pool.wait_ge(so_done, 8)
            pool.dma_start(kT_win[:, :, :, 0:WIN], t["kT_cache"]).then_inc(kwin_loaded, 16)
            pool.dma_start(scan_keep, t["c_scan"]).then_inc(scan_loaded, 16)
            pool.dma_start(v_win[0:WIN - 1], t["v_cache"]).then_inc(vwin_loaded, 16)
            for b in range(NS):
                pool.dma_start(v_win[WIN - 1:WIN, b, :], v_new[b:b + 1, :]).then_inc(vwin_loaded, 16)
            pool.wait_ge(knew_done, 2)
            pool.dma_start(t["winkT"], kT_win[:, :, :, 1:WIN + 1]).then_inc(win_out, 16)
            pool.wait_ge(vwin_loaded, 16 * (1 + NS))
            pool.dma_start(t["winv"], v_win).then_inc(win_out, 16)
            pool.wait_ge(win_out, 32)
            pool.wait_ge(swa_pe, 1)
            pool.dma_start(v_meta_s, t["v_meta"]).then_inc(vmeta_loaded, 16)

            pool.wait_ge(prep_dve, 9)
            pool.tensor_copy(vbuf[:, :, 0:CK], proj[:, GV:GV + 8, M0:TA]).then_inc(g_vbuf, 1)

            def store_state(u):
                pool.wait_ge(n_state, 4 * (u + 1))
                pool.wait_ge(n_o, u + 1)
                pool.dma_start(t["state_s"][u], S0[:, u % 3]).then_inc(s0_stored[u % 3], 16)

            def values(u):
                pool.wait_ge(g_vt, u)
                pool.tensor_copy(vbuf[:], proj[:, GV:GV + 8, pair_cols(u)]).then_inc(g_vbuf, 1)

            def queries(u):
                pool.wait_ge(g_eb, u)
                pool.tensor_tensor(halves(qd), by_half(proj[:, GQ:GQ + 4, pair_cols(u)]), halves(qd),
                                   ALU.mult).then_inc(g_qd, 1)

            values(1)
            with pool.Fori(1, NCP) as u:
                values(u + 1)
                queries(u)
            queries(NCP)

            pool.wait_ge(g_eb, NCP)
            pool.wait_ge(g_mid, 2 * NCP)
            pool.wait_ge(g_diff, 2 * NP_ // CK)
            pool.wait_ge(g_kd, NCP + 1)
            pool.dma_start(S0[:, 0], t["state_in"][0]).then_inc(s0_loaded[0], 16)
            pool.wait_ge(g_S, 4 * (NCP + 1))
            pool.dma_start(t["state_p"], S).then_inc(state_out, 16)
            pool.wait_ge(state_out, 16)
            for u in range(1, NS):
                b = u % 3
                if u >= 3:
                    pool.wait_ge(s0_stored[b], 16 * (u // 3))
                pool.dma_start(S0[:, b], t["state_in"][u]).then_inc(s0_loaded[b], 16)
                if u >= 2:
                    store_state(u - 2)
            for u in range(NS - 2, NS):
                store_state(u)

            pool.wait_ge(on_std, GH)
            for j in range(8):
                if j >= 4:
                    pool.wait_ge(on_g, j - 3)
                pool.tensor_tensor(rsum[:, j % 4], y3_hi[:, j].bitcast(F32), y3_lo[:, j].bitcast(F32),
                                   ALU.add).then_inc(r_sum, 1)
                pool.wait_ge(r_sum, j + 1)
                pool.wait_ge(on_w, j + 1)
                pool.tensor_tensor(ow[:, j % 4], ow[:, j % 4], rsum[:, j % 4], ALU.mult).then_inc(on_g, 1)

            residual_squares(2, W_OUT, TR)
            residual_squares(3, N_PAIRS - KD // 2, TR)

            for m in range(KD - 4, KD):
                h = hT[:, m, 0:TR]
                pool.tensor_tensor(h, h, gains[:, 3, m:m + 1].broadcast_to([P, TR]), ALU.mult).then_inc(y_gain, 1)
            pool.wait_ge(rstd_done, 4)
            for m in range(KD - 4, KD):
                h = hT[:, m, 0:TR]
                pool.wait_ge(y_gain, m - KD + 5)
                pool.tensor_tensor(h, h, rstd[:, 0:TR], ALU.mult).then_inc(y_last, 1)

        @block.scalar
        def _(act):
            def split_hi(half, b, kt, first=False):
                act.wait_ge(raw_loaded[b], 16 * (half + 1))
                if not first:
                    act.wait_ge(slab_done, 2 * half + b - 1)
                act.activation(w_hi[:, b, 0:kt * P], raw[:, b, 0:kt * P], ACT.Copy).then_inc(hi_split, 1)

            def tile_hi(r, m, x, T):
                act.activation(x[:, m, 0:T], hT[:, m, 0:T], ACT.Copy,
                               scale=gains[:, r, m]).then_inc(xhi_done, 1)

            def root(r, T):
                act.activation(warm[:], eps[:, 0:1], ACT.Sqrt)
                act.wait_ge(sumsq_done, r + 1)
                act.activation(std[:, 0:T], bank[7][:, 0:T], ACT.Sqrt, bias=eps[:, 0:1],
                               scale=1.0 / D).then_inc(std_done, 1)

            def ffn(half0, f0, s_hi, T, r, r_next=None, x_next=None, kt_after=KD):
                for c in range(CH):
                    h0 = half0 + c * (FC + KD // 2)

                    def inner(i, kt_next, last_inner=False, first=False):
                        half, f = h0 + i, f0 + c * FC + i
                        split_hi(half + 1, 0, kt_next)
                        if first:
                            root(r, T)
                        act.wait_ge(bank_free, 2 * half + 1)
                        act.activation(sig[:, 0:T], a_n[:, 0:T], ACT.Sigmoid).then_inc(sig_done, 1)
                        if not last_inner:
                            split_hi(half + 1, 1, kt_next)
                        act.wait_ge(s_done, f + 1)
                        act.activation(s_hi[:, bass.ds(i, 1), 0:T], s32[:, 0:T], ACT.Copy).then_inc(shi_done, 1)
                        if last_inner:
                            split_hi(half + 1, 1, kt_next)

                    if c == 0:
                        inner(0, KD, first=True)
                    with act.Fori(1 if c == 0 else 0, FC - 1) as i:
                        inner(i, KD)
                    inner(FC - 1, FC, last_inner=True)
                    h1 = h0 + FC
                    last = c == CH - 1

                    def outer(i, kt_next, split=True):
                        for b in range(2):
                            tile_first = isinstance(i, int)
                            if split and not tile_first:
                                split_hi(h1 + i + 1, b, kt_next)
                            if last and x_next is not None:
                                act.wait_ge(bank_free, 2 * (h1 + i) + b + 1)
                                tile_hi(r_next, bass.ds(2 * i + b, 1), x_next, T)
                            if split and tile_first:
                                split_hi(h1 + i + 1, b, kt_next)

                    with act.Fori(0, KD // 2 - 1) as i:
                        outer(i, FC)
                    outer(KD // 2 - 1, kt_after, split=h1 + KD // 2 < N_PAIRS)

            act.wait_ge(gains_loaded, 16)
            for m in range(KD):
                act.wait_ge(x_loaded[m // 4], 16)
                tile_hi(0, slice(m, m + 1), x_hi, TA)
                if m == 3:
                    split_hi(0, 0, KD, first=True)
            split_hi(0, 1, KD, first=True)
            act.wait_ge(eps_set, 1)
            ffn(0, 0, s1_hi, TA, 0, 1, x_hi)
            act.wait_ge(tables_loaded, 16)
            act.activation(ga_hi, ga_raw, ACT.Copy).then_inc(gahi_done, 1)

            root(1, TA)
            for i in range(6):
                for b in range(2):
                    split_hi(SWA_IN + i + 1, b, KD)
            act.wait_ge(bank_free, 2 * GLA_IN)
            for a in range(2):
                for b in range(2):
                    act.activation(proj[64 * b:64 * b + 64, KDUP + a:KDUP + 4:2, :],
                                   proj[64 * a:64 * a + 64, SK:SK + 2, :], ACT.Copy).then_inc(kdup_done, 1)

            def soft_exp(u):
                nk = 144 if u % 2 == 0 else 272
                act.wait_ge(soft_step, 4 * u + 4)
                for j in range(4):
                    act.activation(sc[:, u % 2, j, 0:nk], sc[:, u % 2, j, 0:nk], ACT.Exp,
                                   bias=stat[:, 8 + j:9 + j], accum_out=stat[:, 16 + j:17 + j]).then_inc(exp_done, 1)
                act.activation(stat[:, 20:24], stat[:, 12:16], ACT.Exp).then_inc(exp_done, 1)

            def move_pT(u):
                act.wait_ge(ptr_done, u + 1)
                if u:
                    act.wait_ge(so_done, u)
                act.activation(pT_meta, bank[5][0:NM, :], ACT.Copy).then_inc(pT_done, 1)
                act.activation(pT[:, 0], bank[6][:], ACT.Copy).then_inc(pT_done, 1)
                src = bank[7] if u % 2 else bank[6]
                act.activation(pT[:, 1 if u % 2 else 2], src[:], ACT.Copy).then_inc(pT_done, 1)

            def out_hi(u):
                g, q0 = u // 2, (u % 2) * WIN
                act.wait_ge(so_done, u + 1)
                for jp in range(2):
                    src = bank[6][0:HD, :].rearrange("p (j e q) -> p e j q", j=2, e=2)[:, jp]
                    act.activation(y3_hi[64 * jp:64 * jp + 64, 8 + 2 * g:10 + 2 * g, q0:q0 + WIN], src,
                                   ACT.Copy).then_inc(sohi_done, 1)

            for u in range(8):
                half = GLA_IN + u
                split_hi(half + 1, 0, KD)
                if u == 0:
                    act.wait_ge(vtr_done, 1)
                    act.activation(v_tok, bank[2][:].rearrange("p (a b) -> p a b", a=2), ACT.Copy).then_inc(vtok_done, 1)
                    act.activation(v_meta, bank[3][0:NM, 0:256], ACT.Copy).then_inc(vtok_done, 1)
                    act.activation(v_new, bank[4][0:NS, 0:256], ACT.Copy).then_inc(vtok_done, 1)
                if u:
                    move_pT(u - 1)
                soft_exp(u)
                split_hi(half + 1, 1, KD)
                if u:
                    out_hi(u - 1)

            act.activation(k_new, proj[:, SK:SK + 2, NP_:TR], ACT.Copy).then_inc(knew_done, 1)
            act.wait_ge(qpad_done, 1)
            for gp in range(2):
                for jp in range(2):
                    src = proj[64 * jp:64 * jp + 64, SQ:SQ + 8, NP_:TR].rearrange(
                        "p (g a j) b -> p a b g j", g=2, a=2)[:, gp]
                    dst = q_pad[64 * gp:64 * gp + 64].rearrange(
                        "p b (g a j e) -> p a e b g j", g=2, a=2, j=2)[:, gp, jp]
                    act.activation(dst, src, ACT.Copy).then_inc(qpad_done, 1)

            def gate_a(half, m):
                act.activation(siga[:, m], siga[:, m], ACT.Sigmoid, bias=gbias[:, 0, m]).then_inc(siga_done, 1)

            for e in range(8):
                half, b = GATE_A + e // 2, e % 2
                split_hi(half + 1, b, KD)
                if e == 0:
                    move_pT(7)
                if e == 1:
                    out_hi(7)
                if e == 3:
                    act.wait_ge(z_done, 1)
                    for h in range(GH):
                        act.activation(spl[:, h], bank[4 + h][:, 0:TA], ACT.Abs, bias=a_bias[:, h:h + 1]).then_inc(prep_act, 1)
                    act.wait_ge(prep_act, 4)
                    act.activation(spl, spl, ACT.Exp, scale=-1.0).then_inc(prep_act, 1)
                    act.wait_ge(prep_act, 5)
                    act.activation(spl, spl, ACT.Ln, bias=1.0).then_inc(prep_act, 1)
                if e == 7:
                    to_tokens(act, 0)
                act.wait_ge(bank_free, 2 * half + b + 1)
                gate_a(half, slice(e, e + 1))
                if e == 2:
                    act.wait_ge(kwin_loaded, 32)
                    act.wait_ge(knew_done, 1)
                    act.activation(kT_win[:, :, :, WIN].rearrange("p b g -> p g b"), k_new, ACT.Copy).then_inc(knew_done, 1)
                if e == 3:
                    act.wait_ge(swa_pe, 1)
                    act.activation(sT, bank[2][:, 0:P], ACT.Copy).then_inc(swa_act, 1)
                    act.activation(sT_meta, bank[3][0:NM, 0:P], ACT.Copy).then_inc(swa_act, 1)
                if e == 4:
                    act.wait_ge(swa_dve, 5)
                    act.activation(ssc, ssc, ACT.Exp, bias=stat[:, 3:4], accum_out=stat[:, 5:6]).then_inc(swa_act, 1)
                    act.activation(stat[:, 6:7], stat[:, 4:5], ACT.Exp).then_inc(swa_act, 1)
                if e == 5:
                    act.wait_ge(prep_dve, 9)
                    act.activation(a_smp, bc[:, :, NP_:TR], ACT.Exp, scale=1.0 / TAU).then_inc(prep_act, 1)
                    key_decay(act, 0)
                if e == 6:
                    act.wait_ge(swa_pe, 3)
                    act.activation(pTs, bank[3][:, 0:P], ACT.Copy).then_inc(swa_act, 1)
                    act.activation(pTs_meta, bank[3][0:NM, P:2 * P], ACT.Copy).then_inc(swa_act, 1)
                    key_decay(act, 1)

            act.wait_ge(swa_pe, 4)
            for gp in range(2):
                for jp in range(2):
                    dst, src = decode_out(gp, jp, y3_hi)
                    act.activation(dst, src, ACT.Copy).then_inc(swa_act, 1)
            token_decay(act, 0)

            def pair_of_slabs(half, v, gate, more=True):
                u = v + 1
                split_hi(half + 1, 0, KD)
                mid_decay(act, u)
                token_decay(act, 2 * v + 1)
                if more:
                    key_decay(act, u + 1)
                gate(half, 0, 2 * v)
                to_tokens(act, u)
                start_decay(act, u)
                split_hi(half + 1, 1, KD)
                if more:
                    token_decay(act, 2 * v + 2)
                gate(half, 1, 2 * v + 1)
                if more:
                    out_tile(act, u)

            def gate_a_slab(half, b, c):
                act.wait_ge(bank_free, 2 * half + b + 1)
                gate_a(half, slice(c + 8, c + 9) if isinstance(c, int) else bass.ds(c + 8, 1))

            def gate_r_slab(half, b, c):
                m = c - 8
                act.wait_ge(bank_free, 2 * half + b + 1)
                act.activation(r_sg, r_act, ACT.Sigmoid).then_inc(r_sig, 1)
                act.wait_ge(r_done, m + 1)
                act.activation(y3_hi[:, slice(m, m + 1) if isinstance(m, int) else bass.ds(m, 1)], r_act,
                               ACT.Copy).then_inc(rhi_done, 1)

            pair_of_slabs(GATE_A + 4, 0, gate_a_slab)
            with act.Fori(1, 4) as v:
                pair_of_slabs(GATE_A + 4 + v, v, gate_a_slab)
            with act.Fori(4, NCP - 1) as v:
                pair_of_slabs(GATE_A + 4 + v, v, gate_r_slab)
            pair_of_slabs(GLA_R + 3, NCP - 1, gate_r_slab, more=False)

            def gate_b(m):
                act.activation(merged[:, m], merged[:, m], ACT.Sigmoid, bias=gbias[:, 1, m:m + 1]).then_inc(sigb_done, 1)

            def pick_token(u):
                if u >= 2:
                    act.wait_ge(n_vbc, u - 1)
                act.activation(pick[:, u % 2], ones[0:32 + NS, :], ACT.Copy,
                               scale=pick_scale[0:32 + NS, u:u + 1]).then_inc(n_pick, 1)

            act.activation(v_split.rearrange("p (a b) -> p a b", a=8),
                           ones[0:32 + NS, :].unsqueeze(1).broadcast_to([32 + NS, 8, P]), ACT.Copy,
                           scale=0.0).then_inc(nv_zero, 1)
            act.wait_ge(nv_tr, 1)
            act.wait_ge(nv_zero, 1)
            for q in range(2):
                act.activation(v_split[0:NS, 512 * q:512 * q + 512], bank[4 + q][0:NS, :], ACT.Copy).then_inc(nv_hi, 1)
            pick_token(0)
            out_tile(act, NCP)
            for u in range(NS):
                half, b = GATE_B + u // 2, u % 2
                if u + 1 < NS:
                    pick_token(u + 1)
                act.wait_ge(s0_loaded[u % 3], 16 * (u // 3 + 1))
                for h in range(GH):
                    act.activation(S0[:, u % 3, h], S0[:, u % 3, h], ACT.Copy, scale=a_smp[:, h, u:u + 1]).then_inc(n_decay, 1)
                if u:
                    act.wait_ge(n_o, u)
                    act.activation(oT[:, :, NP_ + u - 1], bank[3][:, 0:8], ACT.Copy).then_inc(n_oT, 1)
                split_hi(half + 1, b, KD)
                act.wait_ge(bank_free, 2 * half + b + 1)
                gate_b(8 + u)
            act.wait_ge(n_o, NS)
            act.activation(oT[:, :, NP_ + NS - 1], bank[3][:, 0:8], ACT.Copy).then_inc(n_oT, 1)

            act.wait_ge(n_oT, NS)
            act.wait_ge(g_oT, NCP)
            for h in range(GH):
                act.activation(osq[h // 2][:, h % 2 * 2:h % 2 * 2 + 2], oT[:, 2 * h:2 * h + 2, :], ACT.Square).then_inc(on_sq, 1)
            for h in range(GH):
                half, b = GATE_B + 4 + h // 2, h % 2
                split_hi(half + 1, b, KD)
                if h == 0:
                    act.wait_ge(s0_stored[2], 16 * 2)
                    for g in range(GH):
                        act.wait_ge(on_sum, g + 1)
                        act.activation(ostd[:, g], bank[2 + g][:, 0:TR], ACT.Sqrt, bias=eps[:, 0:1],
                                       scale=1.0 / DV).then_inc(on_std, 1)
                if h:
                    for q in range(2 * h - 2, 2 * h):
                        act.wait_ge(on_g, q + 1)
                        act.activation(y3_hi[:, q], ow[:, q % 4], ACT.Copy).then_inc(ohi_done, 1)
                act.wait_ge(bank_free, 2 * half + b + 1)
                gate_b(4 + h)
            for q in range(2 * GH - 2, 2 * GH):
                act.wait_ge(on_g, q + 1)
                act.activation(y3_hi[:, q], ow[:, q % 4], ACT.Copy).then_inc(ohi_done, 1)

            with act.Fori(0, 6) as i:
                for b in range(2):
                    split_hi(MERGE1 + i + 1, b, KD)

            def merged_hi(k0, k1, n):
                act.wait_ge(merged_done, n)
                act.activation(x_hi[:, k0:k1, 0:TR], merged[:, k0:k1, :], ACT.Copy).then_inc(mhi_done, 1)

            for i in range(4):
                half = MERGE2 + i
                split_hi(half + 1, 0, KD)
                act.wait_ge(bank_free, 2 * half + 1)
                act.activation(sigb, gb_n, ACT.Sigmoid, bias=gbias[:, 1, i:i + 1]).then_inc(sigb_done, 1)
                if i == 3:
                    for q in range(1, 4):
                        merged_hi(4 * q, 4 * q + 4, 4 * q)
                    merged_hi(0, 3, KD - 1)
                if i == 3:
                    merged_hi(3, 4, KD)
                split_hi(half + 1, 1, KD)

            with act.Fori(0, KD // 2 - 1) as i:
                for b in range(2):
                    split_hi(W_OUT + i + 1, b, KD)
                    act.wait_ge(bank_free, 2 * (W_OUT + i) + b + 1)
                    tile_hi(2, bass.ds(2 * i + b, 1), y3_hi, TR)
            for b in range(2):
                act.wait_ge(bank_free, 2 * FFN2 - 1 + b)
                tile_hi(2, slice(KD - 2 + b, KD - 1 + b), y3_hi, TR)
                split_hi(FFN2, b, KD)
            ffn(FFN2, FT, x_hi, TR, 2)
            root(3, TR)

        @block.vector
        def _(dve):
            def split_lo(half, b, kt):
                dve.wait_ge(hi_split, 2 * half + b + 1)
                dve.tensor_tensor(w_lo[:, b, 0:kt * P], raw[:, b, 0:kt * P], w_hi[:, b, 0:kt * P].bitcast(F32),
                                  ALU.subtract).then_inc(lo_split, 1)

            def tile_lo(r, m, x, T, n):
                dve.wait_ge(xhi_done, n)
                dve.scalar_tensor_tensor(x[1][:, m, 0:T], hT[:, m, 0:T], gains[:, r, m],
                                         x[0][:, m, 0:T].bitcast(F32), ALU.mult, ALU.subtract).then_inc(xlo_done, 1)

            def inverse(r, T):
                dve.wait_ge(std_done, r + 1)
                dve.reciprocal(rstd[:, 0:T], std[:, 0:T]).then_inc(rstd_done, 1)
                dve.wait_ge(rstd_done, r + 1)

            def ffn(half0, f0, s_hi, s_lo, T, r, r_next=None, x_next=None, kt_after=KD):
                for c in range(CH):
                    h0 = half0 + c * (FC + KD // 2)

                    def inner(i, kt_next, last_inner=False, first=False):
                        half, f = h0 + i, f0 + c * FC + i
                        if first:
                            split_lo(half + 1, 0, kt_next)
                            inverse(r, T)
                        dve.wait_ge(slab_done, 2 * half + 1)
                        dve.tensor_tensor(a_n[:, 0:T], bank[0][:, 0:T], rstd[:, 0:T], ALU.mult).then_inc(bank_free, 1)
                        if not first:
                            split_lo(half + 1, 0, kt_next)
                        dve.wait_ge(sig_done, f + 1)
                        dve.tensor_tensor(act_a[:, 0:T], a_n[:, 0:T], sig[:, 0:T], ALU.mult).then_inc(acta_done, 1)
                        dve.wait_ge(slab_done, 2 * half + 2)
                        dve.tensor_tensor(b_n[:, 0:T], bank[1][:, 0:T], rstd[:, 0:T], ALU.mult).then_inc(bank_free, 1)
                        dve.wait_ge(bank_free, 2 * half + 2)
                        dve.wait_ge(acta_done, f + 1)
                        dve.tensor_tensor(s32[:, 0:T], act_a[:, 0:T], b_n[:, 0:T], ALU.mult).then_inc(s_done, 1)
                        if not last_inner:
                            split_lo(half + 1, 1, kt_next)
                        dve.wait_ge(shi_done, f + 1)
                        dve.tensor_tensor(s_lo[:, bass.ds(i, 1), 0:T], s32[:, 0:T],
                                          s_hi[:, bass.ds(i, 1), 0:T].bitcast(F32), ALU.subtract).then_inc(slo_done, 1)
                        if last_inner:
                            split_lo(half + 1, 1, kt_next)

                    if c == 0:
                        inner(0, KD, first=True)
                    with dve.Fori(1 if c == 0 else 0, FC - 1) as i:
                        inner(i, KD)
                    inner(FC - 1, FC, last_inner=True)
                    h1 = h0 + FC
                    last = c == CH - 1

                    def outer(i, kt_next, split=True):
                        for b in range(2):
                            n, m = 2 * (h1 + i) + b, bass.ds(2 * i + b, 1)
                            dve.wait_ge(slab_done, n + 1)
                            dve.scalar_tensor_tensor(hT[:, m, 0:T], bank[b][:, 0:T], 0.5, hT[:, m, 0:T],
                                                     ALU.mult, ALU.add).then_inc(bank_free, 1)
                            tile_first = isinstance(i, int)
                            if split and not tile_first:
                                split_lo(h1 + i + 1, b, kt_next)
                            if last and x_next is not None:
                                tile_lo(r_next, m, x_next, T, KD * r_next + 2 * i + b + 1)
                            if split and tile_first:
                                split_lo(h1 + i + 1, b, kt_next)

                    with dve.Fori(0, KD // 2 - 1) as i:
                        outer(i, FC)
                    outer(KD // 2 - 1, kt_after, split=h1 + KD // 2 < N_PAIRS)

            dve.wait_ge(gains_loaded, 16)
            for m in range(KD):
                tile_lo(0, slice(m, m + 1), (x_hi, x_lo), TA, m + 1)
                if m == 3:
                    split_lo(0, 0, KD)
            split_lo(0, 1, KD)
            dve.tensor_tensor(acc2, hT[:, 1], hT[:, 1], ALU.mult).then_inc(acc2_done, 1)
            for n in range(1, KD // 2):
                dve.tensor_tensor(sq2, hT[:, 2 * n + 1], hT[:, 2 * n + 1], ALU.mult).then_inc(sq2_done, 1)
                dve.wait_ge(sq2_done, n)
                dve.wait_ge(acc2_done, n)
                dve.tensor_tensor(acc2, acc2, sq2, ALU.add).then_inc(acc2_done, 1)
                dve.wait_ge(acc2_done, n + 1)
            ffn(0, 0, s1_hi, s1_lo, TA, 0, 1, (x_hi, x_lo))
            dve.wait_ge(gahi_done, 1)
            dve.tensor_tensor(ga_lo, ga_raw, ga_hi.bitcast(F32), ALU.subtract).then_inc(galo_done, 1)
            dve.wait_ge(consts_loaded, 16 * N_CONST)
            inverse(1, TA)

            def project(half, b, dst, scale, T):
                dve.wait_ge(slab_done, 2 * half + b + 1)
                dve.scalar_tensor_tensor(dst, bank[b][:, 0:T], scale, rstd[:, 0:T], ALU.mult, ALU.mult).then_inc(bank_free, 1)
                split_lo(half + 1, b, KD)

            for i in range(6):
                for b in range(2):
                    T, scale = (TR, HD ** -0.5) if i < 4 else (TA, 1.0)
                    project(SWA_IN + i, b, proj[:, SQ + 2 * i + b, 0:T], scale, T)
                    if i == 0 and b == 0:
                        dve.wait_ge(gad_done, 1)
                        dve.tensor_tensor(gadT[0:RANK], bank[6][0:RANK, 0:TA], rstd[0:RANK, :], ALU.mult).then_inc(gadT_done, 1)

            def soft_max(u):
                g, blk = u // 2, u % 2
                nk, dist = (272, dist1) if blk else (144, dist0)
                dve.wait_ge(scores_done, u + 1)
                for j in range(4):
                    h = 4 * g + j
                    dve.scalar_tensor_tensor(sc[:, u % 2, j, 0:nk], dist, nslope[:, h:h + 1], bank[2 + j][:, 0:nk],
                                             ALU.mult, ALU.add).then_inc(sc_done, 1)
                dve.wait_ge(sc_done, 4 * u + 4)
                dve.tensor_reduce(stat[:, 0:4], sc[:, u % 2, :, 0:nk], AX.X, ALU.max).then_inc(soft_step, 1)
                dve.wait_ge(soft_step, 4 * u + 1)
                dve.tensor_tensor(stat[:, 4:8], stat[:, 0:4], sinks[:, 4 * g:4 * g + 4], ALU.max).then_inc(soft_step, 1)
                dve.wait_ge(soft_step, 4 * u + 2)
                dve.tensor_scalar(stat[:, 8:12], stat[:, 4:8], -1.0, None, ALU.mult).then_inc(soft_step, 1)
                dve.tensor_tensor(stat[:, 12:16], sinks[:, 4 * g:4 * g + 4], stat[:, 4:8], ALU.subtract).then_inc(soft_step, 1)

            def soft_norm(u):
                nk = 272 if u % 2 else 144
                dve.wait_ge(exp_done, 5 * u + 5)
                dve.tensor_tensor(stat[:, 24:28], stat[:, 16:20], stat[:, 20:24], ALU.add).then_inc(p_ready, 1)
                dve.wait_ge(p_ready, 6 * u + 1)
                dve.reciprocal(stat[:, 28:32], stat[:, 24:28]).then_inc(p_ready, 1)
                dve.wait_ge(p_ready, 6 * u + 2)
                for j in range(4):
                    dve.tensor_scalar(sc[:, u % 2, j, 0:nk], sc[:, u % 2, j, 0:nk], stat[:, 28 + j:29 + j], None,
                                      ALU.mult).then_inc(p_ready, 1)

            def out_lo(u):
                g, q0 = u // 2, (u % 2) * WIN
                dve.wait_ge(sohi_done, 2 * u + 2)
                for jp in range(2):
                    src = bank[6][0:HD, :].rearrange("p (j e q) -> p e j q", j=2, e=2)[:, jp]
                    rows, tiles = slice(64 * jp, 64 * jp + 64), slice(8 + 2 * g, 10 + 2 * g)
                    dve.tensor_tensor(y3_lo[rows, tiles, q0:q0 + WIN], src,
                                      y3_hi[rows, tiles, q0:q0 + WIN].bitcast(F32), ALU.subtract).then_inc(solo_done, 1)

            dve.wait_ge(tables_loaded, 16 * 3)
            for u in range(8):
                T, scale = (TR, DK ** -0.5) if u < 2 else (TA, 1.0)
                project(GLA_IN + u, 0, proj[:, 2 * u, 0:T], scale, T)
                soft_max(u)
                project(GLA_IN + u, 1, proj[:, 2 * u + 1, 0:T], scale, T)
                if u:
                    out_lo(u - 1)
                soft_norm(u)

            def gate_a(half, b, m):
                dve.wait_ge(slab_done, 2 * half + b + 1)
                dve.tensor_tensor(siga[:, m], bank[b][:, 0:TR], rstd[:, 0:TR], ALU.mult).then_inc(bank_free, 1)
                split_lo(half + 1, b, KD)

            dve.wait_ge(kv_out, 32)
            dve.wait_ge(qpad_done, 5)
            dve.wait_ge(knew_done, 1)
            for e in range(8):
                half, b = GATE_A + e // 2, e % 2
                gate_a(half, b, slice(e, e + 1))
                if e == 1:
                    out_lo(7)
                if e == 3:
                    dve.wait_ge(prep_act, 4)
                    for h in range(GH):
                        dve.tensor_scalar(mnz[:, h], bank[4 + h][:, 0:TA], a_bias[:, h:h + 1], 0.0,
                                          ALU.add, ALU.min).then_inc(prep_dve, 1)
                if e == 4:
                    dve.wait_ge(bias_loaded, 16)
                    dve.wait_ge(swa_pe, 2)
                    dve.tensor_tensor(ssc, bank[4][:, 0:144], bias_s, ALU.add).then_inc(swa_dve, 1)
                    dve.wait_ge(swa_dve, 1)
                    dve.tensor_reduce(stat[:, 0:1], ssc, AX.X, ALU.max).then_inc(swa_dve, 1)
                    dve.wait_ge(swa_dve, 2)
                    dve.tensor_tensor(stat[:, 2:3], stat[:, 0:1], sink_bh[:], ALU.max).then_inc(swa_dve, 1)
                    dve.wait_ge(swa_dve, 3)
                    dve.tensor_scalar(stat[:, 3:4], stat[:, 2:3], -1.0, None, ALU.mult).then_inc(swa_dve, 1)
                    dve.tensor_tensor(stat[:, 4:5], sink_bh[:], stat[:, 2:3], ALU.subtract).then_inc(swa_dve, 1)
                if e == 5:
                    dve.wait_ge(swa_act, 4)
                    dve.tensor_tensor(stat[:, 7:8], stat[:, 5:6], stat[:, 6:7], ALU.add).then_inc(swa_dve, 1)
                    dve.wait_ge(swa_dve, 6)
                    dve.reciprocal(stat[:, 8:9], stat[:, 7:8]).then_inc(swa_dve, 1)
                    dve.wait_ge(swa_dve, 7)
                    dve.tensor_scalar(ssc, ssc, stat[:, 8:9], None, ALU.mult).then_inc(swa_dve, 1)
                    dve.wait_ge(prep_dve, 4)
                    dve.wait_ge(prep_act, 6)
                    dve.tensor_tensor(spl, mnz, spl, ALU.subtract).then_inc(prep_dve, 1)
                    dve.wait_ge(prep_dve, 5)
                    dve.wait_ge(scan_loaded, 16)
                    for h in range(GH):
                        dve.tensor_tensor_scan(bc[:, h], scan_keep, spl[:, h], 0.0, ALU.mult,
                                               ALU.add).then_inc(prep_dve, 1)
                    dve.wait_ge(prep_dve, 9)
                    decay_to_end(dve, 0)
                if e == 6:
                    dve.wait_ge(win_out, 32)
                    decayed_keys(dve, 0)
                    decay_to_end(dve, 1)
            decayed_keys(dve, 1)
            dve.wait_ge(swa_pe, 4)
            token_diffs(dve, 0)
            dve.wait_ge(swa_act, 10)
            for gp in range(2):
                for jp in range(2):
                    hi, src = decode_out(gp, jp, y3_hi)
                    lo, _ = decode_out(gp, jp, y3_lo)
                    dve.tensor_tensor(lo, src, hi.bitcast(F32), ALU.subtract).then_inc(swa_dve, 1)
            new_state(dve, 0)
            token_products(dve, 0)

            def tile(m):
                return slice(m, m + 1) if isinstance(m, int) else bass.ds(m, 1)

            def scaled(half, b, c, gate):
                dve.wait_ge(slab_done, 2 * half + b + 1)
                dve.tensor_tensor(siga[:, tile(c + 8)] if gate is None else r_act, bank[b][:, 0:TR], rstd[:, 0:TR],
                                  ALU.mult).then_inc(bank_free, 1)

            def pair_of_slabs(half, v, gate, more=True):
                u = v + 1
                scaled(half, 0, 2 * v, gate)
                mid_diffs(dve, u)
                token_diffs(dve, 2 * v + 1)
                split_lo(half + 1, 0, KD)
                mid_products(dve, u)
                if more:
                    decay_to_end(dve, u + 1)
                token_products(dve, 2 * v + 1)
                if more:
                    decayed_keys(dve, u + 1)
                if gate is not None:
                    gate(2 * v - 8)
                scaled(half, 1, 2 * v + 1, gate)
                if later(v, 0):
                    new_state(dve, v)
                attention(dve, u)
                if more:
                    token_diffs(dve, 2 * v + 2)
                split_lo(half + 1, 1, KD)
                if more:
                    token_products(dve, 2 * v + 2)
                if gate is not None:
                    gate(2 * v - 7)

            def silu_r(m):
                dve.wait_ge(r_sig, m + 1)
                dve.tensor_tensor(r_act, r_act, r_sg, ALU.mult).then_inc(r_done, 1)
                dve.wait_ge(rhi_done, m + 1)
                dve.tensor_tensor(y3_lo[:, tile(m)], r_act, y3_hi[:, tile(m)].bitcast(F32), ALU.subtract).then_inc(rlo_done, 1)
                dve.wait_ge(rlo_done, m + 1)

            pair_of_slabs(GATE_A + 4, 0, None)
            with dve.Fori(1, 4) as v:
                pair_of_slabs(GATE_A + 4 + v, v, None)
            with dve.Fori(4, NCP - 1) as v:
                pair_of_slabs(GATE_A + 4 + v, v, silu_r)
            pair_of_slabs(GLA_R + 3, NCP - 1, silu_r, more=False)
            dve.wait_ge(nv_tr, 1)
            for q in range(2):
                dve.wait_ge(nv_hi, 2)
                dve.tensor_tensor(v_split[32:32 + NS, 512 * q:512 * q + 512], bank[4 + q][0:NS, :],
                                  v_split[0:NS, 512 * q:512 * q + 512].bitcast(F32), ALU.subtract).then_inc(nv_lo, 1)
            new_state(dve, NCP)
            dve.wait_ge(g_vbuf, NCP + 1)
            for u in range(NS):
                half, b = GATE_B + u // 2, u % 2
                dve.wait_ge(n_vbc, u + 1)
                for h in range(GH):
                    dve.wait_ge(n_decay, 4 * u + h + 1)
                    dve.scalar_tensor_tensor(S0[:, u % 3, h], bank[4 + h // 2][:, (h % 2) * DV:(h % 2 + 1) * DV],
                                             proj[:, GK + h, NP_ + u:NP_ + u + 1], S0[:, u % 3, h],
                                             ALU.mult, ALU.add).then_inc(n_state, 1)
                dve.wait_ge(slab_done, 2 * half + b + 1)
                dve.tensor_tensor(merged[:, 8 + u], bank[b][:, 0:TR], rstd[:, 0:TR], ALU.mult).then_inc(bank_free, 1)
                split_lo(half + 1, b, KD)

            def gated_norm(h):
                dve.wait_ge(on_rs, h + 1)
                for q in range(2):
                    j = 2 * h + q
                    if j >= 4:
                        dve.wait_ge(olo_done, j - 3)
                    dve.scalar_tensor_tensor(ow[:, j % 4], oT[:, j], onorm[:, j:j + 1], ors[:, h], ALU.mult,
                                             ALU.mult).then_inc(on_w, 1)

            def branch_lo(h):
                for j in range(2 * h, 2 * h + 2):
                    dve.wait_ge(ohi_done, j + 1)
                    dve.tensor_tensor(y3_lo[:, j], ow[:, j % 4], y3_hi[:, j].bitcast(F32), ALU.subtract).then_inc(olo_done, 1)

            dve.wait_ge(rlo_done, 8)
            for h in range(GH):
                half, b = GATE_B + 4 + h // 2, h % 2
                if h == 0:
                    dve.wait_ge(n_o, NS)
                if h == 1:
                    dve.wait_ge(s0_stored[0], 16 * 3)
                    dve.wait_ge(s0_stored[1], 16 * 3)
                    for g in range(GH):
                        dve.wait_ge(on_std, g + 1)
                        dve.reciprocal(ors[:, g], ostd[:, g]).then_inc(on_rs, 1)
                if h:
                    gated_norm(h - 1)
                dve.wait_ge(slab_done, 2 * half + b + 1)
                dve.tensor_tensor(merged[:, 4 + h], bank[b][:, 0:TR], rstd[:, 0:TR], ALU.mult).then_inc(bank_free, 1)
                split_lo(half + 1, b, KD)
                if h:
                    branch_lo(h - 1)
            gated_norm(GH - 1)
            branch_lo(GH - 1)

            dve.wait_ge(siga_done, KD)
            dve.wait_ge(sigb_done, 12)

            with dve.Fori(0, 6) as i:
                for b in range(2):
                    n, half = 2 * i + b, MERGE1 + i
                    dve.wait_ge(slab_done, 2 * half + b + 1)
                    dve.tensor_tensor(m1, siga[:, bass.ds(n + 4, 1)], bank[b][:, 0:TR], ALU.mult).then_inc(m_step, 1)
                    dve.tensor_tensor(m2, merged[:, bass.ds(n + 4, 1)], bank[2 + b][:, 0:TR], ALU.mult).then_inc(bank_free, 1)
                    dve.wait_ge(m_step, n + 1)
                    dve.wait_ge(bank_free, 2 * half + b + 1)
                    dve.tensor_tensor(merged[:, bass.ds(n + 4, 1)], m1, m2, ALU.add).then_inc(merged_done, 1)
                    split_lo(half + 1, b, KD)
                    dve.wait_ge(merged_done, n + 1)

            def merged_lo(k0, k1, n):
                dve.wait_ge(mhi_done, n)
                dve.tensor_tensor(x_lo[:, k0:k1, 0:TR], merged[:, k0:k1, :], x_hi[:, k0:k1, 0:TR].bitcast(F32),
                                  ALU.subtract).then_inc(mlo_done, 1)

            for i in range(4):
                half = MERGE2 + i
                dve.wait_ge(slab_done, 2 * half + 1)
                dve.tensor_tensor(gb_n, bank[0][:, 0:TR], rstd[:, 0:TR], ALU.mult).then_inc(bank_free, 1)
                split_lo(half + 1, 0, KD)
                if i == 3:
                    for q in range(1, 4):
                        merged_lo(4 * q, 4 * q + 4, q)
                    merged_lo(0, 3, 4)
                dve.wait_ge(slab_done, 2 * half + 2)
                dve.tensor_tensor(m1, siga[:, i], bank[1][:, 0:TR], ALU.mult).then_inc(m_step, 1)
                dve.wait_ge(sigb_done, 13 + i)
                dve.tensor_tensor(m2, sigb, bank[3][:, 0:TR], ALU.mult).then_inc(bank_free, 1)
                dve.wait_ge(m_step, 13 + i)
                dve.wait_ge(bank_free, 2 * half + 2)
                dve.tensor_tensor(merged[:, i], m1, m2, ALU.add).then_inc(merged_done, 1)
                if i == 3:
                    merged_lo(3, 4, 5)
                split_lo(half + 1, 1, KD)
                dve.wait_ge(merged_done, 13 + i)

            def residual(i, b, tile_first=False):
                m = bass.ds(2 * i + b, 1)
                dve.wait_ge(slab_done, 2 * (W_OUT + i) + b + 1)
                dve.tensor_tensor(hT[:, m, 0:TR], bank[b][:, 0:TR], hT[:, m, 0:TR], ALU.add).then_inc(bank_free, 1)
                if not tile_first:
                    split_lo(W_OUT + i + 1, b, KD)
                tile_lo(2, m, (y3_hi, y3_lo), TR, 2 * KD + 2 * i + b + 1)
                if tile_first:
                    split_lo(W_OUT + i + 1, b, KD)

            with dve.Fori(0, KD // 2 - 1) as i:
                for b in range(2):
                    residual(i, b)
            for b in range(2):
                residual(KD // 2 - 1, b, tile_first=True)
            ffn(FFN2, FT, x_hi, x_lo, TR, 2)
            inverse(3, TR)
            for m in range(KD - 4):
                dve.scalar_tensor_tensor(hT[:, m, 0:TR], hT[:, m, 0:TR], gains[:, 3, m:m + 1], rstd[:, 0:TR],
                                         ALU.mult, ALU.mult).then_inc(y_done, 1)

        @block.tensor
        def _(pe):
            def product(out, b, ks, x, T, n, ready=None, beside=None):
                pe.wait_ge(hi_split, n + 1)
                for k in ks:
                    if ready is not None:
                        ready(k)
                    w = w_hi[:, b, k * P:(k + 1) * P]
                    pe.matmul(out, w, x[0][:, k, 0:T], start=(k == ks[0]), stop=False)
                    pe.matmul(out, w, x[1][:, k, 0:T], start=False, stop=False)
                    if beside is not None:
                        beside(k)
                pe.wait_ge(lo_split, n + 1)
                for k in ks:
                    last = pe.matmul(out, w_lo[:, b, k * P:(k + 1) * P], x[0][:, k, 0:T], start=False, stop=(k == ks[-1]))
                    if beside is not None and k != ks[-1]:
                        beside(len(ks) + k)
                return last

            def slab(half, b, kt, x, T, ready=None, first=False, beside=None):
                if not first:
                    pe.wait_ge(bank_free, 2 * half + b - 1)
                product(bank[b][:, 0:T], b, range(kt), x, T, 2 * half + b, ready, beside).then_inc(slab_done, 1)

            def sum_squares(r, T):
                pe.wait_ge(acc_done, KD * (r + 1))
                if r == 0:
                    pe.wait_ge(consts_loaded, 16 * N_CONST)
                    pe.wait_ge(acc2_done, KD // 2)
                    pe.matmul(bank[7][:, 0:T], ones[:], acc2[:, 0:T], start=True, stop=False)
                pe.matmul(bank[7][:, 0:T], ones[:], acc[:, 0:T], start=(r > 0), stop=True).then_inc(sumsq_done, 1)

            def tiles_of_norm(r):
                def ready(k):
                    pe.wait_ge(xlo_done, KD * r + k + 1)
                return ready

            def ffn(half0, f0, x, s, T, r):
                for c in range(CH):
                    h0 = half0 + c * (FC + KD // 2)
                    i0 = 0
                    if c == 0:
                        slab(h0, 0, KD, x, T, ready=tiles_of_norm(r), first=half0 == 0)
                        if r:
                            sum_squares(r, T)
                        slab(h0, 1, KD, x, T, first=half0 == 0)
                        if not r:
                            sum_squares(r, T)
                        i0 = 1
                    with pe.Fori(i0, FC) as i:
                        for b in range(2):
                            slab(h0 + i, b, KD, x, T)
                    h1 = h0 + FC
                    slab(h1, 0, FC, s, T, ready=lambda k: pe.wait_ge(slo_done, f0 + c * FC + k + 1))
                    slab(h1, 1, FC, s, T)
                    with pe.Fori(1, KD // 2) as i:
                        for b in range(2):
                            slab(h1 + i, b, FC, s, T)

            x = (x_hi, x_lo)
            y = (y3_hi, y3_lo)
            ffn(0, 0, x, (s1_hi, s1_lo), TA, 0)

            slab(SWA_IN, 0, KD, x, TR, ready=tiles_of_norm(1))
            sum_squares(1, TA)
            pe.wait_ge(galo_done, 1)
            for k in range(KD):
                cols = slice(k * RANK, k * RANK + P)
                pe.matmul(bank[6][:, 0:TA], ga_hi[:, cols], x_hi[:, k, :], start=(k == 0), stop=False)
                pe.matmul(bank[6][:, 0:TA], ga_hi[:, cols], x_lo[:, k, :], start=False, stop=False)
                last = pe.matmul(bank[6][:, 0:TA], ga_lo[:, cols], x_hi[:, k, :], start=False, stop=(k == KD - 1))
            last.then_inc(gad_done, 1)
            slab(SWA_IN, 1, KD, x, TR)
            for i in range(1, 6):
                for b in range(2):
                    slab(SWA_IN + i, b, KD, x, TR if i < 4 else TA)

            def values_to_rows():
                pe.wait_ge(bank_free, 2 * GLA_IN)
                for ft in range(2):
                    for tt in range(2):
                        o = tt * 256 + ft * P
                        pe.transpose(bank[2][:, o:o + P], proj[:, SV + ft, tt * P:(tt + 1) * P], ident[:])
                    pe.transpose(bank[3][0:NM, ft * P:(ft + 1) * P], proj[:, SV + ft, M0:TA], ident[:])
                    last = pe.transpose(bank[4][0:NS, ft * P:(ft + 1) * P], proj[:, SV + ft, NP_:TR], ident[:])
                last.then_inc(vtr_done, 1)

            def scores(u):
                g, q0, nk = u // 2, (u % 2) * WIN, WIN * (u % 2 + 1)
                for j in range(4):
                    h = 4 * g + j
                    rows = slice(64 * (h % 2), 64 * (h % 2) + 64)
                    q = proj[rows, SQ + h // 2, q0:q0 + WIN]
                    if u and j == 3:
                        pe.wait_ge(pT_done, 3 * (u - 1) + 1)
                    pe.matmul(bank[2 + j][:, 0:nk], q, proj[rows, KDUP + g, 0:nk], start=True, stop=True)
                    last = pe.matmul(bank[2 + j][:, nk:nk + NM], q, proj[rows, KDUP + g, M0:TA], start=True, stop=True)
                last.then_inc(scores_done, 1)

            def turn_scores(u):
                nk = WIN * (u % 2 + 1)
                pe.wait_ge(p_ready, 6 * u + 6)
                if u:
                    pe.wait_ge(solo_done, 2 * u)
                for j in range(4):
                    pe.transpose(bank[5][0:NM, j * P:(j + 1) * P], sc[:, u % 2, j, nk:nk + NM], ident[:])
                for kc in range(u % 2 + 1):
                    for j in range(4):
                        last = pe.transpose(bank[6 + kc][:, j * P:(j + 1) * P], sc[:, u % 2, j, kc * P:(kc + 1) * P], ident[:])
                last.then_inc(ptr_done, 1)

            def weigh_values(u):
                g = u // 2
                cols = slice(g * HD, (g + 1) * HD)
                pe.wait_ge(pT_done, 3 * u + 3)
                out = bank[6][0:HD, :]
                pe.matmul(out, v_meta[:, cols], pT_meta, start=True, stop=False)
                for kc in range(u % 2 + 1):
                    last = pe.matmul(out, v_tok[:, kc, cols], pT[:, kc], start=False, stop=(kc == u % 2))
                last.then_inc(so_done, 1)

            for u in range(8):
                T = TR if u < 2 else TA
                slab(GLA_IN + u, 0, KD, x, T)
                if u == 0:
                    values_to_rows()
                    pe.wait_ge(kdup_done, 4)
                    pe.wait_ge(vtok_done, 3)
                else:
                    turn_scores(u - 1)
                scores(u)
                slab(GLA_IN + u, 1, KD, x, T)
                if u:
                    weigh_values(u - 1)

            for e in range(8):
                slab(GATE_A + e // 2, e % 2, KD, x, TR)
                if e == 0:
                    turn_scores(7)
                if e == 1:
                    weigh_values(7)
                if e == 2:
                    pe.wait_ge(solo_done, 16)
                    pe.wait_ge(pT_done, 24)
                    pe.wait_ge(gadT_done, 1)
                    for h in range(GH):
                        last = pe.matmul(bank[4 + h][:, 0:TA], a_up[0:RANK, h * DK:(h + 1) * DK], gadT[0:RANK], start=True, stop=True)
                    last.then_inc(z_done, 1)
                if e == 3:
                    pe.wait_ge(knew_done, 2)
                    pe.wait_ge(qpad_done, 5)
                    for b in range(NS):
                        for g in range(2):
                            cols = slice(b * NH + 8 * g, b * NH + 8 * g + 8)
                            pe.matmul(bank[2][:, cols], kT_win[:, b, g, 1:WIN + 1], q_pad[:, b, 8 * g:8 * g + 8], start=True, stop=True)
                            last = pe.matmul(bank[3][0:NM, cols], kT_meta[:, g, b, :], q_pad[:, b, 8 * g:8 * g + 8], start=True, stop=True)
                    last.then_inc(swa_pe, 1)
                if e == 4:
                    pe.wait_ge(swa_act, 2)
                    pe.wait_ge(prep_dve, 4)
                    pe.transpose(bank[4][:, 0:P], sT, ident[:])
                    pe.transpose(bank[4][:, P:P + NM], sT_meta, ident[0:NM, 0:NM]).then_inc(swa_pe, 1)
                if e == 6:
                    pe.wait_ge(swa_dve, 8)
                    pe.transpose(bank[3][:, 0:P], ssc[:, 0:P], ident[:])
                    pe.transpose(bank[3][0:NM, P:2 * P], ssc[:, P:P + NM], ident[:]).then_inc(swa_pe, 1)
                if e == 7:
                    pe.wait_ge(swa_act, 6)
                    turn(pe, 0)
                    pe.wait_ge(vwin_loaded, 16 * (1 + NS))
                    pe.wait_ge(vmeta_loaded, 16)
                    for b in range(NS):
                        for g in range(2):
                            cols = slice(b * NH + 8 * g, b * NH + 8 * g + 8)
                            pe.matmul(bank[2][:, cols], v_win[:, b, g * P:(g + 1) * P], pTs[:, cols], start=True, stop=False)
                            last = pe.matmul(bank[2][:, cols], v_meta_s[:, b, g * P:(g + 1) * P], pTs_meta[:, cols], start=False, stop=True)
                    last.then_inc(swa_pe, 1)
            turn(pe, 1)
            for h in range(GH):
                keys_by_values(pe, 0, h)

            def pair_of_slabs(half, v, more=True):
                def outputs_beside(i):
                    if 8 <= i < 24:
                        outputs(pe, v, i - 8)

                def state_beside(i):
                    if i < 16 and i % 4 == 3:
                        keys_by_values(pe, v, i // 4)

                slab(half, 0, KD, x, TR, beside=outputs_beside if later(v, 0) else None)
                if later(v, 0):
                    pe.wait_ge(g_oT, v)
                attend(pe, 2 * v, 0)
                slab(half, 1, KD, x, TR, beside=state_beside if later(v, 0) else None)
                attend(pe, 2 * v + 1, 1)
                attend_across(pe, v + 1)
                if more:
                    turn(pe, v + 2)

            pair_of_slabs(GATE_A + 4, 0)
            with pe.Fori(1, NCP - 1) as v:
                pair_of_slabs(GATE_A + 4 + v, v)
            pair_of_slabs(GLA_R + 3, NCP - 1, more=False)
            pe.wait_ge(g_vtok, 2 * NCP + 2)
            for j in range(8):
                last = pe.transpose(bank[4 + j // 4][0:NS, (j % 4) * P:(j % 4 + 1) * P], proj[:, GV + j, NP_:TR], ident[:])
            last.then_inc(nv_tr, 1)
            for n in range(16):
                outputs(pe, NCP, n)
            for h in range(GH):
                keys_by_values(pe, NCP, h)

            def decode_outputs(u, n):
                if n == 0:
                    pe.wait_ge(n_state, 4 * u + 4)
                    if u:
                        pe.wait_ge(n_oT, u)
                h, q = n // 2, n % 2
                last = pe.matmul(bank[3][:, n:n + 1], S0[:, u % 3, h, q * P:(q + 1) * P],
                                 proj[:, GQ + h, NP_ + u:NP_ + u + 1], start=True, stop=True)
                if n == 7:
                    last.then_inc(n_o, 1)

            pe.wait_ge(nv_lo, 2)
            for u in range(NS):
                pe.wait_ge(n_pick, u + 1)
                if u:
                    pe.wait_ge(n_state, 4 * u)
                for q in range(2):
                    last = pe.matmul(bank[4 + q][:], pick[:, u % 2], v_split[:, 512 * q:512 * q + 512], start=True, stop=True)
                last.then_inc(n_vbc, 1)
                slab(GATE_B + u // 2, u % 2, KD, x, TR,
                     beside=(lambda i: decode_outputs(u - 1, i // 2) if i % 2 and i < 16 else None) if u else None)
            for n in range(8):
                decode_outputs(NS - 1, n)

            for h in range(GH):
                slab(GATE_B + 4 + h // 2, h % 2, KD, x, TR)
                if h == 0:
                    pe.wait_ge(n_oT, NS)
                    for g in range(GH):
                        pe.wait_ge(on_sq, g + 1)
                        pe.matmul(bank[2 + g][:, 0:TR], ones[:], osq[g // 2][:, g % 2 * 2], start=True, stop=False)
                        pe.matmul(bank[2 + g][:, 0:TR], ones[:], osq[g // 2][:, g % 2 * 2 + 1], start=False, stop=True).then_inc(on_sum, 1)

            def branches(half, b, ready=None):
                n = 2 * half + b
                pe.wait_ge(bank_free, n - 1)
                product(bank[2 + b][:, 0:TR], b, range(8, 16), y, TR, n)
                product(bank[b][:, 0:TR], b, range(8), y, TR, n, ready).then_inc(slab_done, 1)

            pe.wait_ge(solo_done, 16)
            pe.wait_ge(on_std, GH)
            branches(MERGE1, 0, ready=lambda k: pe.wait_ge(olo_done, k + 1))
            branches(MERGE1, 1)
            with pe.Fori(1, 6) as i:
                for b in range(2):
                    branches(MERGE1 + i, b)
            for i in range(4):
                slab(MERGE2 + i, 0, KD, x, TR)
                branches(MERGE2 + i, 1)

            pe.wait_ge(bank_free, 2 * W_OUT - 1)
            product(bank[0][:, 0:TR], 0, (*range(4, KD), *range(4)), x, TR, 2 * W_OUT,
                    ready=lambda k: pe.wait_ge(mlo_done, 5 if k == 3 else k // 4 or 4)).then_inc(slab_done, 1)
            slab(W_OUT, 1, KD, x, TR)
            with pe.Fori(1, KD // 2) as i:
                for b in range(2):
                    slab(W_OUT + i, b, KD, x, TR)
            ffn(FFN2, FT, y, x, TR, 2)
            sum_squares(3, TR)


def _slabs(np_, w, kt):
    K, N = w.shape
    return np_.ascontiguousarray(w.reshape(kt, 128, N // 128, 128).transpose(2, 1, 0, 3)).reshape(N // 128, 128, kt * 128)


def _cols(np_, v):
    return np_.ascontiguousarray(v.reshape(-1, 128).T)


def kernel(**inputs):
    import numpy as _np
    import concourse.bacc as _bacc
    from concourse import mybir as _mybir
    from concourse.bass_utils import run_bass_kernel_spmd as _run

    x = {k: _np.asarray(v) for k, v in inputs.items()}
    cat, con = _np.concatenate, _np.ascontiguousarray
    a = {}
    tokens = cat([x["x_prompt"][0], x["x_sample"][:, 0], x["meta_tokens"]], 0)
    a["xT"] = con(tokens.T.reshape(KD, P, TA).transpose(1, 0, 2))
    for n in ("1", "2"):
        w = _slabs(_np, x[f"ffn{n}_w_in"][0], KD)
        a[f"w{n}_in"] = con(w.reshape(2, FT, P, ROW).transpose(1, 0, 2, 3))
        w = x[f"ffn{n}_w_out"][0].reshape(CH, FC, P, KD, P).transpose(0, 3, 2, 1, 4)
        a[f"w{n}_out"] = con(w).reshape(CH, KD // 2, 2, P, FC * P)
    w = x["w_in"][0]
    o_gla, o_r, o_ga, o_swa = 0, 2048, 3072, 3072 + RANK
    o_gate = o_swa + 1536
    order = [w[:, o_swa:o_gate], w[:, o_gla:o_r], w[:, o_gate:o_gate + D], w[:, o_r:o_ga]]
    a["w_proj"] = _slabs(_np, cat(order, 1), KD).reshape(26, 2, P, ROW)
    w_ga = w[:, o_ga:o_swa].reshape(KD, P, RANK).transpose(1, 0, 2).reshape(P, KD * RANK)
    a["w_ga"] = cat([w_ga, _np.zeros((P, GA_COLS - KD * RANK), w.dtype)], 1)
    gate_b = _slabs(_np, w[:, o_gate + D:], KD)
    both = _slabs(_np, cat([x["w_gla_o"][0], x["w_swa_o"][0]], 0), KD)
    rest = con(_np.stack([gate_b[:4], both[:4]], 1)).reshape(8, P, ROW)
    a["w_merge"] = cat([gate_b[8:], gate_b[4:8], both[4:], rest], 0).reshape(KD, 2, P, ROW)
    a["w_o"] = _slabs(_np, x["w_out"][0], KD).reshape(KD // 2, 2, P, ROW)
    norms = [x["ffn1_norm"][0], x["mix_norm"][0], x["ffn2_norm"][0], x["final_norm"]]
    a["gains"] = con(_np.stack([_cols(_np, v) for v in norms], 1))
    a["gbias"] = con(_cols(_np, x["gate_bias"][0]).reshape(P, 2, KD))
    a["onorm"] = _cols(_np, x["gla_out_norm"][0])
    a["a_up"] = con(x["gla_a_up"][0])
    a["a_bias"] = _cols(_np, x["gla_a_bias"][0])
    a["sinks"] = con(x["swa_sinks"])
    a["sink_bh"] = con(_np.tile(x["swa_sinks"][0], NS)[:, None])
    a["kT_cache"] = con(x["cache_win_k"][0].transpose(2, 3, 0, 1).reshape(2, P, NS, WIN).transpose(1, 2, 0, 3))
    a["kT_meta"] = con(x["cache_meta_k"][0].transpose(2, 3, 0, 1).reshape(2, P, NS, NM).transpose(1, 0, 2, 3))
    a["v_cache"] = con(x["cache_win_v"][0, :, 1:].reshape(NS, WIN - 1, 256).transpose(1, 0, 2))
    a["v_meta"] = con(x["cache_meta_v"][0].reshape(NS, NM, 256).transpose(1, 0, 2))
    a["state_in"] = con(x["state_gla"][0].transpose(0, 2, 1, 3))
    f = _np.float32
    slope = _np.exp2(-8.0 * _np.arange(1, NH + 1, dtype=f) / NH).astype(f)
    i, j = _np.arange(WIN)[:, None], _np.arange(2 * WIN)[None, :]
    dist = i + WIN - j
    dist = _np.where((dist >= 0) & (dist < WIN), dist, 1e36).astype(f)
    none = _np.zeros((P, NM), f)
    a["c_dist0"] = cat([dist[:, WIN:], none], 1)
    a["c_dist1"] = cat([dist, none], 1)
    a["c_nslope"] = con(_np.broadcast_to(-slope, (P, NH)))
    bias = -slope[:, None] * (WIN - 1 - _np.arange(WIN, dtype=f))[None, :]
    a["c_bias_s"] = cat([_np.tile(bias, (NS, 1)), none], 1).astype(f)
    a["c_ones"] = _np.ones((P, P), f)
    pick = (_np.arange(P)[:, None] % 32 == _np.arange(NS)[None, :]) & (_np.arange(P)[:, None] < 64)
    a["c_pick"] = pick.astype(f)
    a["c_ident"] = _np.eye(P, dtype=f)
    a["c_band"] = con(_np.broadcast_to((_np.arange(2 * CP - 1) == CP - 1).astype(f), (P, 2 * CP - 1)))
    keep = _np.ones((P, TA), f)
    keep[:, 0:NP_:CP] = 0
    keep[:, NP_:M0 + 1] = 0
    a["c_scan"] = keep
    s, tt = _np.arange(CP)[:, None, None, None], _np.arange(CP).reshape(1, 2, 1, CK)
    a["c_causal"] = con(_np.broadcast_to((tt >= s).astype(f), (CP, 2, GH, CK)))
    outs = {"yT": (P, KD, TR), "kvT": (P, 4, WIN + NM), "winkT": (P, NS, 2, WIN), "winv": (WIN, NS, 256),
            "state_p": (P, GH, DV), "state_s": (NS, P, GH, DV)}

    nc = _bacc.Bacc("TRN2", target_bir_lowering=False, num_devices=1)
    t = {n: nc.dram_tensor(f"in_{n}", v.shape, _mybir.dt.from_np(v.dtype), kind="ExternalInput").ap() for n, v in a.items()}
    t |= {n: nc.dram_tensor(f"out_{n}", s, _mybir.dt.float32, kind="ExternalOutput").ap() for n, s in outs.items()}
    build_layer(nc, t)
    r = _run(nc, [{f"in_{n}": v for n, v in a.items()}], core_ids=[0]).results[0]

    y = r["out_yT"].transpose(2, 1, 0).reshape(TR, D)
    kv = r["out_kvT"].transpose(2, 1, 0).reshape(WIN + NM, 2, 4, HD)
    wk = r["out_winkT"].transpose(1, 3, 2, 0).reshape(1, NS, WIN, 4, HD)
    wv = r["out_winv"].transpose(1, 0, 2).reshape(1, NS, WIN, 4, HD)
    return (con(y[:NP_])[None], con(y[NP_:])[:, None],
            con(kv[WIN:, 0])[None, None], con(kv[WIN:, 1])[None, None],
            con(kv[:WIN, 0])[None, None], con(kv[:WIN, 1])[None, None],
            con(r["out_state_p"].transpose(1, 0, 2))[None, None], con(wk), con(wv),
            con(r["out_state_s"].transpose(0, 2, 1, 3))[None])
```
